# Optimizing a Trainium2 kernel written in Bass

```python
import jax, jax.numpy as jnp
from jax import lax
import numpy as np

D_MODEL = 1024
BATCH = 1
SEQ = 512
DEPTH = 2
DEC_BATCH = 8
DEC_SEQ = 1
PAST_LEN = 4096
PAGE_SIZE = 128

ML_HEADS = 4
ML_DH = 128
ML_W = ML_HEADS * ML_DH
GLA_HEADS = 4
GLA_DK = 64
GLA_DV = 128
GLA_KW = GLA_HEADS * GLA_DK
GLA_VW = GLA_HEADS * GLA_DV
GLA_RANK = 16
GLA_TAU = 16.0
POOL_GROUPS = 4
POOL_GDIM = 128
POOL_W = POOL_GROUPS * POOL_GDIM
POOL_WINDOWS = (2, 4, 8, 16)
POOL_BUF = 15
N_BRANCH = 3
CHUNK = 64
D_FF = 2816
N_EXPERTS = 8
TOP_K = 2
D_FF_EXPERT = 1408
N_DENSE = (DEPTH + 1) // 2
N_MOE = DEPTH // 2
EPS = 1e-6
NEG = -1e30
IN_SPLITS = (ML_W, ML_W, ML_W, ML_HEADS, ML_HEADS, ML_W,
             GLA_KW, GLA_KW, GLA_VW, GLA_RANK, GLA_VW,
             POOL_W, N_BRANCH * D_MODEL)
D_IN = sum(IN_SPLITS)

kernel_name = 'hybrid_mlstm_gla_pool_decoder_step'

def rmsnorm(x, g):
    xf = x.astype(jnp.float32)
    y = xf * lax.rsqrt(jnp.mean(xf * xf, axis=-1, keepdims=True) + EPS)
    return (y * g.astype(jnp.float32)).astype(x.dtype)

def head_rmsnorm(h, g):
    y = h * lax.rsqrt(jnp.mean(h * h, axis=-1, keepdims=True) + EPS)
    return y.reshape(h.shape[:2] + (-1,)) * g.astype(jnp.float32)

def split_cols(z):
    parts, off = [], 0
    for w in IN_SPLITS:
        parts.append(z[..., off:off + w])
        off += w
    return parts

def to_chunks(a, L, pad_value):
    B, T = a.shape[:2]
    n = -(-T // L)
    pad = n * L - T
    a = jnp.pad(a, [(0, 0), (0, pad)] + [(0, 0)] * (a.ndim - 2), constant_values=pad_value)
    a = a.reshape((B, n, L) + a.shape[2:])
    return jnp.moveaxis(a, 1, 0)

def from_chunks(h, T):
    h = jnp.moveaxis(h, 0, 1)
    h = h.reshape((h.shape[0], h.shape[1] * h.shape[2]) + h.shape[3:])
    return h[:, :T]

def mlstm_chunked(q, k, v, i_pre, logf, C0, n0, m0):
    T = q.shape[1]
    L = min(CHUNK, T)
    qc, kc, vc = to_chunks(q, L, 0.0), to_chunks(k, L, 0.0), to_chunks(v, L, 0.0)
    ic = to_chunks(i_pre, L, NEG)
    fc = to_chunks(logf, L, 0.0)
    causal = jnp.tril(jnp.ones((L, L), dtype=bool))[None, :, :, None]

    def step(carry, inp):
        C, n, m = carry
        qb, kb, vb, ib, fb = inp
        b = jnp.cumsum(fb, axis=1)
        Dm = b[:, :, None, :] - b[:, None, :, :] + ib[:, None, :, :]
        Dm = jnp.where(causal, Dm, NEG)
        inter = b + m[:, None, :]
        m_t = jnp.maximum(inter, jnp.max(Dm, axis=2))
        w_intra = jnp.exp(Dm - m_t[:, :, None, :])
        w_inter = jnp.exp(inter - m_t)
        s = jnp.einsum('bthd,bshd->btsh', qb, kb) * w_intra
        num = (jnp.einsum('btsh,bshe->bthe', s, vb)
               + w_inter[..., None] * jnp.einsum('bhed,bthd->bthe', C, qb))
        den = jnp.sum(s, axis=2) + w_inter * jnp.einsum('bhd,bthd->bth', n, qb)
        h = num / jnp.maximum(jnp.abs(den), jnp.exp(-m_t))[..., None]
        bL = b[:, -1, :]
        g = bL[:, None, :] - b + ib
        m_new = jnp.maximum(bL + m, jnp.max(g, axis=1))
        w_s = jnp.exp(g - m_new[:, None, :])
        w_c = jnp.exp(bL + m - m_new)
        C_new = w_c[..., None, None] * C + jnp.einsum('bsh,bshe,bshd->bhed', w_s, vb, kb)
        n_new = w_c[..., None] * n + jnp.einsum('bsh,bshd->bhd', w_s, kb)
        return (C_new, n_new, m_new), h

    (C1, n1, m1), hs = lax.scan(step, (C0, n0, m0), (qc, kc, vc, ic, fc))
    return from_chunks(hs, T), C1, n1, m1

def gla_chunked(q, k, v, log_a, S0):
    T = q.shape[1]
    L = min(CHUNK, T)
    qc, kc, vc = to_chunks(q, L, 0.0), to_chunks(k, L, 0.0), to_chunks(v, L, 0.0)
    ac = to_chunks(log_a, L, 0.0)
    causal = jnp.tril(jnp.ones((L, L), dtype=bool))[None, :, :, None, None]

    def step(S, inp):
        qb, kb, vb, ab = inp
        b = jnp.cumsum(ab, axis=1)
        diff = b[:, :, None] - b[:, None, :]
        decay = jnp.where(causal, jnp.exp(jnp.where(causal, diff, 0.0)), 0.0)
        A = jnp.einsum('bthd,bshd,btshd->btsh', qb, kb, decay)
        o = (jnp.einsum('btsh,bshe->bthe', A, vb)
             + jnp.einsum('bthd,bhde->bthe', qb * jnp.exp(b), S))
        bL = b[:, -1]
        S_new = (jnp.exp(bL)[..., None] * S
                 + jnp.einsum('bshd,bshe->bhde', kb * jnp.exp(bL[:, None] - b), vb))
        return S_new, o

    S1, os_ = lax.scan(step, S0, (qc, kc, vc, ac))
    return from_chunks(os_, T), S1

def pool_mixer(u, buf, pos0, pool_w, pool_scale):
    B, T, P = u.shape
    ext = jnp.concatenate([buf, u], axis=1)
    cs = jnp.concatenate([jnp.zeros((B, 1, P), jnp.float32), jnp.cumsum(ext, axis=1)], axis=1)
    end = cs[:, POOL_BUF + 1:]
    pos = pos0 + jnp.arange(T)
    outs = []
    for gi, w in enumerate(POOL_WINDOWS):
        lo, hi = gi * POOL_GDIM, (gi + 1) * POOL_GDIM
        start = cs[:, POOL_BUF + 1 - w:POOL_BUF + 1 - w + T, lo:hi]
        cnt = jnp.minimum(pos + 1, w).astype(jnp.float32)[None, :, None]
        outs.append((end[..., lo:hi] - start) / cnt - u[..., lo:hi])
    d = jnp.stack(outs, axis=2)
    y = jnp.einsum('btgc,gcd->btgd', d, pool_w.astype(jnp.float32)).reshape(B, T, P)
    return y * pool_scale.astype(jnp.float32), ext[:, -POOL_BUF:]

def token_mix(x, C0, n0, m0, S0, buf0, pos0, norm1_g, w_in, if_bias, ml_g,
              gla_gw, gla_gb, gla_g, pool_w, pool_scale, w_branch, w_out):
    f32 = jnp.float32
    B, T, _ = x.shape
    h = rmsnorm(x, norm1_g)
    z = h @ w_in
    mq, mk, mv, mi, mf, mo, gq, gk, gv, glr, go, pu, gates = split_cols(z)
    q = mq.astype(f32).reshape(B, T, ML_HEADS, ML_DH)
    k = mk.astype(f32).reshape(B, T, ML_HEADS, ML_DH) * (ML_DH ** -0.5)
    v = mv.astype(f32).reshape(B, T, ML_HEADS, ML_DH)
    i_pre = mi.astype(f32) + if_bias[0].astype(f32)
    logf = jax.nn.log_sigmoid(mf.astype(f32) + if_bias[1].astype(f32))
    hm, C1, n1, m1 = mlstm_chunked(q, k, v, i_pre, logf, C0.astype(f32), n0.astype(f32), m0.astype(f32))
    y_ml = head_rmsnorm(hm, ml_g) * jax.nn.sigmoid(mo.astype(f32))
    q2 = gq.astype(f32).reshape(B, T, GLA_HEADS, GLA_DK) * (GLA_DK ** -0.5)
    k2 = gk.astype(f32).reshape(B, T, GLA_HEADS, GLA_DK)
    v2 = gv.astype(f32).reshape(B, T, GLA_HEADS, GLA_DV)
    log_a = jax.nn.log_sigmoid(glr.astype(f32) @ gla_gw.astype(f32) + gla_gb.astype(f32))
    log_a = log_a.reshape(B, T, GLA_HEADS, GLA_DK) / GLA_TAU
    og, S1 = gla_chunked(q2, k2, v2, log_a, S0.astype(f32))
    y_gla = head_rmsnorm(og, gla_g) * jax.nn.silu(go.astype(f32))
    y_pool, buf1 = pool_mixer(pu.astype(f32), buf0.astype(f32), pos0, pool_w, pool_scale)
    br = jnp.stack([y_ml, y_gla, y_pool], axis=2).astype(x.dtype)
    proj = jnp.einsum('btnc,ncd->btnd', br, w_branch)
    gate = jax.nn.sigmoid(gates.reshape(B, T, N_BRANCH, D_MODEL))
    mixed = jnp.sum(gate * proj, axis=2) @ w_out
    return x + mixed.astype(x.dtype), C1, n1, m1, S1, buf1

def swiglu(h, wg, wu, wd):
    return (jax.nn.silu(h @ wg) * (h @ wu)) @ wd

def moe_swiglu(h, router_w, wg, wu, wd):
    logits = (h @ router_w).astype(jnp.float32)
    probs = jax.nn.softmax(logits, axis=-1)
    top_p, top_i = lax.top_k(probs, TOP_K)
    top_p = top_p / jnp.sum(top_p, axis=-1, keepdims=True)
    comb = jnp.sum(jax.nn.one_hot(top_i, N_EXPERTS, dtype=jnp.float32) * top_p[..., None], axis=-2)
    out = jnp.zeros(h.shape[:-1] + (D_MODEL,), jnp.float32)
    for e in range(N_EXPERTS):
        out = out + comb[..., e:e + 1] * swiglu(h, wg[e], wu[e], wd[e]).astype(jnp.float32)
    return out.astype(h.dtype)

def channel_mix(l, x, norm2_g, ffn_wg, ffn_wu, ffn_wd, router_w, moe_wg, moe_wu, moe_wd):
    h = rmsnorm(x, norm2_g[l])
    j = l // 2
    if l % 2 == 0:
        return x + swiglu(h, ffn_wg[j], ffn_wu[j], ffn_wd[j])
    return x + moe_swiglu(h, router_w[j], moe_wg[j], moe_wu[j], moe_wd[j])

def setup_inputs(seed: int = 0) -> dict:
    key = jax.random.key(seed)
    ks = jax.random.split(key, 32)
    f32 = jnp.float32

    def nrm(k, shape, s):
        return jax.random.normal(k, shape, f32) * s

    forget_base = jnp.linspace(3.0, 6.0, ML_HEADS, dtype=f32)
    return {
        'x_prompt': nrm(ks[0], (BATCH, SEQ, D_MODEL), 1.0),
        'x_sample': nrm(ks[1], (DEC_BATCH, DEC_SEQ, D_MODEL), 1.0),
        'state_mlstm_C': nrm(ks[2], (DEPTH, DEC_BATCH, ML_HEADS, ML_DH, ML_DH), 0.1),
        'state_mlstm_n': nrm(ks[3], (DEPTH, DEC_BATCH, ML_HEADS, ML_DH), 0.1),
        'state_mlstm_m': nrm(ks[4], (DEPTH, DEC_BATCH, ML_HEADS), 0.5),
        'state_gla_S': nrm(ks[5], (DEPTH, DEC_BATCH, GLA_HEADS, GLA_DK, GLA_DV), 1.0),
        'state_pool_buf': nrm(ks[6], (DEPTH, DEC_BATCH, POOL_BUF, POOL_W), 1.0),
        'norm1_g': 1.0 + nrm(ks[7], (DEPTH, D_MODEL), 0.02),
        'w_in': nrm(ks[8], (DEPTH, D_MODEL, D_IN), D_MODEL ** -0.5),
        'mlstm_if_bias': jnp.stack([nrm(ks[9], (DEPTH, ML_HEADS), 0.1),
                                    forget_base + nrm(ks[10], (DEPTH, ML_HEADS), 0.1)], axis=1),
        'mlstm_norm_g': 1.0 + nrm(ks[11], (DEPTH, ML_W), 0.02),
        'gla_gate_w': nrm(ks[12], (DEPTH, GLA_RANK, GLA_KW), GLA_RANK ** -0.5),
        'gla_gate_b': nrm(ks[13], (DEPTH, GLA_KW), 0.1),
        'gla_norm_g': 1.0 + nrm(ks[14], (DEPTH, GLA_VW), 0.02),
        'pool_w': nrm(ks[15], (DEPTH, POOL_GROUPS, POOL_GDIM, POOL_GDIM), POOL_GDIM ** -0.5),
        'pool_scale': 1.0 + nrm(ks[16], (DEPTH, POOL_W), 0.02),
        'w_branch': nrm(ks[17], (DEPTH, N_BRANCH, ML_W, D_MODEL), ML_W ** -0.5),
        'w_out': nrm(ks[18], (DEPTH, D_MODEL, D_MODEL), D_MODEL ** -0.5),
        'norm2_g': 1.0 + nrm(ks[19], (DEPTH, D_MODEL), 0.02),
        'ffn_wg': nrm(ks[20], (N_DENSE, D_MODEL, D_FF), D_MODEL ** -0.5),
        'ffn_wu': nrm(ks[21], (N_DENSE, D_MODEL, D_FF), D_MODEL ** -0.5),
        'ffn_wd': nrm(ks[22], (N_DENSE, D_FF, D_MODEL), D_FF ** -0.5),
        'router_w': nrm(ks[23], (N_MOE, D_MODEL, N_EXPERTS), D_MODEL ** -0.5),
        'moe_wg': nrm(ks[24], (N_MOE, N_EXPERTS, D_MODEL, D_FF_EXPERT), D_MODEL ** -0.5),
        'moe_wu': nrm(ks[25], (N_MOE, N_EXPERTS, D_MODEL, D_FF_EXPERT), D_MODEL ** -0.5),
        'moe_wd': nrm(ks[26], (N_MOE, N_EXPERTS, D_FF_EXPERT, D_MODEL), D_FF_EXPERT ** -0.5),
        'final_norm_g': 1.0 + nrm(ks[27], (D_MODEL,), 0.02),
    }

def reference(x_prompt, x_sample, state_mlstm_C, state_mlstm_n, state_mlstm_m, state_gla_S,
              state_pool_buf, norm1_g, w_in, mlstm_if_bias, mlstm_norm_g, gla_gate_w, gla_gate_b,
              gla_norm_g, pool_w, pool_scale, w_branch, w_out, norm2_g, ffn_wg, ffn_wu, ffn_wd,
              router_w, moe_wg, moe_wu, moe_wd, final_norm_g):
    f32 = jnp.float32
    xp, xs = x_prompt, x_sample
    Cp_l, Cs_l, np_l, ns_l, mp_l, ms_l, Sp_l, Ss_l, bp_l, bs_l = [], [], [], [], [], [], [], [], [], []
    for l in range(DEPTH):
        lw = (norm1_g[l], w_in[l], mlstm_if_bias[l], mlstm_norm_g[l], gla_gate_w[l], gla_gate_b[l],
              gla_norm_g[l], pool_w[l], pool_scale[l], w_branch[l], w_out[l])
        xp, Cp, np_, mp, Sp, bp = token_mix(
            xp, jnp.zeros((BATCH, ML_HEADS, ML_DH, ML_DH), f32), jnp.zeros((BATCH, ML_HEADS, ML_DH), f32),
            jnp.zeros((BATCH, ML_HEADS), f32), jnp.zeros((BATCH, GLA_HEADS, GLA_DK, GLA_DV), f32),
            jnp.zeros((BATCH, POOL_BUF, POOL_W), f32), 0, *lw)
        xs, Cs, ns, ms, Ss, bs = token_mix(
            xs, state_mlstm_C[l], state_mlstm_n[l], state_mlstm_m[l], state_gla_S[l],
            state_pool_buf[l], PAST_LEN, *lw)
        xp = channel_mix(l, xp, norm2_g, ffn_wg, ffn_wu, ffn_wd, router_w, moe_wg, moe_wu, moe_wd)
        xs = channel_mix(l, xs, norm2_g, ffn_wg, ffn_wu, ffn_wd, router_w, moe_wg, moe_wu, moe_wd)
        Cp_l.append(Cp); Cs_l.append(Cs); np_l.append(np_); ns_l.append(ns)
        mp_l.append(mp); ms_l.append(ms); Sp_l.append(Sp); Ss_l.append(Ss)
        bp_l.append(bp); bs_l.append(bs)
    y_prompt = rmsnorm(xp, final_norm_g)
    y_sample = rmsnorm(xs, final_norm_g)
    mlstm_C_prompt = jnp.stack(Cp_l).astype(state_mlstm_C.dtype)
    mlstm_C_sample = jnp.stack(Cs_l).astype(state_mlstm_C.dtype)
    mlstm_n_prompt = jnp.stack(np_l).astype(state_mlstm_n.dtype)
    mlstm_n_sample = jnp.stack(ns_l).astype(state_mlstm_n.dtype)
    mlstm_m_prompt = jnp.stack(mp_l).astype(state_mlstm_m.dtype)
    mlstm_m_sample = jnp.stack(ms_l).astype(state_mlstm_m.dtype)
    gla_S_prompt = jnp.stack(Sp_l).astype(state_gla_S.dtype)
    gla_S_sample = jnp.stack(Ss_l).astype(state_gla_S.dtype)
    pool_buf_prompt = jnp.stack(bp_l).astype(state_pool_buf.dtype)
    pool_buf_sample = jnp.stack(bs_l).astype(state_pool_buf.dtype)
    return (y_prompt, y_sample, mlstm_C_prompt, mlstm_C_sample, mlstm_n_prompt, mlstm_n_sample,
            mlstm_m_prompt, mlstm_m_sample, gla_S_prompt, gla_S_sample, pool_buf_prompt, pool_buf_sample)


_drawn_inputs = setup_inputs


def setup_inputs(seed=0):
    import zlib

    import numpy as np

    out = dict(_drawn_inputs(seed))
    spreads = {}
    factors = {'mlstm_norm_g': 4.259,
     'gla_norm_g': 11.032,
     'pool_scale': 2.961,
     'final_norm_g': 9.702,
     'norm2_g': 2.933}
    for name, (base, spread) in spreads.items():
        noise = np.random.default_rng([zlib.crc32(name.encode()), seed]).standard_normal(out[name].shape)
        drawn = base * np.exp(spread * noise) if base else spread * noise
        out[name] = __import__('jax').numpy.asarray(drawn.astype(out[name].dtype))
    for name, factor in factors.items():
        out[name] = (out[name] * factor).astype(out[name].dtype)
    return out
```

```python
from contextlib import ExitStack

import numpy as np

import concourse.bass as bass
from concourse import mybir

F32 = mybir.dt.float32
F32R = mybir.dt.float32r
ALU = mybir.AluOpType
ACT = mybir.ActivationFunctionType
AX = mybir.AxisListType

P = 128
DEPTH = 2
D = 1024
KT = D // P
NP_TOK, NS_TOK = 512, 8
T = NP_TOK + NS_TOK
HALF = T // 2
TT = NP_TOK // P
H = 4
DK = 64
WINDOWS = (2, 4, 8, 16)
POOL_BUF = 15
F_TILES = 2816 // P
E = 8
NJ = 16
FE_TILES = 1408 // P
CAP = 168
WIDE = 192
REST = CAP - P
EPS = 1e-6
MASKED = -1e30

Z_SMALL, Z_GK, Z_GQ, Z_GV, Z_Q, Z_K, Z_V, Z_PU, Z_MO, Z_GO, N_Z = 0, 1, 3, 5, 9, 13, 17, 21, 25, 29, 33
PAIR_SLABS = 9
S_GATE = N_Z
S_OUT = S_GATE + KT // 2 * PAIR_SLABS
S_MIX = S_OUT + KT
S_DOWN = 2 * F_TILES
S_FFN = S_DOWN + F_TILES
S_JOB = 3 * FE_TILES
LAYER1 = S_MIX + S_FFN
ROUTER = LAYER1 + S_MIX
MOE0 = ROUTER + 1
N_SLABS = MOE0 + E * S_JOB
O_GATE = N_Z
O_OUT = O_GATE + KT // 2 * 12
O_MIX = O_OUT + KT
O_DOWN = 2 * F_TILES
O_FFN = O_DOWN + KT
O_LAYER1 = O_MIX + O_FFN
O_ROUTER = O_LAYER1 + O_MIX
RAW = 3
SPL = 3

C_ID, C_ONE, C_NEG, C_KEEP, C_SEL, C_INV, C_IOTA = 0, 128, 256, 384, 512, 1024, 1088
C_PART = C_IOTA + WIDE
C_TIE, C_EPS, C_HM = C_PART + 2 * NJ, C_PART + 2 * NJ + 64, C_PART + 2 * NJ + 65
N_CONST = C_HM + 2
V_N1, V_N2, V_ML, V_GLA, V_GB, V_PS, V_FN, N_VEC = 0, 8, 16, 20, 24, 26, 30, 38


class Steps:

    def __init__(self, sem, **phases):
        self.sem, self.end, n = sem, {}, 0
        for name, k in phases.items():
            n += k
            self.end[name] = n
        self.total = n

    def after(self, name, rep=0):
        return rep * self.total + self.end[name]


def token_tile(tt):
    return slice(tt * P, (tt + 1) * P)


def decoder(nc, slabs, x_in, vectors, if_bias, gate_w, pool_w, consts, ml_m0, ml_n0, ml_C0,
            gla_S0, pool_in, pool_old, y_out, C_p, C_s, n_p, n_s, m_p, m_s, S_p, S_s, pool_u,
            pool_keep):
    ctx = ExitStack()

    def sb(name, shape, dt=F32, where=ctx):
        return where.enter_context(nc.sbuf_tensor(name, shape, dt))

    def sem(name):
        return ctx.enter_context(nc.semaphore(name))

    ps = ctx.enter_context(nc.psum_tensor("ps", [P, 8, 512], F32))
    x = sb("x", [P, KT, T])
    h_hi = sb("h_hi", [P, KT, T], F32R)
    h_lo = sb("h_lo", [P, KT, T], F32R)
    raw = sb("raw", [P, RAW, KT, P])
    w_hi = sb("w_hi", [P, SPL, KT, P], F32R)
    w_lo = sb("w_lo", [P, SPL, KT, P], F32R)
    con = sb("con", [P, N_CONST])
    vec = sb("vec", [P, DEPTH, N_VEC])
    ifb = sb("ifb", [H, DEPTH, 2])
    sq = sb("sq", [P, 2, T])
    rs = sb("rs", [P, 2, T])

    ident = con[:, C_ID:C_ID + P]
    ones = con[:, C_ONE:C_ONE + P]
    neg_mask = con[:, C_NEG:C_NEG + P]
    keep_mask = con[:, C_KEEP:C_KEEP + P]
    select = con[0:H, C_SEL:C_SEL + H * P].rearrange("k (r c) -> k r c", c=P)
    inv_count = con[:, C_INV:C_INV + 64].rearrange("p (g t) -> p g t", t=16)
    iota = con[:, C_IOTA:C_IOTA + WIDE]
    part_index = con[:, C_PART:C_PART + 2 * NJ].rearrange("p (j a) -> p j a", a=2)
    tie = con[:, C_TIE:C_TIE + 64].rearrange("p (e j) -> p e j", j=8)
    eps = con[:, C_EPS:C_EPS + 1]
    head_half = con[:, C_HM:C_HM + 2]

    mix, early, late = ExitStack(), ExitStack(), ExitStack()
    br = sb("br", [P, 12, T], where=mix)
    gq = sb("gq", [P, 2, T], where=early)
    gk = sb("gk", [P, 2, T], where=early)
    gv = sb("gv", [P, H, T], where=early)
    q = sb("q", [P, H, T], where=early)
    k = sb("k", [P, H, T], where=early)
    v = sb("v", [P, H, T], where=early)
    row_i = sb("row_i", [H, T], where=early)
    row_f = sb("row_f", [H, T], where=early)
    row_b = sb("row_b", [H, T], where=early)
    row_M = sb("row_M", [H, T], where=early)
    acol = sb("acol", [P, TT, H], where=early)
    w3 = sb("w3", [H, 3, NS_TOK], where=early)
    w3b = sb("w3b", [P, H, 3 * NS_TOK], where=early)
    w3t = sb("w3t", [NS_TOK, 3, H], where=early)
    m_s0 = sb("m_s0", [H, NS_TOK], where=early)
    m_new = sb("m_new", [H, NS_TOK], where=early)
    m_inter = sb("m_inter", [H, NS_TOK], where=early)
    ea = sb("ea", [P, 2, NS_TOK], where=early)
    gla_mem, gla_a, gla_b, gla_c = ExitStack(), ExitStack(), ExitStack(), ExitStack()
    qz = sb("qz", [P, H, T], where=gla_mem)
    glr = sb("glr", [16, T], where=gla_a)
    ggw = sb("ggw", [16, 256], where=gla_a)
    la = sb("la", [P, 2, T], where=gla_a)
    gvt = sb("gvt", [P, TT, H * P], where=gla_a)
    gkt = sb("gkt", [P, TT, 256], where=gla_a)
    ge = sb("ge", [P, 3, 2, TT], where=gla_a)
    S = sb("S", [P, 2, P], where=gla_a)
    dec = sb("dec", [P, 2, T], where=gla_b)
    gla_b.close()
    att = sb("att", [P, H, P], where=gla_c)
    S_in = sb("S_in", [P, 2, P], where=gla_c)
    Ut = sb("Ut", [P, 2, P], where=gla_c)
    gla_c.close()
    gla_a.close()
    gd = ExitStack()
    Ss = sb("Ss", [P, NS_TOK, P], where=gd)
    gdiag = sb("gdiag", [NS_TOK, 2, NS_TOK, P], where=gd)
    gt8 = sb("gt8", [NS_TOK, 3, P], where=gd)
    gd.close()
    gla_mem.close()
    ml_mem = ExitStack()
    kt = sb("kt", [P, TT, P], where=ml_mem)
    vt = sb("vt", [P, TT, P], where=ml_mem)
    wgt = sb("wgt", [P, TT, NP_TOK], where=ml_mem)
    dm = sb("dm", [P, TT, P], where=ml_mem)
    den = sb("den", [P, NP_TOK], where=ml_mem)
    den2 = sb("den2", [P, NP_TOK], where=ml_mem)
    vw = sb("vw", [P, TT, P], where=ml_mem)
    wcol = sb("wcol", [P, TT], where=ml_mem)
    C_t = sb("C_t", [P, H, P], where=ml_mem)
    n_row = sb("n_row", [1, H * P], where=ml_mem)
    ml_mem.close()
    samp = ExitStack()
    Cs = sb("Cs", [P, NS_TOK, P], where=samp)
    Cq = sb("Cq", [P, NS_TOK, P], where=samp)
    diag = sb("diag", [NS_TOK, 2, NS_TOK, P], where=samp)
    tok8 = sb("tok8", [NS_TOK, 3, P], where=samp)
    n_s0 = sb("n_s0", [NS_TOK, H, P], where=samp)
    nq = sb("nq", [NS_TOK, P], where=samp)
    n_tmp = sb("n_tmp", [NS_TOK, P], where=samp)
    dcol = sb("dcol", [NS_TOK, 3], where=samp)
    rdiag = sb("rdiag", [NS_TOK, NS_TOK], where=samp)
    num8 = sb("num8", [P, NS_TOK], where=samp)
    vs8 = sb("vs8", [P, NS_TOK], where=samp)
    samp.close()
    pool_mem = ExitStack()
    pa = sb("pa", [P, 2, NP_TOK], where=pool_mem)
    pd = sb("pd", [P, T], where=pool_mem)
    pw = sb("pw", [P, 4, P], where=pool_mem)
    ext = sb("ext", [P, 4, NS_TOK, 16], where=pool_mem)
    pred = sb("pred", [P, NS_TOK], where=pool_mem)
    pool_mem.close()
    early.close()
    br_hi = sb("br_hi", [P, 12, T], F32R, where=late)
    br_lo = sb("br_lo", [P, 12, T], F32R, where=late)
    mixed = sb("mixed", [P, KT, T], where=late)
    gs = sb("gs", [P, 4, T], where=late)
    gt = sb("gt", [P, T], where=late)
    late.close()
    mix.close()

    ffn = ExitStack()
    a_hi = sb("a_hi", [P, F_TILES, T], F32R, where=ffn)
    a_lo = sb("a_lo", [P, F_TILES, T], F32R, where=ffn)
    sig = sb("sig", [P, T], where=ffn)
    af = sb("af", [P, 2, T], where=ffn)
    ffn.close()

    moe = ExitStack()
    ht_hi = sb("ht_hi", [P, 5, D], F32R, where=moe)
    ht_lo = sb("ht_lo", [P, 5, D], F32R, where=moe)
    lrow = sb("lrow", [E, T], where=moe)
    crow = sb("crow", [E, T], where=moe)
    cum = sb("cum", [E, T], where=moe)
    lt = sb("lt", [P, 5, E], where=moe)
    rk = sb("rk", [P, 2, 5 * E, E], where=moe)
    sel_t = sb("sel_t", [P, 5, E], where=moe)
    comb = sb("comb", [P, 5, E], where=moe)
    red = sb("red", [P, 5], where=moe)
    passes = sb("passes", [E, 3], where=moe)
    J = sb("J", [E, NJ], where=moe)
    jt = sb("jt", [1, NJ + 1], mybir.dt.int32, where=moe)
    postj = sb("postj", [P, NJ, 5], where=moe)
    combj = sb("combj", [P, NJ, 5], where=moe)
    pcol = sb("pcol", [P, 5], where=moe)
    ccol = sb("ccol", [P, 5], where=moe)
    Jb = sb("Jb", [E, P], where=moe)
    places = sb("places", [P, 2], where=moe)
    G = sb("G", [P, 5, WIDE], F32R, where=moe)
    GT = sb("GT", [P, 2, T], F32R, where=moe)
    hg = sb("hg", [P, KT, 2 * CAP], F32R, where=moe)
    gsum = sb("gsum", [P, CAP], where=moe)
    usum = sb("usum", [P, CAP], where=moe)
    msig = sb("msig", [P, CAP], where=moe)
    ma = sb("ma", [P, 2, CAP], where=moe)
    ma_hi = sb("ma_hi", [P, 2, CAP], F32R, where=moe)
    ma_lo = sb("ma_lo", [P, 2, CAP], F32R, where=moe)
    yt_hi = sb("yt_hi", [P, 2, D], F32R, where=moe)
    yt_lo = sb("yt_lo", [P, 2, D], F32R, where=moe)
    cw = sb("cw", [P, 2], where=moe)
    moe.close()
    last = ExitStack()
    yfin = sb("yfin", [P, KT, T], where=last)
    last.close()

    loaded = sem("loaded")
    arrived = [sem(f"arrived{i}") for i in range(RAW)]
    hi_ready, lo_ready = sem("hi_ready"), sem("lo_ready")
    slab_done = sem("slab_done")
    emptied = [sem("emptied0"), sem("emptied1")]
    x_updated = sem("x_updated")
    squared, squares_used, ssq_done = sem("squared"), sem("squares_used"), sem("ssq_done")
    rs_steps, normed = sem("rs_steps"), sem("normed")
    h_hi_ready, h_lo_ready = sem("h_hi_ready"), sem("h_lo_ready")
    ggw_in, m0_in = sem("ggw_in"), sem("m0_in")
    n0_in, C_in, S_in_s, pool_loaded = sem("n0_in"), sem("C_in"), sem("S_in_s"), sem("pool_loaded")
    st_S, st_C, st_nm, st_Cs, st_ns, st_Ss, st_pu, st_y, st_keep = (
        sem(n) for n in ("st_S", "st_C", "st_nm", "st_Cs", "st_ns", "st_Ss", "st_pu", "st_y", "st_keep"))
    g = Steps(sem("gla"), loga_pe=1, y=2, abs=2, exp=1, ln=1, loga=1, scan=8, diff=8, clip=1, e=5,
              qk=11, turn=TT, copy=TT, turnk=TT, copyk=TT)
    gc = Steps(sem("gla_chunk"), att=1, mask=1, sin=2, o=1, ocopy=1, su=4, ns=2)
    dg = Steps(sem("gla_decode"), turn=1, copy=1, diag=2, outer=1, decay=1, add=1, o=1, oc=1)
    rows = Steps(sem("rows"), gates=2, abs=2, exp=1, ln=1, logf=1, b=1, a=1, M=1, m=2, enm=1,
                 inter=1, smax=1, sdiff=3, sexp=1, turn=1, turned=3)
    ml = Steps(sem("mlstm"), turn=1, copies=2, dm=1, exps=7, scol=1, sc01=1, p01=2, sc23=1, p23=2,
               vw=1, out=1, cst=2, absd=1, maxd=1, rec=1, h=1)
    ds = Steps(sem("mlstm_decode"), vs=1, turn=1, copy=1, diag=2, outer=1, carry=1, add=1, cq=1,
               num=1, nt=1, n=1, nq=1, den=1, dabs=1, dmax=1, drec=1, rd=1, rb=1, h=1)
    pool_phases = {"ext": 1}
    for gi in range(4):
        pool_phases[f"w{gi}"] = 2 * (gi + 1) + 5
        pool_phases[f"mm{gi}"] = 1
        pool_phases[f"y{gi}"] = 1
    po = Steps(sem("pool"), **pool_phases)
    hn_n, hn_sq, hn_ssq = sem("head_normed"), sem("head_squared"), sem("head_ssq")
    hn_rs, hn_used = sem("head_rs"), sem("head_squares_used")
    gated, br_hi_ready, br_lo_ready = sem("gated"), sem("br_hi_ready"), sem("br_lo_ready")
    gate_sig, mix_steps = sem("gate_sig"), sem("mix_steps")
    mx_hi, mx_lo = sem("mx_hi"), sem("mx_lo")
    sig_ready, act_hi, act_lo = sem("sig_ready"), sem("act_hi"), sem("act_lo")
    rt = Steps(sem("routing"), logits=1, turn=1, zero=1, lt=2, gt=1, eq=1, tie=1, rank=1, sum=1, sel=1,
               mx=1, sub=1, exp=1, tot=1, rtot=1, prob=1, chosen=1, two=1, rtwo=1, comb=1, back=1,
               backed=4, cum=1, place=1, one=1, pass1=1, pass2=1, pass3=1, last=1, ends=1, first=1,
               J0=1, J=1, shift=1, table=1, tables=4)
    ht_turned, ht_hi_ready, ht_lo_ready = sem("ht_turned"), sem("ht_hi_ready"), sem("ht_lo_ready")
    g_ready, gathered, weighed, cw_ready = (sem(n) for n in ("g_ready", "gathered", "weighed", "cw_ready"))
    hg_hi_ready, hg_lo_ready = sem("hg_hi_ready"), sem("hg_lo_ready")
    job_cols, placed, gt_ready = sem("job_cols"), sem("placed"), sem("gt_ready")
    m_sum, m_sig, m_gate, m_up, m_act = (sem(n) for n in ("m_sum", "m_sig", "m_gate", "m_up", "m_act"))
    m_hi, m_lo = sem("m_hi"), sem("m_lo")
    yt_hi_ready, yt_lo_ready = sem("yt_hi_ready"), sem("yt_lo_ready")
    scattered, x_added = sem("scattered"), sem("x_added")
    block = ctx.enter_context(nc.Block())

    def evac(o):
        return emptied[o % 2], o // 2 + 1

    def gate_slab(f):
        return 3 * f - 1 if f else 0

    def down_slab(f):
        return 3 * f + 4 if f < FE_TILES - 1 else S_JOB - 1

    def out_ps(o):
        return ps[:, 2 * (o % 2):2 * (o % 2) + 2, 0:HALF]

    def gathered_ps(b):
        return ps[:, 2 * b:2 * b + 2, 0:2 * WIDE].rearrange("p b (a c) -> p b a c", a=2)[:, :, :, 0:CAP]

    def hg_part(b, lo):
        return hg[:, 4 * b:4 * b + 4, CAP * lo:CAP * (lo + 1)].rearrange("p (b a) c -> p b a c", a=2)

    def y_ps(ct):
        return ps[0:(P, REST)[ct], 4 + 2 * ct:6 + 2 * ct]

    def halves(ap):
        return ap.rearrange("p (a b) -> p a b", a=2)

    def mixers_done(l):
        return ((po.sem, po.after("y3", l)), (st_S, 16 * (l + 1)), (st_Ss, 32 * (l + 1)),
                (st_C, 16 * H * (l + 1)), (st_nm, 48 * (l + 1)), (st_Cs, 16 * H * (l + 1)),
                (st_ns, 16 * (l + 1)))

    @block.sync
    def _(sp):
        sp.dma_start(x[:], x_in).then_inc(loaded, 16)
        sp.dma_start(con[:], consts).then_inc(loaded, 16)
        sp.dma_start(vec[:], vectors).then_inc(loaded, 16)
        sp.dma_start(ifb[:], if_bias).then_inc(loaded, 16)
        for n in range(MOE0 + RAW):
            if n >= RAW:
                sp.wait_ge(lo_ready, n - RAW + 1)
            sp.dma_start(raw[:, n % RAW], slabs[n]).then_inc(arrived[n % RAW], 16)
        sp.wait_ge(rt.sem, rt.after("tables"))
        passes_sp = sp.value_load(jt[:, NJ:NJ + 1], min_val=E, max_val=NJ - 2)
        with sp.Fori(0, passes_sp) as j:
            own = sp.value_load(jt[:, bass.ds(j, 1)], min_val=0, max_val=(E - 1) * S_JOB)
            after = sp.value_load(jt[:, bass.ds(j + 1, 1)], min_val=0, max_val=(E - 1) * S_JOB)
            for i in range(RAW, S_JOB + RAW):
                n = MOE0 + i
                first = own + n if i < S_JOB else after + (n - S_JOB)
                sp.wait_ge(lo_ready, j * S_JOB + (n - RAW + 1))
                sp.dma_start(raw[:, n % RAW],
                             slabs[bass.ds(first, 1)].rearrange("o p k c -> p (o k) c")).then_inc(
                                 arrived[n % RAW], 16)
        sp.wait_ge(normed, 8 * 5)
        sp.dma_start(y_out, yfin[:]).then_inc(st_y, 16)
        sp.wait_ge(st_y, 16)
        sp.wait_ge(st_keep, 16)

    @block.gpsimd
    def _(pool):
        for l in range(DEPTH):
            if l > 0:
                pool.wait_ge(*evac(O_LAYER1 - 1))
                pool.wait_ge(*evac(O_LAYER1 - 2))
            else:
                pool.dma_start(pool_keep, pool_old).then_inc(st_keep, 16)
            pool.dma_start(m_s0[:], ml_m0[l]).then_inc(m0_in, 16)
            pool.dma_start(ggw[:], gate_w[l]).then_inc(ggw_in, 16)
            pool.wait_ge(gc.sem, gc.after("ns", TT * l + TT - 1))
            pool.dma_start(S_p[l], S[:]).then_inc(st_S, 16)
            for j in range(2):
                i = 2 * l + j
                if j == 0:
                    pool.wait_ge(st_S, 16 * (l + 1))
                else:
                    pool.wait_ge(st_Ss, 16 * i)
                pool.dma_start(Ss[:], gla_S0[l, j]).then_inc(S_in_s, 16)
                pool.wait_ge(dg.sem, dg.after("oc", i))
                pool.dma_start(S_s[l, j], Ss[:]).then_inc(st_Ss, 16)
            for h in range(H):
                i = H * l + h
                pool.wait_ge(ml.sem, ml.after("cst", i))
                pool.dma_start(C_p[l, h], C_t[:, h]).then_inc(st_C, 16)
            pool.dma_start(n_p[l], n_row[:]).then_inc(st_nm, 16)
            pool.dma_start(m_p[l], row_b[:, NP_TOK - 1:NP_TOK]).then_inc(st_nm, 16)
            pool.dma_start(m_s[l], m_new[:]).then_inc(st_nm, 16)
            pool.wait_ge(ml.sem, ml.after("h", H * l + H - 1))
            pool.wait_ge(st_C, 16 * H * (l + 1))
            pool.wait_ge(st_nm, 48 * (l + 1))
            pool.dma_start(n_s0[:], ml_n0[l]).then_inc(n0_in, 16)
            for h in range(H):
                i = H * l + h
                if h > 0:
                    pool.wait_ge(st_Cs, 16 * i)
                pool.dma_start(Cs[:], ml_C0[l, h]).then_inc(C_in, 16)
                pool.wait_ge(ds.sem, ds.after("h", i))
                pool.dma_start(C_s[l, h], Cs[:]).then_inc(st_Cs, 16)
            pool.dma_start(n_s[l], n_s0[:]).then_inc(st_ns, 16)
            pool.wait_ge(st_Cs, 16 * H * (l + 1))
            pool.wait_ge(st_ns, 16 * (l + 1))
            pool.dma_start(pw[:], pool_w[l]).then_inc(pool_loaded, 16)
            pool.dma_start(ext[:, :, :, 0:POOL_BUF], pool_in[l]).then_inc(pool_loaded, 16)
            pool.dma_start(pool_u[l], br[:, 8:12, NP_TOK - POOL_BUF:T]).then_inc(st_pu, 16)
            pool.wait_ge(st_pu, 16 * (l + 1))

    @block.scalar
    def _(act):
        def split_hi(n, j=0):
            act.wait_ge(arrived[n % RAW], j * (16 * S_JOB // RAW) + 16 * (n // RAW + 1))
            if n >= SPL:
                act.wait_ge(slab_done, j * S_JOB + (n - SPL + 1))
            nc.scalar.activation(w_hi[:, n % SPL], raw[:, n % RAW], ACT.Copy).then_inc(hi_ready, 1)

        def out_done(n):
            act.wait_ge(slab_done, n + 1)

        def norm(r, hs, ready):
            if r > 0:
                act.wait_ge(h_lo_ready, 8 * hs)
            for kk in range(KT):
                i = 8 * r + kk
                for s, n in ready(kk):
                    act.wait_ge(s, n)
                if i >= 2:
                    act.wait_ge(squares_used, i - 1)
                nc.scalar.activation(sq[:, kk % 2], x[:, kk], ACT.Square).then_inc(squared, 1)
            act.wait_ge(squares_used, 8 * (r + 1))
            if r > 0:
                act.wait_ge(normed, 8 * r)
            nc.scalar.activation(halves(rs[:, 0]), ps[:, 4:6, 0:HALF], ACT.Ln, bias=eps,
                                 scale=1.0 / D).then_inc(rs_steps, 1)
            act.wait_ge(rs_steps, 2 * r + 1)
            nc.scalar.activation(rs[:, 0], rs[:, 0], ACT.Exp, scale=-0.5).then_inc(rs_steps, 1)
            if r < 4:
                for kk in range(KT):
                    act.wait_ge(normed, 8 * r + kk + 1)
                    nc.scalar.activation(h_hi[:, kk], sq[:, kk % 2], ACT.Copy).then_inc(h_hi_ready, 1)

        def inputs(l, nb, ob):
            for i in range(Z_MO):
                n, o = nb + i, ob + i
                split_hi(n + 2)
                if i == Z_SMALL:
                    out_done(n)
                    src = out_ps(o)
                    nc.scalar.activation(halves(row_i[:]), src[0:H], ACT.Identity,
                                         bias=ifb[:, l, 0:1]).then_inc(rows.sem, 1)
                    nc.scalar.activation(halves(row_f[:]), src[32:32 + H], ACT.Identity,
                                         bias=ifb[:, l, 1:2]).then_inc(rows.sem, 1)
                    nc.scalar.activation(halves(glr[:]), src[64:80], ACT.Copy).then_inc(emptied[o % 2], 1)
                    continue
                for first, buf, at in ((Z_GV, gv, 0), (Z_Q, q, 0), (Z_V, v, 0), (Z_PU, br, 8)):
                    if first <= i < first + 4:
                        out_done(n)
                        nc.scalar.activation(halves(buf[:, at + i - first]), out_ps(o),
                                             ACT.Copy).then_inc(emptied[o % 2], 1)

        def gla(l):
            act.wait_ge(g.sem, g.after("loga_pe", l))
            for j in range(2):
                nc.scalar.activation(halves(la[:, j]), ps[:, 4 + 2 * j:6 + 2 * j, 0:HALF], ACT.Identity,
                                     bias=vec[:, l, V_GB + j:V_GB + j + 1]).then_inc(g.sem, 1)
            act.wait_ge(g.sem, g.after("abs", l))
            nc.scalar.activation(dec[:], dec[:], ACT.Exp, scale=-1.0).then_inc(g.sem, 1)
            act.wait_ge(g.sem, g.after("exp", l))
            nc.scalar.activation(dec[:], dec[:], ACT.Ln, bias=1.0).then_inc(g.sem, 1)
            act.wait_ge(g.sem, g.after("clip", l))
            mid = dec[:, :, P // 2 - 1:NP_TOK:P]
            end = la[:, :, P - 1:NP_TOK:P]
            nc.scalar.activation(ge[:, 0], mid, ACT.Exp, scale=1.0 / 16).then_inc(g.sem, 1)
            nc.scalar.activation(ge[:, 1], end, ACT.Exp, scale=1.0 / 16).then_inc(g.sem, 1)
            nc.scalar.activation(ea[:], la[:, :, NP_TOK:T], ACT.Exp, scale=1.0 / 16).then_inc(g.sem, 1)
            act.wait_ge(g.sem, g.after("clip", l) + 3)
            nc.scalar.activation(dec[:, :, 0:NP_TOK], la[:, :, 0:NP_TOK], ACT.Exp,
                                 scale=1.0 / 16).then_inc(g.sem, 1)
            act.wait_ge(g.sem, g.after("clip", l) + 4)
            nc.scalar.activation(la[:, :, 0:NP_TOK], la[:, :, 0:NP_TOK], ACT.Exp,
                                 scale=-1.0 / 16).then_inc(g.sem, 1)
            for tt in range(TT):
                act.wait_ge(g.sem, g.after("turn", l))
                nc.scalar.activation(gvt[:, tt], ps[:, 4 + tt], ACT.Copy).then_inc(g.sem, 1)
            for tt in range(TT):
                act.wait_ge(g.sem, g.after("turnk", l))
                nc.scalar.activation(gkt[:, tt], ps[:, 4 + tt, 0:256], ACT.Copy).then_inc(g.sem, 1)
            for tt in range(TT):
                rep = TT * l + tt
                act.wait_ge(gc.sem, gc.after("o", rep))
                nc.scalar.activation(br[:, 4:8, token_tile(tt)],
                                     ps[:, 6, :].rearrange("p (h t) -> p h t", t=P),
                                     ACT.Copy).then_inc(gc.sem, 1)

        def mlstm(l):
            act.wait_ge(rows.sem, rows.after("abs", l))
            nc.scalar.activation(row_M[:], row_M[:], ACT.Exp, scale=-1.0).then_inc(rows.sem, 1)
            act.wait_ge(rows.sem, rows.after("exp", l))
            nc.scalar.activation(row_M[:], row_M[:], ACT.Ln, bias=1.0).then_inc(rows.sem, 1)
            act.wait_ge(rows.sem, rows.after("m", l))
            nc.scalar.activation(row_f[:, 0:NP_TOK], row_b[:, 0:NP_TOK], ACT.Exp,
                                 scale=-1.0).then_inc(rows.sem, 1)
            act.wait_ge(rows.sem, rows.after("sdiff", l))
            nc.scalar.activation(w3[:], w3[:], ACT.Exp).then_inc(rows.sem, 1)
            for h in range(H):
                rep = H * l + h
                at = lambda name: act.wait_ge(ml.sem, ml.after(name, rep))
                at("turn")
                nc.scalar.activation(kt[:], ps[:, 4].rearrange("p (a d) -> p a d", d=P),
                                     ACT.Copy).then_inc(ml.sem, 1)
                at("dm")
                for tt in range(TT):
                    nc.scalar.activation(wgt[:, tt, token_tile(tt)], dm[:, tt], ACT.Exp,
                                         bias=acol[:, tt, h:h + 1]).then_inc(ml.sem, 1)
                for tt in range(TT - 1):
                    rest = slice((tt + 1) * P, NP_TOK)
                    nc.scalar.activation(wgt[:, tt, rest], ps[:, 6, rest], ACT.Exp,
                                         bias=acol[:, tt, h:h + 1]).then_inc(ml.sem, 1)
                at("out")
                nc.scalar.activation(C_t[:, h], ps[:, 5, 0:P], ACT.Copy).then_inc(ml.sem, 1)
                nc.scalar.activation(n_row[:, h * P:(h + 1) * P], ps[0:1, 5, P:2 * P],
                                     ACT.Copy).then_inc(ml.sem, 1)
                at("cst")
                nc.scalar.activation(den[:], ps[:, 7], ACT.Abs).then_inc(ml.sem, 1)

        def pool_mix(l):
            for gi in range(4):
                act.wait_ge(po.sem, po.after(f"mm{gi}", l))
                act.wait_ge(st_pu, 16 * (l + 1))
                nc.scalar.activation(halves(br[:, 8 + gi]), ps[:, 4:6, 0:HALF], ACT.Copy,
                                     scale=vec[:, l, V_PS + gi:V_PS + gi + 1]).then_inc(po.sem, 1)

        def head_norm(l):
            act.wait_ge(h_lo_ready, 8 * (3 * l + 1))
            act.wait_ge(ds.sem, ds.after("h", H * l + H - 1))
            for t in range(9):
                if t < 8:
                    i = 8 * l + t
                    if t >= 2:
                        act.wait_ge(hn_ssq, i - 1)
                    nc.scalar.activation(sq[:, t % 2], br[:, t], ACT.Square).then_inc(hn_sq, 1)
                if t > 0:
                    b, i = (t - 1) % 2, 8 * l + t - 1
                    act.wait_ge(hn_ssq, i + 1)
                    if t > 2:
                        act.wait_ge(hn_n, i - 1)
                    nc.scalar.activation(halves(rs[:, b]), ps[:, 4 + 2 * b:6 + 2 * b, 0:HALF], ACT.Ln,
                                         bias=eps, scale=1.0 / P).then_inc(hn_rs, 1)
                    act.wait_ge(hn_rs, 2 * i + 1)
                    nc.scalar.activation(rs[:, b], rs[:, b], ACT.Exp, scale=-0.5).then_inc(hn_rs, 1)

        def gates(l, nb, ob):
            for s, n in mixers_done(l):
                act.wait_ge(s, n)
            for j in range(9):
                i = 8 * l + j
                if j < 8:
                    n, o = nb + Z_MO + j, ob + Z_MO + j
                    split_hi(n + 2)
                    out_done(n)
                    if j < 4:
                        if j >= 2:
                            act.wait_ge(gated, i - 1)
                        nc.scalar.activation(halves(gs[:, j % 2]), out_ps(o),
                                             ACT.Sigmoid).then_inc(emptied[o % 2], 1)
                    else:
                        if j > 4:
                            act.wait_ge(*evac(o - 1))
                        nc.scalar.activation(halves(gt[:]), out_ps(o), ACT.Sigmoid).then_inc(gate_sig, 1)
                if j > 0:
                    act.wait_ge(gated, i)
                    nc.scalar.activation(br_hi[:, j - 1], br[:, j - 1], ACT.Copy).then_inc(br_hi_ready, 1)
            for t in range(8, 12):
                nc.scalar.activation(br_hi[:, t], br[:, t], ACT.Copy).then_inc(br_hi_ready, 1)

        def merge(l, nb, ob):
            for mp in range(KT // 2):
                n0, o0 = nb + S_GATE + PAIR_SLABS * mp, ob + O_GATE + 12 * mp
                for s, out, slot, reader in ((0, 0, 0, -5), (1, 1, 1, -4), (2, None, 0, 0),
                                             (3, 4, 2, -2), (4, 5, 0, 2), (5, 6, 1, 3),
                                             (6, None, 0, 0), (7, 9, 3, -1), (8, None, 0, 0)):
                    split_hi(n0 + s + 2)
                    if out is None:
                        continue
                    out_done(n0 + s)
                    if reader > 0 or mp > 0:
                        act.wait_ge(*evac(o0 + reader))
                    nc.scalar.activation(halves(gs[:, slot]), out_ps(o0 + out),
                                         ACT.Sigmoid).then_inc(emptied[(o0 + out) % 2], 1)
            act.wait_ge(slab_done, nb + S_OUT)
            act.wait_ge(mix_steps, 16 * (l + 1))
            for kk in range(KT):
                nc.scalar.activation(h_hi[:, kk], mixed[:, kk], ACT.Copy).then_inc(h_hi_ready, 1)
            for m in range(KT):
                split_hi(nb + S_OUT + m + 2)

        def feed_forward(nf, of):
            for f in range(F_TILES + 1):
                if f < F_TILES:
                    split_hi(nf + 2 * f + 2)
                    out_done(nf + 2 * f)
                    if f > 0:
                        act.wait_ge(*evac(of + 2 * f - 2))
                    nc.scalar.activation(halves(sig[:]), out_ps(of + 2 * f),
                                         ACT.Sigmoid).then_inc(sig_ready, 1)
                    split_hi(nf + 2 * f + 3)
                if f > 0:
                    act.wait_ge(*evac(of + 2 * f - 1))
                    nc.scalar.activation(a_hi[:, f - 1], af[:, (f - 1) % 2], ACT.Copy).then_inc(act_hi, 1)
            for s in range(F_TILES):
                split_hi(nf + S_DOWN + s + 2)


        def gathered_hi(p):
            act.wait_ge(gathered, p + 1)
            for b in range(2):
                nc.scalar.activation(hg_part(b, 0), gathered_ps(b), ACT.Copy).then_inc(hg_hi_ready, 1)

        def routing():
            split_hi(ROUTER + 2)
            act.wait_ge(rt.sem, rt.after("sub"))
            nc.scalar.activation(comb[:], comb[:], ACT.Exp).then_inc(rt.sem, 1)
            for i in range(5):
                rws = P if i < 4 else NS_TOK
                act.wait_ge(ht_turned, 2 * i + 1)
                nc.scalar.activation(ht_hi[0:rws, i].rearrange("p (a d) -> p a d", a=2), ps[0:rws, 4:6],
                                     ACT.Copy).then_inc(ht_hi_ready, 1)

        def expert_pass(j):
            s0, f0 = MOE0, j * FE_TILES
            for f in range(FE_TILES):
                split_hi(s0 + gate_slab(f) + 2, j)
                act.wait_ge(m_sum, f0 + (f + 1))
                nc.scalar.activation(msig[:], gsum[:], ACT.Sigmoid).then_inc(m_sig, 1)
                split_hi(s0 + gate_slab(f) + 3, j)
                act.wait_ge(m_act, f0 + (f + 1))
                nc.scalar.activation(ma_hi[:, f % 2], ma[:, f % 2], ACT.Copy).then_inc(m_hi, 1)
                if f > 0:
                    split_hi(s0 + down_slab(f - 1) + 2, j)
            split_hi(s0 + down_slab(FE_TILES - 1) + 2, j)
            gathered_hi(j + 1)
            act.wait_ge(slab_done, j * S_JOB + (s0 + S_JOB))
            act.wait_ge(cw_ready, j * 2 + 2)
            for ct in range(2):
                rws = slice(0, (P, REST)[ct])
                nc.scalar.activation(yt_hi[rws, ct].rearrange("p (a d) -> p a d", a=2), y_ps(ct),
                                     ACT.Copy, scale=cw[rws, ct:ct + 1]).then_inc(yt_hi_ready, 1)

        act.wait_ge(loaded, 64)
        split_hi(0)
        split_hi(1)
        for l in range(DEPTH):
            nb, ob = l * LAYER1, l * O_LAYER1
            norm(2 * l, 3 * l, lambda kk: [evac(O_LAYER1 - KT + kk)] if l else [])
            inputs(l, nb, ob)
            gla(l)
            mlstm(l)
            pool_mix(l)
            head_norm(l)
            gates(l, nb, ob)
            merge(l, nb, ob)
            norm(2 * l + 1, 3 * l + 2, lambda kk: [evac(ob + O_OUT + kk)])
            if l == 0:
                feed_forward(S_MIX, O_MIX)
            else:
                routing()
                act.wait_ge(rt.sem, rt.after("tables"))
                passes_act = act.value_load(jt[:, NJ:NJ + 1], min_val=E, max_val=NJ - 2)
                gathered_hi(0)
                with act.Fori(0, passes_act) as j:
                    expert_pass(j)
        norm(4, 6, lambda kk: [] if kk else [(x_added, passes_act * KT + KT)])

    @block.vector
    def _(dve):
        tt_op = nc.vector.tensor_tensor
        ts_op = nc.vector.tensor_scalar
        stt_op = nc.vector.scalar_tensor_tensor

        def split_lo(n, j=0):
            dve.wait_ge(hi_ready, j * S_JOB + (n + 1))
            tt_op(w_lo[:, n % SPL], raw[:, n % RAW], w_hi[:, n % SPL].bitcast(F32),
                  ALU.subtract).then_inc(lo_ready, 1)

        def out_done(n):
            dve.wait_ge(slab_done, n + 1)

        def norm(r, hs):
            gain = vec[:, 1, V_FN:V_FN + KT] if r == 4 else vec[:, r // 2, (V_N1, V_N2)[r % 2]:][:, 0:KT]
            dve.wait_ge(rs_steps, 2 * r + 2)
            for kk in range(KT + 1):
                if kk < KT:
                    if r < 4 and kk >= 2:
                        dve.wait_ge(h_lo_ready, 8 * hs + kk - 1)
                    to = yfin[:, kk] if r == 4 else sq[:, kk % 2]
                    stt_op(to, x[:, kk], gain[:, kk:kk + 1], rs[:, 0], ALU.mult,
                           ALU.mult).then_inc(normed, 1)
                if r < 4 and kk > 0:
                    dve.wait_ge(h_hi_ready, 8 * hs + kk)
                    tt_op(h_lo[:, kk - 1], sq[:, (kk - 1) % 2], h_hi[:, kk - 1].bitcast(F32),
                          ALU.subtract).then_inc(h_lo_ready, 1)

        def inputs(l, nb, ob):
            for i in range(Z_MO):
                n, o = nb + i, ob + i
                split_lo(n + 2)
                for first, last, buf, scale in ((Z_GK, Z_GQ, gk, 1.0), (Z_GQ, Z_GV, gq, DK ** -0.5),
                                                (Z_K, Z_V, k, P ** -0.5)):
                    if first <= i < last:
                        out_done(n)
                        ts_op(halves(buf[:, i - first]), out_ps(o), scale, None,
                              ALU.mult).then_inc(emptied[o % 2], 1)

        def gla(l):
            at = lambda name, more=0: dve.wait_ge(g.sem, g.after(name, l) + more)
            inc = lambda ins: ins.then_inc(g.sem, 1)
            at("y")
            inc(stt_op(dec[:], la[:], -1.0, la[:], ALU.mult, ALU.max))
            inc(ts_op(la[:], la[:], 0.0, None, ALU.min))
            at("ln")
            inc(tt_op(la[:], la[:], dec[:], ALU.subtract))
            at("loga")
            for j in range(2):
                for tt in range(TT):
                    inc(nc.vector.tensor_tensor_scan(dec[:, j, token_tile(tt)], la[:, j, token_tile(tt)],
                                                     la[:, j, token_tile(tt)], 0.0, ALU.add, ALU.bypass))
            at("scan")
            for j in range(2):
                for tt in range(TT):
                    c = tt * P + P // 2 - 1
                    inc(ts_op(la[:, j, token_tile(tt)], dec[:, j, token_tile(tt)], dec[:, j, c:c + 1],
                              -1280.0, ALU.subtract, ALU.max))
            at("diff")
            inc(ts_op(la[:, :, 0:NP_TOK], la[:, :, 0:NP_TOK], 1280.0, None, ALU.min))
            at("e")
            for h in range(H):
                inc(stt_op(qz[:, h, 0:NP_TOK], gq[:, h // 2, 0:NP_TOK], head_half[:, h % 2:h % 2 + 1],
                           dec[:, h // 2, 0:NP_TOK], ALU.mult, ALU.mult))
                inc(ts_op(qz[:, h, NP_TOK:T], gq[:, h // 2, NP_TOK:T], head_half[:, h % 2:h % 2 + 1],
                          None, ALU.mult))
            inc(tt_op(gk[:, :, 0:NP_TOK], gk[:, :, 0:NP_TOK], la[:, :, 0:NP_TOK], ALU.mult))
            inc(tt_op(ge[:, 2], ge[:, 0], ge[:, 1], ALU.mult))
            inc(nc.vector.memset(S[:], 0.0))
            at("copyk")
            for tt in range(TT):
                rep = TT * l + tt
                at = lambda name: dve.wait_ge(gc.sem, gc.after(name, rep))
                inc = lambda ins: ins.then_inc(gc.sem, 1)
                at("att")
                inc(tt_op(att[:], ps[:, 4].rearrange("p (h t) -> p h t", t=P),
                          keep_mask.unsqueeze(1).to_broadcast([P, H, P]), ALU.mult))
                for j in range(2):
                    inc(ts_op(S_in[:, j], S[:, j], ge[:, 0, j, tt:tt + 1], None, ALU.mult))
                at("ocopy")
                for j in range(2):
                    for half in range(2):
                        rws = slice(64 * half, 64 * half + 64)
                        c = 256 * j + P * half
                        inc(ts_op(Ut[rws, j], ps[rws, 5, c:c + P], ge[rws, 1, j, tt:tt + 1], None,
                                  ALU.mult))
                at("su")
                for j in range(2):
                    inc(stt_op(S[:, j], S[:, j], ge[:, 2, j, tt:tt + 1], Ut[:, j], ALU.mult, ALU.add))

        def gla_decode(l):
            for j in range(2):
                rep = 2 * l + j
                at = lambda name: dve.wait_ge(dg.sem, dg.after(name, rep))
                inc = lambda ins: ins.then_inc(dg.sem, 1)
                at("turn")
                inc(nc.vector.tensor_copy(gt8[:], ps[0:NS_TOK, 4, 0:3 * P].rearrange(
                    "b (a d) -> b a d", d=P)))
                at("copy")
                for half in range(2):
                    spread(inc, gdiag[:, half], gt8[:, 1 + half])
                at("outer")
                dve.wait_ge(S_in_s, 16 * (rep + 1))
                inc(tt_op(Ss[:], Ss[:], ea[:, j].unsqueeze(2).to_broadcast([P, NS_TOK, P]), ALU.mult))
                at("decay")
                inc(tt_op(Ss[:].rearrange("p (a b) d -> p a (b d)", a=2), Ss[:].rearrange("p (a b) d -> p a (b d)", a=2),
                          ps[:, 4:6], ALU.add))
                at("o")
                inc(nc.vector.tensor_copy(br[:, 4 + 2 * j:6 + 2 * j, NP_TOK:T],
                                          ps[:, 6, 0:16].rearrange("p (b h) -> p h b", h=2)))

        def spread(inc, to, rows8):
            inc(tt_op(to, rows8.unsqueeze(1).to_broadcast([NS_TOK, NS_TOK, P]),
                      ident[0:NS_TOK, 0:NS_TOK].unsqueeze(2).to_broadcast([NS_TOK, NS_TOK, P]),
                      ALU.mult))

        def mlstm_rows(l):
            at = lambda name: dve.wait_ge(rows.sem, rows.after(name, l))
            inc = lambda ins: ins.then_inc(rows.sem, 1)
            pr, sa = slice(0, NP_TOK), slice(NP_TOK, T)
            at("gates")
            inc(stt_op(row_M[:], row_f[:], -1.0, row_f[:], ALU.mult, ALU.max))
            inc(ts_op(row_f[:], row_f[:], 0.0, None, ALU.min))
            at("ln")
            inc(tt_op(row_f[:], row_f[:], row_M[:], ALU.subtract))
            at("logf")
            inc(nc.vector.tensor_tensor_scan(row_b[:, pr], row_f[:, pr], row_f[:, pr], 0.0, ALU.add,
                                             ALU.bypass))
            at("b")
            inc(tt_op(row_i[:, pr], row_i[:, pr], row_b[:, pr], ALU.subtract))
            at("a")
            inc(nc.vector.tensor_tensor_scan(row_M[:, pr], row_i[:, pr], row_i[:, pr], 0.0, ALU.max,
                                             ALU.bypass))
            at("M")
            inc(tt_op(row_b[:, pr], row_b[:, pr], row_M[:, pr], ALU.add))
            dve.wait_ge(rows.sem, rows.after("M", l) + 1)
            inc(ts_op(row_M[:, pr], row_M[:, pr], -1.0, None, ALU.mult))
            at("enm")
            dve.wait_ge(m0_in, 16 * (l + 1))
            inc(tt_op(m_inter[:], row_f[:, sa], m_s0[:], ALU.add))
            at("inter")
            inc(tt_op(m_new[:], m_inter[:], row_i[:, sa], ALU.max))
            at("smax")
            inc(tt_op(w3[:, 0], row_i[:, sa], m_new[:], ALU.subtract))
            inc(tt_op(w3[:, 1], m_inter[:], m_new[:], ALU.subtract))
            inc(ts_op(w3[:, 2], m_new[:], -1.0, None, ALU.mult))
            at("turn")
            inc(nc.vector.tensor_copy(acol[:], ps[:, 4, 0:16].rearrange("p (a h) -> p a h", h=H)))
            inc(nc.vector.tensor_copy(w3t[:], ps[0:NS_TOK, 4, 32:44].rearrange("p (a h) -> p a h", h=H)))
            inc(nc.vector.tensor_copy(w3b[:], ps[:, 5, 0:96].rearrange("p (h w) -> p h w", h=H)))
            at("turned")

        def mlstm(l):
            for h in range(H):
                rep = H * l + h
                at = lambda name: dve.wait_ge(ml.sem, ml.after(name, rep))
                inc = lambda ins: ins.then_inc(ml.sem, 1)
                at("turn")
                inc(nc.vector.tensor_copy(vt[:], ps[:, 5].rearrange("p (a d) -> p a d", d=P)))
                at("copies")
                inc(tt_op(dm[:], ps[:, 6].rearrange("p (a d) -> p a d", d=P),
                          neg_mask.unsqueeze(1).to_broadcast([P, TT, P]), ALU.add))
                at("exps")
                inc(nc.vector.tensor_copy(wcol[:], wgt[:, :, NP_TOK - 1]))
                at("sc01")
                for tt in range(2):
                    inc(tt_op(wgt[:, tt, tt * P:], wgt[:, tt, tt * P:], ps[:, 4 + tt, 0:NP_TOK - tt * P],
                              ALU.mult))
                at("sc23")
                for tt in range(2, 4):
                    at_ps = ps[:, 4, 256 * (tt - 2):256 * (tt - 2) + NP_TOK - tt * P]
                    inc(tt_op(wgt[:, tt, tt * P:], wgt[:, tt, tt * P:], at_ps, ALU.mult))
                at("scol")
                dve.wait_ge(ml.sem, ml.after("p23", rep))
                inc(tt_op(vw[:], vt[:], wcol[:].unsqueeze(2).to_broadcast([P, TT, P]), ALU.mult))
                at("absd")
                inc(tt_op(den[:], den[:], ps[:, 4], ALU.max))
                at("maxd")
                inc(nc.vector.reciprocal(den2[:], den[:]))
                at("rec")
                inc(tt_op(br[:, h, 0:NP_TOK], ps[:, 6], den2[:], ALU.mult))
                at("h")

        def mlstm_decode(l):
            dve.wait_ge(st_C, 16 * H * (l + 1))
            dve.wait_ge(st_nm, 48 * (l + 1))
            for h in range(H):
                rep = H * l + h
                at = lambda name: dve.wait_ge(ds.sem, ds.after(name, rep))
                inc = lambda ins: ins.then_inc(ds.sem, 1)
                if h > 0:
                    dve.wait_ge(ds.sem, ds.after("h", rep - 1))
                inc(tt_op(vs8[:], v[:, h, NP_TOK:T], w3b[:, h, 0:NS_TOK], ALU.mult))
                at("turn")
                inc(nc.vector.tensor_copy(tok8[:], ps[0:NS_TOK, 4, 0:3 * P].rearrange(
                    "b (a d) -> b a d", d=P)))
                at("copy")
                for a in range(2):
                    spread(inc, diag[:, a], tok8[:, 1 + a])
                at("outer")
                dve.wait_ge(C_in, 16 * (rep + 1))
                inc(tt_op(Cs[:], Cs[:], w3b[:, h, NS_TOK:2 * NS_TOK].unsqueeze(2).to_broadcast(
                    [P, NS_TOK, P]), ALU.mult))
                at("carry")
                Cs2 = Cs[:].rearrange("p (a b) d -> p a (b d)", a=2)
                inc(tt_op(Cs2, Cs2, ps[:, 4:6], ALU.add))
                at("add")
                inc(tt_op(Cq[:].rearrange("p (a b) d -> p a (b d)", a=2), Cs2, ps[:, 6:8], ALU.mult))
                at("cq")
                inc(nc.vector.tensor_reduce(num8[:], Cq[:], AX.X, ALU.add))
                at("num")
                inc(ts_op(n_tmp[:], tok8[:, 1], w3t[:, 0, h:h + 1], None, ALU.mult))
                at("nt")
                dve.wait_ge(n0_in, 16 * (l + 1))
                inc(stt_op(n_s0[:, h], n_s0[:, h], w3t[:, 1, h:h + 1], n_tmp[:], ALU.mult, ALU.add))
                at("n")
                inc(tt_op(nq[:], n_s0[:, h], tok8[:, 2], ALU.mult))
                at("nq")
                inc(nc.vector.tensor_reduce(dcol[:, 0:1], nq[:], AX.X, ALU.add))
                at("den")
                inc(stt_op(dcol[:, 1:2], dcol[:, 0:1], -1.0, dcol[:, 0:1], ALU.mult, ALU.max))
                at("dabs")
                inc(ts_op(dcol[:, 1:2], dcol[:, 1:2], w3t[:, 2, h:h + 1], None, ALU.max))
                at("dmax")
                inc(nc.vector.reciprocal(dcol[:, 2:3], dcol[:, 1:2]))
                at("drec")
                inc(ts_op(rdiag[:], ident[0:NS_TOK, 0:NS_TOK], dcol[:, 2:3], None, ALU.mult))
                at("rb")
                inc(tt_op(br[:, h, NP_TOK:T], num8[:], ps[:, 4, 0:NS_TOK], ALU.mult))

        def pool_mix(l):
            dve.wait_ge(pool_loaded, 32 * (l + 1))
            count = [po.total * l]

            def step(ins):
                ins.then_inc(po.sem, 1)
                count[0] += 1
                dve.wait_ge(po.sem, count[0])

            step(nc.vector.tensor_copy(ext[:, :, :, POOL_BUF], br[:, 8:12, NP_TOK:T]))
            for gi, w in enumerate(WINDOWS):
                src, shift = br[:, 8 + gi, 0:NP_TOK], 1
                for level in range(gi + 1):
                    to = pa[:, level % 2]
                    step(tt_op(to[:, shift:], src[:, shift:], src[:, 0:NP_TOK - shift], ALU.add))
                    step(nc.vector.tensor_copy(to[:, 0:shift], src[:, 0:shift]))
                    src, shift = to, 2 * shift
                step(ts_op(pd[:, 0:NP_TOK], src, 1.0 / w, None, ALU.mult))
                step(tt_op(pd[:, 0:16], src[:, 0:16], inv_count[:, gi], ALU.mult))
                step(tt_op(pd[:, 0:NP_TOK], pd[:, 0:NP_TOK], br[:, 8 + gi, 0:NP_TOK], ALU.subtract))
                step(nc.vector.tensor_reduce(pred[:], ext[:, gi, :, 16 - w:16], AX.X, ALU.add))
                step(stt_op(pd[:, NP_TOK:T], pred[:], 1.0 / w, br[:, 8 + gi, NP_TOK:T], ALU.mult,
                            ALU.subtract))
                count[0] += 2
                dve.wait_ge(po.sem, po.after(f"y{gi}", l))

        def head_norm(l):
            for t in range(8):
                i = 8 * l + t
                dve.wait_ge(hn_rs, 2 * i + 2)
                gain = vec[:, l, V_ML + t:V_ML + t + 1]
                stt_op(br[:, t], br[:, t], gain, rs[:, t % 2], ALU.mult, ALU.mult).then_inc(hn_n, 1)

        def gates(l, nb, ob):
            for s, n in mixers_done(l):
                dve.wait_ge(s, n)
            for j in range(9):
                i = 8 * l + j
                if j < 8:
                    n, o = nb + Z_MO + j, ob + Z_MO + j
                    split_lo(n + 2)
                    if j < 4:
                        dve.wait_ge(*evac(o))
                        dve.wait_ge(hn_n, i + 1)
                        tt_op(br[:, j], br[:, j], gs[:, j % 2], ALU.mult).then_inc(gated, 1)
                    else:
                        dve.wait_ge(gate_sig, 4 * l + j - 3)
                        if j > 4:
                            dve.wait_ge(gated, i)
                        tt_op(halves(gs[:, 2]), out_ps(o), halves(gt[:]), ALU.mult).then_inc(
                            emptied[o % 2], 1)
                        dve.wait_ge(*evac(o))
                        dve.wait_ge(hn_n, i + 1)
                        tt_op(br[:, j], br[:, j], gs[:, 2], ALU.mult).then_inc(gated, 1)
                if j > 0:
                    rest(l, j - 1)
            for t in range(8, 12):
                rest(l, t)

        def rest(l, t):
            dve.wait_ge(br_hi_ready, 12 * l + t + 1)
            tt_op(br_lo[:, t], br[:, t], br_hi[:, t].bitcast(F32), ALU.subtract).then_inc(br_lo_ready, 1)

        def merge(l, nb, ob):
            for mp in range(KT // 2):
                n0, o0 = nb + S_GATE + PAIR_SLABS * mp, ob + O_GATE + 12 * mp
                steps = 16 * l + 4 * mp
                for s, outs in ((0, ()), (1, ()), (2, ((2, 0, 0, 0), (3, 1, 1, 0))), (3, ()), (4, ()),
                                (5, ()), (6, ((7, 5, 0, 1), (8, 6, 1, 1))), (7, ()),
                                (8, ((10, 4, 2, 0), (11, 9, 3, 1)))):
                    split_lo(n0 + s + 2)
                    for out, gate, slot, m in outs:
                        out_done(n0 + s)
                        dve.wait_ge(*evac(o0 + gate))
                        o = o0 + out
                        first = slot == 0
                        if not first and steps > 0:
                            dve.wait_ge(mix_steps, steps)
                        to = mixed[:, 2 * mp + m] if first else gt[:]
                        tt_op(halves(to), out_ps(o), halves(gs[:, slot]), ALU.mult).then_inc(
                            emptied[o % 2], 1)
                        if not first:
                            dve.wait_ge(*evac(o))
                            dve.wait_ge(*evac(o0 + (2, 7)[m]))
                            tt_op(mixed[:, 2 * mp + m], mixed[:, 2 * mp + m], gt[:], ALU.add).then_inc(
                                mix_steps, 1)
                            steps += 1
            for kk in range(KT):
                dve.wait_ge(h_hi_ready, 8 * (3 * l + 1) + kk + 1)
                tt_op(h_lo[:, kk], mixed[:, kk], h_hi[:, kk].bitcast(F32), ALU.subtract).then_inc(
                    h_lo_ready, 1)
            for m in range(KT):
                n, o = nb + S_OUT + m, ob + O_OUT + m
                split_lo(n + 2)
                out_done(n)
                tt_op(halves(x[:, m]), halves(x[:, m]), out_ps(o), ALU.add).then_inc(emptied[o % 2], 1)

        def feed_forward(nf, of):
            for f in range(F_TILES + 1):
                if f < F_TILES:
                    split_lo(nf + 2 * f + 2)
                    o = of + 2 * f
                    split_lo(nf + 2 * f + 3)
                    dve.wait_ge(sig_ready, f + 1)
                    if f >= 2:
                        dve.wait_ge(act_lo, f - 1)
                    tt_op(halves(af[:, f % 2]), out_ps(o), halves(sig[:]), ALU.mult).then_inc(
                        emptied[o % 2], 1)
                    dve.wait_ge(*evac(o))
                    out_done(nf + 2 * f + 1)
                    tt_op(halves(af[:, f % 2]), halves(af[:, f % 2]), out_ps(o + 1), ALU.mult).then_inc(
                        emptied[(o + 1) % 2], 1)
                if f > 0:
                    dve.wait_ge(act_hi, f)
                    tt_op(a_lo[:, f - 1], af[:, (f - 1) % 2], a_hi[:, f - 1].bitcast(F32),
                          ALU.subtract).then_inc(act_lo, 1)
            m = 0
            for s in range(F_TILES):
                split_lo(nf + S_DOWN + s + 2)
                while m < KT and (F_TILES * (m + 1) - 1) // 8 == s:
                    o = of + O_DOWN + m
                    out_done(nf + S_DOWN + s)
                    tt_op(halves(x[:, m]), halves(x[:, m]), out_ps(o), ALU.add).then_inc(
                        emptied[o % 2], 1)
                    m += 1


        def prepare(p):
            nc.vector.tensor_copy(pcol[:], postj[:, bass.ds(p, 1)].rearrange("p o t -> p (o t)")).then_inc(g_ready, 1)
            nc.vector.tensor_copy(ccol[:], combj[:, bass.ds(p, 1)].rearrange("p o t -> p (o t)")).then_inc(g_ready, 1)
            dve.wait_ge(g_ready, p * 7 + 2)
            for tt in range(5):
                rws = P if tt < 4 else NS_TOK
                ts_op(G[0:rws, tt], iota[0:rws], pcol[0:rws, tt:tt + 1], None, ALU.is_equal).then_inc(
                    g_ready, 1)

        def gathered_lo(p):
            for b in range(2):
                dve.wait_ge(hg_hi_ready, p * 2 + (b + 1))
                tt_op(hg_part(b, 1), gathered_ps(b), hg_part(b, 0).bitcast(F32),
                      ALU.subtract).then_inc(hg_lo_ready, 1)

        def routing():
            split_lo(ROUTER + 2)
            at = lambda name, more=0: dve.wait_ge(rt.sem, rt.after(name) + more)
            inc = lambda ins: ins.then_inc(rt.sem, 1)
            out_done(ROUTER)
            inc(nc.vector.tensor_copy(halves(lrow[:]), out_ps(O_ROUTER)[0:E]))
            at("turn")
            inc(nc.vector.memset(lt[:], 0.0))
            at("zero")
            inc(nc.vector.tensor_copy(lt[:, 0:4], ps[:, 4, 0:4 * E].rearrange("p (t e) -> p t e", e=E)))
            inc(nc.vector.tensor_copy(lt[0:NS_TOK, 4], ps[0:NS_TOK, 4, 4 * E:5 * E]))
            at("lt")
            other = lt[:].unsqueeze(2).to_broadcast([P, 5, E, E])
            own = lt[:].unsqueeze(3).to_broadcast([P, 5, E, E])
            rk4 = [rk[:, a].rearrange("p (t e) j -> p t e j", e=E) for a in range(2)]
            inc(tt_op(rk4[0], other, own, ALU.is_gt))
            inc(tt_op(rk4[1], other, own, ALU.is_equal))
            at("eq")
            inc(tt_op(rk4[1], rk4[1], tie.unsqueeze(1).to_broadcast([P, 5, E, E]), ALU.mult))
            at("tie")
            inc(tt_op(rk[:, 0], rk[:, 0], rk[:, 1], ALU.add))
            at("rank")
            inc(nc.vector.tensor_reduce(sel_t[:].rearrange("p t e -> p (t e)"), rk[:, 0], AX.X, ALU.add))
            at("sum")
            inc(ts_op(sel_t[:], sel_t[:], 2.0, None, ALU.is_lt))
            inc(nc.vector.tensor_reduce(red[:], lt[:], AX.X, ALU.max))
            at("mx")
            wide = red[:].unsqueeze(2).to_broadcast([P, 5, E])
            inc(tt_op(comb[:], lt[:], wide, ALU.subtract))
            at("exp")
            inc(nc.vector.tensor_reduce(red[:], comb[:], AX.X, ALU.add))
            at("tot")
            inc(nc.vector.reciprocal(red[:], red[:]))
            at("rtot")
            inc(tt_op(comb[:], comb[:], wide, ALU.mult))
            at("prob")
            inc(tt_op(comb[:], comb[:], sel_t[:], ALU.mult))
            at("chosen")
            inc(nc.vector.tensor_reduce(red[:], comb[:], AX.X, ALU.add))
            at("two")
            inc(nc.vector.reciprocal(red[:], red[:]))
            at("rtwo")
            inc(tt_op(comb[:], comb[:], wide, ALU.mult))
            at("back")
            inc(nc.vector.tensor_copy(lrow[:, 0:NP_TOK], ps[0:E, 4]))
            inc(nc.vector.tensor_copy(crow[:, 0:NP_TOK], ps[0:E, 5]))
            inc(nc.vector.tensor_copy(lrow[:, NP_TOK:T], ps[0:E, 6, 0:NS_TOK]))
            inc(nc.vector.tensor_copy(crow[:, NP_TOK:T], ps[0:E, 6, NS_TOK:2 * NS_TOK]))
            at("backed")
            inc(nc.vector.tensor_tensor_scan(cum[:], lrow[:], lrow[:], 0.0, ALU.add, ALU.bypass))
            at("cum")
            inc(tt_op(lrow[:], lrow[:], cum[:], ALU.mult))
            at("place")
            inc(ts_op(lrow[:], lrow[:], -1.0, None, ALU.add))
            n = cum[:, T - 1:T]
            inc(ts_op(passes[:, 0:1], n, float(CAP), 1.0, ALU.is_gt, ALU.add))
            at("pass1")
            inc(stt_op(passes[:, 0:1], n, float(2 * CAP), passes[:, 0:1], ALU.is_gt, ALU.add))
            at("pass2")
            inc(stt_op(passes[:, 0:1], n, float(3 * CAP), passes[:, 0:1], ALU.is_gt, ALU.add))
            at("last")
            inc(nc.vector.tensor_copy(passes[:, 1:2], ps[0:E, 7, 0:1]))
            at("ends")
            inc(tt_op(passes[:, 2:3], passes[:, 1:2], passes[:, 0:1], ALU.subtract))
            at("first")
            inc(ts_op(J[:], iota[0:E, 0:NJ], passes[:, 2:3], None, ALU.is_ge))
            at("J0")
            inc(stt_op(J[:], iota[0:E, 0:NJ], passes[:, 1:2], J[:], ALU.is_lt, ALU.mult))
            at("J")
            inc(stt_op(lrow[:], passes[:, 2:3].to_broadcast([E, T]), float(CAP), lrow[:], ALU.mult,
                       ALU.add))
            at("table")
            inc(stt_op(postj[:].rearrange("p j t -> p t j"), iota[:, 0:NJ].unsqueeze(1).to_broadcast([P, 5, NJ]),
                       -float(CAP), ps[:, 4, 0:5 * NJ].rearrange("p (t j) -> p t j", j=NJ), ALU.mult,
                       ALU.add))
            inc(nc.vector.tensor_copy(combj[:].rearrange("p j t -> p t j"),
                                      ps[:, 5, 0:5 * NJ].rearrange("p (t j) -> p t j", j=NJ)))
            inc(ts_op(jt[:, 0:NJ], ps[0:1, 6, 0:NJ], float(S_JOB), None, ALU.mult))
            inc(nc.vector.tensor_copy(jt[:, NJ:NJ + 1], ps[0:1, 6, NJ:NJ + 1]))
            at("tables")
            for i in range(5):
                rws = P if i < 4 else NS_TOK
                dve.wait_ge(ht_turned, 2 * i + 2)
                nc.vector.tensor_copy(ht_lo[0:rws, i].rearrange("p (a d) -> p a d", a=2),
                                      ps[0:rws, 6:8]).then_inc(ht_lo_ready, 1)
            for buf in (yt_hi, yt_lo):
                nc.vector.memset(buf[:].bitcast(F32), 0.0).then_inc(yt_lo_ready, 1)
            for ct in range(2):
                nc.vector.memset(GT[:, ct].bitcast(F32), 0.0).then_inc(gt_ready, 1)

        def addends(b):
            return ps[:, b, 0:2 * CAP].rearrange("p (a c) -> p c a", a=2)

        def scattered_in(j):
            for m in range(KT):
                dve.wait_ge(scattered, j * KT + (m + 1))
                b = 4 + 2 * (m % 2)
                tt_op(halves(x[:, m]), halves(x[:, m]), ps[:, b:b + 2, 0:HALF], ALU.add).then_inc(
                    x_added, 1)

        def expert_pass(j):
            s0, f0 = MOE0, j * FE_TILES
            nc.vector.tensor_copy(Jb[:], J[:, bass.ds(j, 1)].to_broadcast([E, P])).then_inc(job_cols, 1)
            nc.vector.tensor_copy(places[:], part_index[:, bass.ds(j, 1)].rearrange(
                "p o t -> p (o t)")).then_inc(job_cols, 1)
            for f in range(FE_TILES):
                split_lo(s0 + gate_slab(f) + 2, j)
                if f > 0:
                    lo_of_act(f - 1, f0)
                dve.wait_ge(slab_done, j * S_JOB + (s0 + gate_slab(f) + 1))
                b = 2 * (f % 2)
                if f > 0:
                    dve.wait_ge(m_act, f0 + f)
                nc.vector.tensor_reduce(gsum[:], addends(b), AX.X, ALU.add).then_inc(m_sum, 1)
                split_lo(s0 + gate_slab(f) + 3, j)
                dve.wait_ge(m_sig, f0 + (f + 1))
                tt_op(ma[:, f % 2], gsum[:], msig[:], ALU.mult).then_inc(m_gate, 1)
                if f == 1:
                    scattered_in(j)
                    dve.wait_ge(placed, j + 1)
                    dve.wait_ge(job_cols, j * 2 + 2)
                    for ct in range(2):
                        ts_op(halves(GT[:, ct]), ps[:, 4:6, 0:HALF], places[:, ct:ct + 1], None,
                              ALU.is_equal).then_inc(gt_ready, 1)
                    dve.wait_ge(weighed, j + 1)
                    for ct in range(2):
                        rws = slice(0, (P, REST)[ct])
                        nc.vector.tensor_copy(cw[rws, ct:ct + 1], ps[rws, 6, 400 + ct:401 + ct]).then_inc(
                            cw_ready, 1)
                dve.wait_ge(slab_done, j * S_JOB + (s0 + gate_slab(f) + 2))
                nc.vector.tensor_reduce(usum[:], addends(b + 1), AX.X, ALU.add).then_inc(m_up, 1)
                dve.wait_ge(m_up, f0 + (f + 1))
                tt_op(ma[:, f % 2], ma[:, f % 2], usum[:], ALU.mult).then_inc(m_act, 1)
                if f > 0:
                    split_lo(s0 + down_slab(f - 1) + 2, j)
                if f == 5:
                    prepare(j + 1)
            lo_of_act(FE_TILES - 1, f0)
            split_lo(s0 + down_slab(FE_TILES - 1) + 2, j)
            gathered_lo(j + 1)
            for ct in range(2):
                rws = slice(0, (P, REST)[ct])
                dve.wait_ge(yt_hi_ready, j * 2 + (ct + 1))
                wide = yt_hi[rws, ct].bitcast(F32).rearrange("p (a d) -> p a d", a=2)
                stt_op(yt_lo[rws, ct].rearrange("p (a d) -> p a d", a=2), y_ps(ct),
                       cw[rws, ct:ct + 1], wide, ALU.mult, ALU.subtract).then_inc(yt_lo_ready, 1)
            dve.wait_ge(yt_lo_ready, j * 2 + 4)

        def lo_of_act(f, f0):
            dve.wait_ge(m_hi, f0 + (f + 1))
            tt_op(ma_lo[:, f % 2], ma[:, f % 2], ma_hi[:, f % 2].bitcast(F32), ALU.subtract).then_inc(
                m_lo, 1)

        dve.wait_ge(loaded, 64)
        split_lo(0)
        split_lo(1)
        for l in range(DEPTH):
            nb, ob = l * LAYER1, l * O_LAYER1
            norm(2 * l, 3 * l)
            inputs(l, nb, ob)
            gla(l)
            gla_decode(l)
            mlstm_rows(l)
            mlstm(l)
            mlstm_decode(l)
            pool_mix(l)
            head_norm(l)
            gates(l, nb, ob)
            merge(l, nb, ob)
            norm(2 * l + 1, 3 * l + 2)
            if l == 0:
                feed_forward(S_MIX, O_MIX)
            else:
                routing()
                passes_dve = dve.value_load(jt[:, NJ:NJ + 1], min_val=E, max_val=NJ - 2)
                prepare(0)
                gathered_lo(0)
                with dve.Fori(0, passes_dve) as j:
                    expert_pass(j)
                scattered_in(passes_dve)
        norm(4, 6)

    @block.tensor
    def _(pe):
        mm = nc.tensor.matmul

        def exact(out, a, b, start=True, stop=True):
            return mm(out, a, b, start=start, stop=stop, skip_group_check=True)

        def tile_product(out, slot, tile, in_hi, in_lo, kk, first, last):
            for wgt_part, in_part, ends in ((w_hi, in_hi, 0), (w_hi, in_lo, 0), (w_lo, in_hi, 1)):
                for hf in range(2):
                    ins = mm(out[:, hf], wgt_part[:, slot, tile], in_part[:, kk, HALF * hf:HALF * (hf + 1)],
                             start=first and not ends and in_part is in_hi, stop=last and bool(ends))
            return ins

        def slab_ready(n):
            pe.wait_ge(lo_ready, n + 1)

        def out_free(o):
            if o >= 2:
                pe.wait_ge(*evac(o - 2))

        def slab_to_out(n, o, in_hi, in_lo):
            slab_ready(n)
            out_free(o)
            for kk in range(KT):
                ins = tile_product(out_ps(o), n % SPL, kk, in_hi, in_lo, kk, kk == 0, kk == KT - 1)
            ins.then_inc(slab_done, 1)

        def mean_squares(r, bank_free):
            for s, n in bank_free:
                pe.wait_ge(s, n)
            for kk in range(KT):
                pe.wait_ge(squared, 8 * r + kk + 1)
                for hf in range(2):
                    ins = exact(ps[:, 4 + hf, 0:HALF], ones, sq[:, kk % 2, HALF * hf:HALF * (hf + 1)],
                                kk == 0, kk == KT - 1)
                ins.then_inc(squares_used, 1)

        def normed_in(hs):
            pe.wait_ge(h_lo_ready, 8 * (hs + 1))

        def gla(l, ob):
            pe.wait_ge(ggw_in, 16 * (l + 1))
            pe.wait_ge(*evac(ob + Z_SMALL))
            pe.wait_ge(*evac(ob + Z_MO - 1))
            pe.wait_ge(*evac(ob + Z_MO - 2))
            for j in range(2):
                for hf in range(2):
                    ins = exact(ps[:, 4 + 2 * j + hf, 0:HALF], ggw[:, j * P:(j + 1) * P],
                                glr[:, HALF * hf:HALF * (hf + 1)])
            ins.then_inc(g.sem, 1)
            pe.wait_ge(g.sem, g.after("qk", l))
            for tt in range(TT):
                for h in range(H):
                    ins = nc.tensor.transpose(ps[:, 4 + tt, h * P:(h + 1) * P], gv[:, h, token_tile(tt)],
                                              ident)
                ins.then_inc(g.sem, 1)
            pe.wait_ge(g.sem, g.after("copy", l))
            for tt in range(TT):
                for j in range(2):
                    ins = nc.tensor.transpose(ps[:, 4 + tt, j * P:(j + 1) * P], gk[:, j, token_tile(tt)],
                                              ident)
                ins.then_inc(g.sem, 1)
            pe.wait_ge(g.sem, g.after("copyk", l))
            for tt in range(TT):
                rep = TT * l + tt
                if tt > 0:
                    pe.wait_ge(gc.sem, gc.after("ns", rep - 1))
                for h in range(H):
                    exact(ps[:, 4, h * P:(h + 1) * P], gk[:, h // 2, token_tile(tt)],
                          qz[:, h, token_tile(tt)])
                for j in range(2):
                    ins = exact(ps[:, 5, 256 * j:256 * (j + 1)], gkt[:, tt, j * P:(j + 1) * P],
                                gvt[:, tt, 256 * j:256 * (j + 1)])
                ins.then_inc(gc.sem, 1)
                pe.wait_ge(gc.sem, gc.after("sin", rep))
                for h in range(H):
                    out = ps[:, 6, h * P:(h + 1) * P]
                    exact(out, gvt[:, tt, h * P:(h + 1) * P], att[:, h], True, False)
                    ins = exact(out, S_in[:, h // 2], qz[:, h, token_tile(tt)], False, True)
                ins.then_inc(gc.sem, 1)

        def gla_decode(l):
            pe.wait_ge(gc.sem, gc.after("ns", TT * l + TT - 1))
            for j in range(2):
                rep = 2 * l + j
                if j > 0:
                    pe.wait_ge(dg.sem, dg.after("oc", rep - 1))
                sa = slice(NP_TOK, T)
                nc.tensor.transpose(ps[0:NS_TOK, 4, 0:P], gk[:, j, sa], ident)
                nc.tensor.transpose(ps[0:NS_TOK, 4, P:2 * P], gv[:, 2 * j, sa], ident)
                nc.tensor.transpose(ps[0:NS_TOK, 4, 2 * P:3 * P], gv[:, 2 * j + 1, sa],
                                    ident).then_inc(dg.sem, 1)
                pe.wait_ge(dg.sem, dg.after("diag", rep))
                for half in range(2):
                    for c in range(2):
                        ins = exact(ps[64 * half:64 * half + 64, 4 + c],
                                    gt8[:, 0, 64 * half:64 * half + 64],
                                    gdiag[:, half, 4 * c:4 * c + 4])
                ins.then_inc(dg.sem, 1)
                pe.wait_ge(dg.sem, dg.after("add", rep))
                for b in range(NS_TOK):
                    ins = exact(ps[:, 6, 2 * b:2 * b + 2], Ss[:, b], qz[:, 2 * j:2 * j + 2, NP_TOK + b])
                ins.then_inc(dg.sem, 1)

        def mlstm(l):
            pe.wait_ge(rows.sem, rows.after("sexp", l))
            pe.wait_ge(dg.sem, dg.after("oc", 2 * l + 1))
            for tt in range(TT):
                nc.tensor.transpose(ps[:, 4, H * tt:H * tt + H], row_i[:, token_tile(tt)],
                                    ident[0:H, 0:H])
            for a in range(3):
                nc.tensor.transpose(ps[0:NS_TOK, 4, 32 + H * a:32 + H * a + H], w3[:, a],
                                    ident[0:H, 0:H])
            for h in range(H):
                ins = exact(ps[:, 5, 24 * h:24 * h + 24], select[:, h], w3[:].rearrange("h a b -> h (a b)"))
            ins.then_inc(rows.sem, 1)
            pe.wait_ge(rows.sem, rows.after("turned", l))
            pe.wait_ge(st_Ss, 32 * (l + 1))
            for h in range(H):
                rep = H * l + h
                at = lambda name: pe.wait_ge(ml.sem, ml.after(name, rep))
                if h > 0:
                    pe.wait_ge(ml.sem, ml.after("h", rep - 1))
                for tt in range(TT):
                    nc.tensor.transpose(ps[:, 4, tt * P:(tt + 1) * P], k[:, h, token_tile(tt)], ident)
                    nc.tensor.transpose(ps[:, 5, tt * P:(tt + 1) * P], v[:, h, token_tile(tt)], ident)
                exact(ps[:, 6], select[:, h], row_M[:, 0:NP_TOK]).then_inc(ml.sem, 1)
                at("scol")
                for tt in range(2):
                    ins = exact(ps[:, 4 + tt, 0:NP_TOK - tt * P], k[:, h, token_tile(tt)],
                                q[:, h, tt * P:NP_TOK])
                ins.then_inc(ml.sem, 1)
                at("p01")
                for tt in range(2, 4):
                    c = 256 * (tt - 2)
                    ins = exact(ps[:, 4, c:c + NP_TOK - tt * P], k[:, h, token_tile(tt)],
                                q[:, h, tt * P:NP_TOK])
                ins.then_inc(ml.sem, 1)
                at("vw")
                for tt in range(TT):
                    exact(ps[:, 6, tt * P:], vt[:, tt], wgt[:, tt, tt * P:], tt == 0, tt == TT - 1)
                for tt in range(TT):
                    exact(ps[:, 7, tt * P:], ones, wgt[:, tt, tt * P:], tt == 0, tt == TT - 1)
                exact(ps[:, 4], select[:, h], row_f[:, 0:NP_TOK])
                for tt in range(TT):
                    exact(ps[:, 5, 0:P], vw[:, tt], kt[:, tt], tt == 0, tt == TT - 1)
                for tt in range(TT):
                    ins = exact(ps[0:1, 5, P:2 * P], wcol[:, tt:tt + 1], kt[:, tt], tt == 0, tt == TT - 1)
                ins.then_inc(ml.sem, 1)

        def mlstm_decode(l):
            for h in range(H):
                rep = H * l + h
                at = lambda name: pe.wait_ge(ds.sem, ds.after(name, rep))
                at("vs")
                nc.tensor.transpose(ps[0:NS_TOK, 4, 0:P], vs8[:], ident)
                nc.tensor.transpose(ps[0:NS_TOK, 4, P:2 * P], k[:, h, NP_TOK:T], ident)
                nc.tensor.transpose(ps[0:NS_TOK, 4, 2 * P:3 * P], q[:, h, NP_TOK:T],
                                    ident).then_inc(ds.sem, 1)
                at("diag")
                for c in range(2):
                    exact(ps[:, 4 + c], tok8[:, 0], diag[:, 0, 4 * c:4 * c + 4])
                for c in range(2):
                    ins = exact(ps[:, 6 + c], ones[0:NS_TOK], diag[:, 1, 4 * c:4 * c + 4])
                ins.then_inc(ds.sem, 1)
                at("rd")
                exact(ps[:, 4, 0:NS_TOK], ones[0:NS_TOK], rdiag[:]).then_inc(ds.sem, 1)

        def pool_mix(l):
            for gi in range(4):
                pe.wait_ge(po.sem, po.after(f"w{gi}", l))
                for hf in range(2):
                    ins = exact(ps[:, 4 + hf, 0:HALF], pw[:, gi], pd[:, HALF * hf:HALF * (hf + 1)])
                ins.then_inc(po.sem, 1)

        def head_norm(l):
            pe.wait_ge(po.sem, po.after("y3", l))
            for t in range(8):
                i = 8 * l + t
                pe.wait_ge(hn_sq, i + 1)
                if t >= 2:
                    pe.wait_ge(hn_rs, 2 * i - 3)
                for hf in range(2):
                    ins = exact(ps[:, 4 + 2 * (t % 2) + hf, 0:HALF], ones,
                                sq[:, t % 2, HALF * hf:HALF * (hf + 1)])
                ins.then_inc(hn_ssq, 1)

        def merge(l, nb, ob):
            for mp in range(KT // 2):
                n0, o0 = nb + S_GATE + PAIR_SLABS * mp, ob + O_GATE + 12 * mp
                for s, outs in ((0, (0,)), (1, (1,)), (2, ((2, 0), (3, 1))), (3, (4,)), (4, (5,)),
                                (5, (6,)), (6, ((7, 0), (8, 1))), (7, (9,)), (8, ((10, 2), (11, 2)))):
                    n = n0 + s
                    if len(outs) == 1:
                        slab_to_out(n, o0 + outs[0], h_hi, h_lo)
                        continue
                    slab_ready(n)
                    pe.wait_ge(br_lo_ready, 12 * (l + 1))
                    for i, (out, branch) in enumerate(outs):
                        out_free(o0 + out)
                        for kk in range(4):
                            ins = tile_product(out_ps(o0 + out), n % SPL, 4 * i + kk, br_hi, br_lo,
                                               4 * branch + kk, kk == 0, kk == 3)
                    ins.then_inc(slab_done, 1)
            normed_in(3 * l + 1)
            for m in range(KT):
                slab_to_out(nb + S_OUT + m, ob + O_OUT + m, h_hi, h_lo)

        def feed_forward(nf, of):
            for i in range(2 * F_TILES):
                slab_to_out(nf + i, of + i, h_hi, h_lo)
            pe.wait_ge(act_lo, F_TILES)
            for s in range(F_TILES):
                n = nf + S_DOWN + s
                slab_ready(n)
                for tile in range(8):
                    m, f = divmod(8 * s + tile, F_TILES)
                    o = of + O_DOWN + m
                    if f == 0:
                        out_free(o)
                    ins = tile_product(out_ps(o), n % SPL, tile, a_hi, a_lo, f, f == 0, f == F_TILES - 1)
                ins.then_inc(slab_done, 1)


        def gather(p):
            pe.wait_ge(g_ready, p * 7 + 7)
            for m in range(KT):
                out = ps[:, m // 2, WIDE * (m % 2):WIDE * (m % 2 + 1)]
                for tt in range(5):
                    rws = P if tt < 4 else NS_TOK
                    for part in (ht_hi, ht_lo):
                        ins = mm(out, part[0:rws, tt, m * P:(m + 1) * P], G[0:rws, tt],
                                 start=m % 2 == 0 and tt == 0 and part is ht_hi, stop=True,
                                 skip_group_check=True)
            ins.then_inc(gathered, 1)

        def weigh(j):
            pe.wait_ge(job_cols, j * 2 + 2)
            pe.wait_ge(x_added, j * KT + (KT - 1))
            for hf in range(2):
                ins = exact(ps[:, 4 + hf, 0:HALF], Jb[:], lrow[:, HALF * hf:HALF * (hf + 1)])
            ins.then_inc(placed, 1)
            pe.wait_ge(x_added, j * KT + KT)
            for ct in range(2):
                c = slice(P * ct, min(CAP, P * (ct + 1)))
                for tt in range(5):
                    rws = P if tt < 4 else NS_TOK
                    ins = exact(ps[0:c.stop - c.start, 6, 400 + ct:401 + ct], G[0:rws, tt, c].bitcast(F32),
                                ccol[0:rws, tt:tt + 1], tt == 0, tt == 4)
            ins.then_inc(weighed, 1)

        def routing():
            slab_to_out(ROUTER, O_ROUTER, h_hi, h_lo)
            at = lambda name: pe.wait_ge(rt.sem, rt.after(name))
            at("logits")
            for i in range(5):
                rws = P if i < 4 else NS_TOK
                ins = nc.tensor.transpose(ps[0:rws, 4, E * i:E * (i + 1)], lrow[:, P * i:P * i + rws],
                                          ident[0:E, 0:E])
            ins.then_inc(rt.sem, 1)
            at("comb")
            for i in range(4):
                nc.tensor.transpose(ps[0:E, 4, P * i:P * (i + 1)], sel_t[:, i], ident)
                nc.tensor.transpose(ps[0:E, 5, P * i:P * (i + 1)], comb[:, i], ident)
            nc.tensor.transpose(ps[0:E, 6, 0:NS_TOK], sel_t[0:NS_TOK, 4], ident[0:NS_TOK, 0:NS_TOK])
            nc.tensor.transpose(ps[0:E, 6, NS_TOK:2 * NS_TOK], comb[0:NS_TOK, 4],
                                ident[0:NS_TOK, 0:NS_TOK]).then_inc(rt.sem, 1)
            at("pass3")
            exact(ps[0:E, 7, 0:1], keep_mask[0:E, 0:E], passes[:, 0:1]).then_inc(rt.sem, 1)
            at("shift")
            for i in range(5):
                rws = P if i < 4 else NS_TOK
                exact(ps[0:rws, 4, NJ * i:NJ * (i + 1)], lrow[:, P * i:P * i + rws], J[:])
                exact(ps[0:rws, 5, NJ * i:NJ * (i + 1)], crow[:, P * i:P * i + rws], J[:])
            exact(ps[0:1, 6, 0:NJ], part_index[0:E, 0, 0:1], J[:])
            exact(ps[0:1, 6, NJ:NJ + 1], ones[0:E, 0:1], passes[:, 0:1]).then_inc(rt.sem, 1)
            at("tables")
            for i in range(5):
                rws = P if i < 4 else NS_TOK
                if i > 0:
                    pe.wait_ge(ht_hi_ready, i)
                    pe.wait_ge(ht_lo_ready, i)
                for b, part in ((4, h_hi), (6, h_lo)):
                    for kk in range(KT):
                        ins = nc.tensor.transpose(
                            ps[0:rws, b + kk // 4, P * (kk % 4):P * (kk % 4 + 1)],
                            part[:, kk, P * i:P * i + rws].bitcast(F32), ident)
                    ins.then_inc(ht_turned, 1)
            pe.wait_ge(ht_hi_ready, 5)
            pe.wait_ge(ht_lo_ready, 5)

        def slab_ready_of(j, i):
            pe.wait_ge(lo_ready, j * S_JOB + (MOE0 + i + 1))

        def scatter(j):
            pe.wait_ge(yt_lo_ready, j * 2 + 2)
            pe.wait_ge(gt_ready, j * 2 + 2)
            for m in range(KT):
                if m >= 2:
                    pe.wait_ge(x_added, j * KT + (m - 1))
                for i, (ct, part) in enumerate(((0, yt_hi), (0, yt_lo), (1, yt_hi), (1, yt_lo))):
                    rws = slice(0, (P, REST)[ct])
                    for hf in range(2):
                        ins = mm(ps[:, 4 + 2 * (m % 2) + hf, 0:HALF], part[rws, ct, m * P:(m + 1) * P],
                                 GT[rws, ct, HALF * hf:HALF * (hf + 1)], start=i == 0, stop=i == 3)
                ins.then_inc(scattered, 1)

        def expert_pass(j):
            s0, f0 = MOE0, j * FE_TILES

            def gate_or_up(f, i):
                s = gate_slab(f) + i
                slab_ready_of(j, s)
                out = ps[:, 2 * (f % 2) + i]
                for kk in range(KT):
                    mm(out[:, 0:2 * CAP], w_hi[:, (s0 + s) % SPL, kk], hg[:, kk], start=kk == 0,
                       stop=False, skip_group_check=True)
                    ins = mm(out[:, 0:WIDE], w_lo[:, (s0 + s) % SPL, kk], hg[:, kk, 0:WIDE],
                             start=False, stop=kk == KT - 1, skip_group_check=True)
                ins.then_inc(slab_done, 1)

            def down(f):
                s = down_slab(f)
                slab_ready_of(j, s)
                pe.wait_ge(m_lo, f0 + (f + 1))
                for ct in range(2):
                    c = slice(P * ct, min(CAP, P * (ct + 1)))
                    for a, (t, w) in enumerate(((ma_hi, w_hi), (ma_hi, w_lo), (ma_lo, w_hi))):
                        for hf in range(2):
                            ins = mm(y_ps(ct)[:, hf], t[:, f % 2, c],
                                     w[:, (s0 + s) % SPL, 4 * hf:4 * hf + 4],
                                     start=f == 0 and a == 0, stop=f == FE_TILES - 1 and a == 2)
                ins.then_inc(slab_done, 1)

            pe.wait_ge(hg_lo_ready, j * 2 + 2)
            for f in range(FE_TILES):
                if f >= 2:
                    pe.wait_ge(m_act, f0 + (f - 1))
                gate_or_up(f, 0)
                if f == 1:
                    scatter(j)
                    weigh(j)
                gate_or_up(f, 1)
                if f == 1:
                    pe.wait_ge(gt_ready, j * 2 + 4)
                    pe.wait_ge(cw_ready, j * 2 + 2)
                if f > 0:
                    down(f - 1)
            pe.wait_ge(m_act, f0 + FE_TILES)
            gather(j + 1)
            down(FE_TILES - 1)

        pe.wait_ge(loaded, 64)
        for l in range(DEPTH):
            nb, ob = l * LAYER1, l * O_LAYER1
            mean_squares(2 * l, [])
            normed_in(3 * l)
            for i in range(Z_MO):
                slab_to_out(nb + i, ob + i, h_hi, h_lo)
            gla(l, ob)
            gla_decode(l)
            mlstm(l)
            mlstm_decode(l)
            pool_mix(l)
            head_norm(l)
            for i in range(Z_MO, N_Z):
                slab_to_out(nb + i, ob + i, h_hi, h_lo)
            merge(l, nb, ob)
            mean_squares(2 * l + 1, [])
            normed_in(3 * l + 2)
            if l == 0:
                feed_forward(S_MIX, O_MIX)
            else:
                routing()
                passes_pe = pe.value_load(jt[:, NJ:NJ + 1], min_val=E, max_val=NJ - 2)
                gather(0)
                with pe.Fori(0, passes_pe) as j:
                    expert_pass(j)
                scatter(passes_pe)
        mean_squares(4, [(x_added, passes_pe * KT + KT)])

    ctx.close()


def _tiles(w):
    kk, m = w.shape
    return w.reshape(kk // P, P, m // P, P).transpose(2, 1, 0, 3)


def _columns(w, groups):
    return [w[:, c:c + P].reshape(-1, P, P).transpose(1, 0, 2) for c in groups]


def _slabs(a):
    out = []
    widths = (512, 512, 512, 4, 4, 512, 256, 256, 512, 16, 512, 512, 3072)
    mq, mk, mv, mi, mf, mo, gq, gk, gv, glr, go, pu, gates = np.cumsum((0,) + widths[:-1]).tolist()
    for l in range(DEPTH):
        w = a["w_in"][l]
        small = np.zeros((D, P), w.dtype)
        small[:, 0:4], small[:, 32:36], small[:, 64:80] = (
            w[:, mi:mi + 4], w[:, mf:mf + 4], w[:, glr:glr + 16])
        out += _columns(small, (0,))
        for start, tiles in ((gk, 2), (gq, 2), (gv, 4), (mq, 4), (mk, 4), (mv, 4), (pu, 4), (mo, 4), (go, 4)):
            out += _columns(w, range(start, start + tiles * P, P))
        wb = a["w_branch"][l]
        for m in range(0, D, 2 * P):
            half = {(n, c): _columns(wb[n], (c,))[0] for n in range(3) for c in (m, m + P)}
            for c in (m, m + P):
                out += _columns(w, (gates + c, gates + D + c))
                out.append(np.concatenate((half[0, c], half[1, c]), 1))
                out += _columns(w, (gates + 2 * D + c,))
            out.append(np.concatenate((half[2, m], half[2, m + P]), 1))
        out += list(_tiles(a["w_out"][l]))
        if l == 0:
            up, gate = _tiles(a["ffn_wu"][0]), _tiles(a["ffn_wg"][0])
            for f in range(F_TILES):
                out += [gate[f], up[f]]
            down = _tiles(a["ffn_wd"][0]).transpose(0, 2, 1, 3).reshape(-1, 8, P, P)
            out += list(down.transpose(0, 2, 1, 3))
        else:
            router = np.zeros((D, P), w.dtype)
            router[:, 0:E] = a["router_w"][0]
            out += _columns(router, (0,))
            for e in range(E):
                up, gate = _tiles(a["moe_wu"][0, e]), _tiles(a["moe_wg"][0, e])
                down = a["moe_wd"][0, e].reshape(FE_TILES, P, KT, P)
                for f in range(FE_TILES):
                    out += [gate[f], up[f]] + [down[f - 1]] * (f > 0)
                out.append(down[FE_TILES - 1])
    assert len(out) == N_SLABS
    return np.stack(out)


def _constants():
    con = np.zeros((P, N_CONST), np.float32)
    con[:, C_ID:C_ID + P] = np.eye(P)
    con[:, C_ONE:C_ONE + P] = 1
    causal = np.arange(P)[:, None] <= np.arange(P)[None, :]
    con[:, C_NEG:C_NEG + P] = np.where(causal, 0, MASKED)
    con[:, C_KEEP:C_KEEP + P] = causal
    for r in range(H):
        con[r, C_SEL + r * P:C_SEL + (r + 1) * P] = 1
    for gi, w in enumerate(WINDOWS):
        con[:, C_INV + 16 * gi:C_INV + 16 * gi + 16] = 1 / np.minimum(np.arange(16) + 1, w)
    con[:, C_IOTA:C_IOTA + WIDE] = np.arange(WIDE)
    con[:, C_PART:C_PART + 2 * NJ] = (np.arange(P)[:, None, None] + CAP * np.arange(NJ)[:, None] +
                                      P * np.arange(2)).reshape(P, 2 * NJ)
    con[:, C_TIE:C_TIE + 64] = (np.arange(8)[None, :] < np.arange(8)[:, None]).reshape(1, 64)
    con[:, C_EPS] = EPS
    con[:64, C_HM], con[64:, C_HM + 1] = 1, 1
    return con


def _vector(v):
    return v.reshape(-1, P).T


def kernel(**inputs):
    import concourse.bacc as bacc
    from concourse.bass_utils import run_bass_kernel_spmd

    a = {name: np.asarray(value) for name, value in inputs.items()}
    tokens = np.concatenate((a["x_prompt"].reshape(NP_TOK, D), a["x_sample"].reshape(NS_TOK, D)))
    vectors = np.stack([np.concatenate([_vector(a[n][l]) for n in (
        "norm1_g", "norm2_g", "mlstm_norm_g", "gla_norm_g", "gla_gate_b", "pool_scale")] +
        [_vector(a["final_norm_g"])], 1) for l in range(DEPTH)], 1)
    arrays = {
        "slabs": _slabs(a),
        "x_in": tokens.reshape(T, KT, P).transpose(2, 1, 0),
        "vectors": vectors,
        "if_bias": a["mlstm_if_bias"].transpose(2, 0, 1),
        "gate_w": a["gla_gate_w"],
        "pool_w": a["pool_w"].transpose(0, 2, 1, 3),
        "consts": _constants(),
        "ml_m0": a["state_mlstm_m"].transpose(0, 2, 1),
        "ml_n0": a["state_mlstm_n"],
        "ml_C0": a["state_mlstm_C"].transpose(0, 2, 3, 1, 4),
        "gla_S0": a["state_gla_S"].reshape(DEPTH, NS_TOK, 2, P, P).transpose(0, 2, 3, 1, 4),
        "pool_in": a["state_pool_buf"].reshape(DEPTH, NS_TOK, POOL_BUF, 4, P).transpose(0, 4, 3, 1, 2),
        "pool_old": a["state_pool_buf"][:, :, 1:],
    }
    outs = {
        "y_out": (P, KT, T), "C_p": (DEPTH, H, P, P), "C_s": (DEPTH, H, P, NS_TOK, P),
        "n_p": (DEPTH, 1, H * P), "n_s": (DEPTH, NS_TOK, H, P), "m_p": (DEPTH, H, 1),
        "m_s": (DEPTH, H, NS_TOK), "S_p": (DEPTH, P, 2, P), "S_s": (DEPTH, 2, P, NS_TOK, P),
        "pool_u": (DEPTH, P, 4, POOL_BUF + NS_TOK), "pool_keep": (DEPTH, NS_TOK, POOL_BUF - 1, 512),
    }
    nc = bacc.Bacc("TRN2", target_bir_lowering=False, num_devices=1)
    args = []
    for name in arrays:
        arrays[name] = np.ascontiguousarray(arrays[name])
        args.append(nc.dram_tensor(name, arrays[name].shape, F32, kind="ExternalInput").ap())
    for name, shape in outs.items():
        args.append(nc.dram_tensor(name, shape, F32, kind="ExternalOutput").ap())
    decoder(nc, *args)
    got = run_bass_kernel_spmd(nc, [arrays], core_ids=[0]).results[0]

    y = got["y_out"].transpose(2, 1, 0).reshape(T, D)
    u = got["pool_u"].transpose(0, 3, 2, 1).reshape(DEPTH, POOL_BUF + NS_TOK, 512)
    return (
        y[:NP_TOK].reshape(1, NP_TOK, D), y[NP_TOK:].reshape(NS_TOK, 1, D),
        got["C_p"].reshape(DEPTH, 1, H, P, P), got["C_s"].transpose(0, 3, 1, 2, 4),
        got["n_p"].reshape(DEPTH, 1, H, P), got["n_s"].reshape(DEPTH, NS_TOK, H, P),
        got["m_p"].reshape(DEPTH, 1, H), got["m_s"].transpose(0, 2, 1),
        got["S_p"].transpose(0, 2, 1, 3).reshape(DEPTH, 1, H, DK, P),
        got["S_s"].transpose(0, 3, 1, 2, 4).reshape(DEPTH, NS_TOK, H, DK, P),
        u[:, None, :POOL_BUF], np.concatenate((got["pool_keep"], u[:, POOL_BUF:][:, :, None]), 2),
    )
```

```python
from contextlib import ExitStack

import numpy as np

import concourse.bass as bass
from concourse import mybir

F32 = mybir.dt.float32
F32R = mybir.dt.float32r
ALU = mybir.AluOpType
ACT = mybir.ActivationFunctionType
AX = mybir.AxisListType

P = 128
DEPTH = 2
D = 1024
KT = D // P
NP_TOK, NS_TOK = 512, 8
T = NP_TOK + NS_TOK
HALF = T // 2
TT = NP_TOK // P
H = 4
DK = 64
WINDOWS = (2, 4, 8, 16)
POOL_BUF = 15
F_TILES = 2816 // P
E = 8
NJ = 16
FE_TILES = 1408 // P
CAP = 168
WIDE = 192
REST = CAP - P
EPS = 1e-6
MASKED = -1e30

Z_SMALL, Z_GK, Z_GQ, Z_GV, Z_Q, Z_K, Z_V, Z_PU, Z_MO = 0, 1, 3, 5, 9, 13, 17, 21, 25
N_GATES = 2 * H + 3 * KT
S_BRANCH = Z_MO + N_GATES
S_OUT = S_BRANCH + KT // 2 * 3
S_MIX = S_OUT + KT
S_DOWN = 2 * F_TILES
S_FFN = S_DOWN + F_TILES
S_JOB = 3 * FE_TILES
LAYER1 = S_MIX + S_FFN
ROUTER = LAYER1 + S_MIX
MOE0 = ROUTER + 1
N_SLABS = MOE0 + E * S_JOB
O_BRANCH = Z_MO + N_GATES
O_OUT = O_BRANCH + KT // 2 * 6
O_MIX = O_OUT + KT
O_DOWN = 2 * F_TILES
O_FFN = O_DOWN + KT
O_LAYER1 = O_MIX + O_FFN
O_ROUTER = O_LAYER1 + O_MIX
RAW = 4
SPL = 3
GATE_PLACES = 6

C_ID, C_ONE, C_NEG, C_KEEP, C_SEL, C_INV, C_IOTA = 0, 128, 256, 384, 512, 1024, 1088
C_PART = C_IOTA + WIDE
C_TIE, C_EPS, C_HM = C_PART + 2 * NJ, C_PART + 2 * NJ + 64, C_PART + 2 * NJ + 65
N_CONST = C_HM + 2
V_N1, V_N2, V_ML, V_GLA, V_GB, V_PS, V_FN, N_VEC = 0, 8, 16, 20, 24, 26, 30, 38


class Steps:

    def __init__(self, sem, **phases):
        self.sem, self.end, n = sem, {}, 0
        for name, k in phases.items():
            n += k
            self.end[name] = n
        self.total = n

    def after(self, name, rep=0):
        return rep * self.total + self.end[name]


JOB_PLACE = [i % RAW for i in range(6 * RAW)] + [i % (RAW - 1) for i in range(S_JOB - 6 * RAW)]


def place(n):
    return n % RAW if n < MOE0 else (MOE0 + JOB_PLACE[(n - MOE0) % S_JOB]) % RAW


def arrivals(n, j=0):
    before = sum(place(m) == place(n) for m in range(n + 1))
    return 16 * before + j * (16 * sum(place(m) == place(n) for m in range(MOE0, MOE0 + S_JOB)))


def down_slab(f):
    return 3 * f + 4 if f < FE_TILES - 1 else S_JOB - 1


REST_ON_GPSIMD = [2, 3] + [down_slab(f) for f in range(FE_TILES)]


def rest_on_gpsimd(n):
    return n >= MOE0 and (n - MOE0) % S_JOB in REST_ON_GPSIMD


def rests(n, j=0):
    own = rest_on_gpsimd(n)
    return (sum(rest_on_gpsimd(m) == own for m in range(n + 1)) +
            j * sum(rest_on_gpsimd(m) == own for m in range(MOE0, MOE0 + S_JOB)))


def slab_before(n):
    return max(m for m in range(n) if place(m) == place(n))


def token_tile(tt):
    return slice(tt * P, (tt + 1) * P)


def branch_out(k):
    return O_BRANCH + k - 2 * H


def decoder(nc, slabs, x_in, vectors, if_bias, gate_w, pool_w, consts, ml_m0, ml_n0, ml_C0,
            gla_S0, pool_in, pool_old, y_out, C_p, C_s, n_p, n_s, m_p, m_s, S_p, S_s, pool_u,
            pool_keep, gates_kept):
    ctx = ExitStack()

    def sb(name, shape, dt=F32, where=ctx):
        return where.enter_context(nc.sbuf_tensor(name, shape, dt))

    def sem(name):
        return ctx.enter_context(nc.semaphore(name))

    ps = ctx.enter_context(nc.psum_tensor("ps", [P, 8, 512], F32))
    x = sb("x", [P, KT, T])
    h_hi = sb("h_hi", [P, KT, T], F32R)
    h_lo = sb("h_lo", [P, KT, T], F32R)
    raw = sb("raw", [P, RAW, KT, P])
    w_hi = sb("w_hi", [P, SPL, KT, P], F32R)
    w_lo = sb("w_lo", [P, SPL, KT, P], F32R)
    con = sb("con", [P, N_CONST])
    vec = sb("vec", [P, DEPTH, N_VEC])
    ifb = sb("ifb", [H, DEPTH, 2])
    sq = sb("sq", [P, 2, T])
    rs = sb("rs", [P, 2, T])

    ident = con[:, C_ID:C_ID + P]
    ones = con[:, C_ONE:C_ONE + P]
    neg_mask = con[:, C_NEG:C_NEG + P]
    keep_mask = con[:, C_KEEP:C_KEEP + P]
    select = con[0:H, C_SEL:C_SEL + H * P].rearrange("k (r c) -> k r c", c=P)
    inv_count = con[:, C_INV:C_INV + 64].rearrange("p (g t) -> p g t", t=16)
    iota = con[:, C_IOTA:C_IOTA + WIDE]
    part_index = con[:, C_PART:C_PART + 2 * NJ].rearrange("p (j a) -> p j a", a=2)
    tie = con[:, C_TIE:C_TIE + 64].rearrange("p (e j) -> p e j", j=8)
    eps = con[:, C_EPS:C_EPS + 1]
    head_half = con[:, C_HM:C_HM + 2]

    mix, early, late = ExitStack(), ExitStack(), ExitStack()
    br = sb("br", [P, 12, T], where=mix)
    gq = sb("gq", [P, 2, T], where=early)
    gk = sb("gk", [P, 2, T], where=early)
    gv = sb("gv", [P, H, T], where=early)
    q = sb("q", [P, H, T], where=early)
    k = sb("k", [P, H, T], where=early)
    v = sb("v", [P, H, T], where=early)
    row_i = sb("row_i", [H, T], where=early)
    row_f = sb("row_f", [H, T], where=early)
    row_b = sb("row_b", [H, T], where=early)
    row_M = sb("row_M", [H, T], where=early)
    acol = sb("acol", [P, TT, H], where=early)
    w3 = sb("w3", [H, 3, NS_TOK], where=early)
    w3b = sb("w3b", [P, H, 3 * NS_TOK], where=early)
    w3t = sb("w3t", [NS_TOK, 3, H], where=early)
    m_s0 = sb("m_s0", [H, NS_TOK], where=early)
    m_new = sb("m_new", [H, NS_TOK], where=early)
    m_inter = sb("m_inter", [H, NS_TOK], where=early)
    ea = sb("ea", [P, 2, NS_TOK], where=early)
    gla_mem, gla_a, gla_b, gla_c = ExitStack(), ExitStack(), ExitStack(), ExitStack()
    qz = sb("qz", [P, H, T], where=gla_mem)
    la = sb("la", [P, 2, T], where=gla_a)
    gvt = sb("gvt", [P, TT, H * P], where=gla_a)
    gkt = sb("gkt", [P, TT, 256], where=gla_a)
    ge = sb("ge", [P, 3, 2, TT], where=gla_a)
    S = sb("S", [P, 2, P], where=gla_a)
    gla_i = ExitStack()
    glr = sb("glr", [16, T], where=gla_i)
    ggw = sb("ggw", [16, 256], where=gla_i)
    gla_i.close()
    dec = sb("dec", [P, 2, T], where=gla_b)
    gla_b.close()
    att = sb("att", [P, H, P], where=gla_c)
    S_in = sb("S_in", [P, 2, P], where=gla_c)
    Ut = sb("Ut", [P, 2, P], where=gla_c)
    gla_c.close()
    gla_a.close()
    gd = ExitStack()
    Ss = sb("Ss", [P, NS_TOK, P], where=gd)
    gdiag = sb("gdiag", [NS_TOK, 2, NS_TOK, P], where=gd)
    gt8 = sb("gt8", [NS_TOK, 3, P], where=gd)
    gd.close()
    gla_mem.close()
    ml_mem = ExitStack()
    kt = sb("kt", [P, TT, P], where=ml_mem)
    vt = sb("vt", [P, TT, P], where=ml_mem)
    wgt = sb("wgt", [P, TT, NP_TOK], where=ml_mem)
    dm = sb("dm", [P, TT, P], where=ml_mem)
    den = sb("den", [P, NP_TOK], where=ml_mem)
    den2 = sb("den2", [P, NP_TOK], where=ml_mem)
    vw = sb("vw", [P, TT, P], where=ml_mem)
    wcol = sb("wcol", [P, TT], where=ml_mem)
    C_t = sb("C_t", [P, H, P], where=ml_mem)
    n_row = sb("n_row", [1, H * P], where=ml_mem)
    ml_mem.close()
    samp = ExitStack()
    Cs = sb("Cs", [P, NS_TOK, P], where=samp)
    Cq = sb("Cq", [P, NS_TOK, P], where=samp)
    diag = sb("diag", [NS_TOK, 2, NS_TOK, P], where=samp)
    tok8 = sb("tok8", [NS_TOK, 3, P], where=samp)
    n_s0 = sb("n_s0", [NS_TOK, H, P], where=samp)
    nq = sb("nq", [NS_TOK, P], where=samp)
    n_tmp = sb("n_tmp", [NS_TOK, P], where=samp)
    dcol = sb("dcol", [NS_TOK, 3], where=samp)
    rdiag = sb("rdiag", [NS_TOK, NS_TOK], where=samp)
    num8 = sb("num8", [P, NS_TOK], where=samp)
    vs8 = sb("vs8", [P, NS_TOK], where=samp)
    samp.close()
    pool_mem = ExitStack()
    pa = sb("pa", [P, 2, NP_TOK], where=pool_mem)
    pd = sb("pd", [P, T], where=pool_mem)
    pw = sb("pw", [P, 4, P], where=pool_mem)
    ext = sb("ext", [P, 4, NS_TOK, 16], where=pool_mem)
    pred = sb("pred", [P, NS_TOK], where=pool_mem)
    pool_mem.close()
    early.close()
    br_hi = sb("br_hi", [P, 12, T], F32R, where=late)
    br_lo = sb("br_lo", [P, 12, T], F32R, where=late)
    mixed = sb("mixed", [P, KT, T], where=late)
    gs = sb("gs", [P, GATE_PLACES, T], where=late)
    gt = sb("gt", [P, T], where=late)
    late.close()
    mix.close()

    ffn = ExitStack()
    a_hi = sb("a_hi", [P, F_TILES, T], F32R, where=ffn)
    a_lo = sb("a_lo", [P, F_TILES, T], F32R, where=ffn)
    sig = sb("sig", [P, T], where=ffn)
    af = sb("af", [P, 2, T], where=ffn)
    ffn.close()

    moe = ExitStack()
    ht_hi = sb("ht_hi", [P, 5, D], F32R, where=moe)
    ht_lo = sb("ht_lo", [P, 5, D], F32R, where=moe)
    lrow = sb("lrow", [E, T], where=moe)
    crow = sb("crow", [E, T], where=moe)
    cum = sb("cum", [E, T], where=moe)
    lt = sb("lt", [P, 5, E], where=moe)
    rk = sb("rk", [P, 2, 5 * E, E], where=moe)
    sel_t = sb("sel_t", [P, 5, E], where=moe)
    comb = sb("comb", [P, 5, E], where=moe)
    red = sb("red", [P, 5], where=moe)
    passes = sb("passes", [E, 3], where=moe)
    J = sb("J", [E, NJ], where=moe)
    jt = sb("jt", [1, NJ + 1], mybir.dt.int32, where=moe)
    postj = sb("postj", [P, NJ, 5], where=moe)
    combj = sb("combj", [P, NJ, 5], where=moe)
    pcol = sb("pcol", [P, 5], where=moe)
    ccol = sb("ccol", [P, 5], where=moe)
    Jb = sb("Jb", [E, P], where=moe)
    places = sb("places", [P, 2], where=moe)
    G = sb("G", [P, 5, WIDE], F32R, where=moe)
    GT = sb("GT", [P, 2, T], F32R, where=moe)
    hg = sb("hg", [P, KT, 2 * CAP], F32R, where=moe)
    gsum = sb("gsum", [P, CAP], where=moe)
    usum = sb("usum", [P, CAP], where=moe)
    msig = sb("msig", [P, CAP], where=moe)
    ma = sb("ma", [P, 2, CAP], where=moe)
    ma_hi = sb("ma_hi", [P, 2, CAP], F32R, where=moe)
    ma_lo = sb("ma_lo", [P, 2, CAP], F32R, where=moe)
    yt_hi = sb("yt_hi", [P, 2, D], F32R, where=moe)
    yt_lo = sb("yt_lo", [P, 2, D], F32R, where=moe)
    cw = sb("cw", [P, 2], where=moe)
    moe.close()
    last = ExitStack()
    yfin = sb("yfin", [P, KT, T], where=last)
    last.close()

    loaded = sem("loaded")
    arrived = [sem(f"arrived{i}") for i in range(RAW)]
    hi_ready, lo_ready = sem("hi_ready"), sem("lo_ready")
    lo_ready_gpsimd = sem("lo_ready_gpsimd")
    slab_done = sem("slab_done")
    emptied = [sem("emptied0"), sem("emptied1")]
    x_updated = sem("x_updated")
    squared, squares_used, ssq_done = sem("squared"), sem("squares_used"), sem("ssq_done")
    rs_steps, normed = sem("rs_steps"), sem("normed")
    h_hi_ready, h_lo_ready = sem("h_hi_ready"), sem("h_lo_ready")
    ggw_in, m0_in = sem("ggw_in"), sem("m0_in")
    n0_in, C_in, S_in_s, pool_loaded = sem("n0_in"), sem("C_in"), sem("S_in_s"), sem("pool_loaded")
    st_S, st_C, st_nm, st_Cs, st_ns, st_Ss, st_pu, st_y, st_keep = (
        sem(n) for n in ("st_S", "st_C", "st_nm", "st_Cs", "st_ns", "st_Ss", "st_pu", "st_y", "st_keep"))
    g = Steps(sem("gla"), loga_pe=1, y=2, abs=2, exp=1, ln=1, loga=1, scan=8, diff=8, clip=1, e=5,
              qk=11, turn=TT, copy=TT, turnk=TT, copyk=TT)
    gc = Steps(sem("gla_chunk"), att=1, mask=1, sin=2, o=1, ocopy=1, su=4, ns=2)
    dg = Steps(sem("gla_decode"), turn=1, copy=1, diag=2, outer=1, decay=1, add=1, o=1, oc=1)
    rows = Steps(sem("rows"), gates=2, abs=2, exp=1, ln=1, logf=1, b=1, a=1, M=1, m=2, enm=1,
                 inter=1, smax=1, sdiff=3, sexp=1, turn=1, turned=3)
    ml = Steps(sem("mlstm"), turn=1, copies=2, dm=1, exps=7, scol=1, sc01=1, p01=2, sc23=1, p23=2,
               vw=1, out=1, cst=2, absd=1, maxd=1, rec=1, h=1)
    ds = Steps(sem("mlstm_decode"), vs=1, turn=1, copy=1, diag=2, outer=1, carry=1, add=1, cq=1,
               num=1, nt=1, n=1, nq=1, den=1, dabs=1, dmax=1, drec=1, rd=1, rb=1, h=1)
    pool_phases = {"ext": 1}
    for gi in range(4):
        pool_phases[f"w{gi}"] = 2 * (gi + 1) + 5
        pool_phases[f"mm{gi}"] = 1
        pool_phases[f"y{gi}"] = 1
    po = Steps(sem("pool"), **pool_phases)
    hn_n, hn_sq, hn_ssq = sem("head_normed"), sem("head_squared"), sem("head_ssq")
    hn_rs, hn_used = sem("head_rs"), sem("head_squares_used")
    gated, br_hi_ready, br_lo_ready = sem("gated"), sem("br_hi_ready"), sem("br_lo_ready")
    gate_sig, mix_steps = sem("gate_sig"), sem("mix_steps")
    mx_hi, mx_lo = sem("mx_hi"), sem("mx_lo")
    sig_ready, act_hi, act_lo = sem("sig_ready"), sem("act_hi"), sem("act_lo")
    rt = Steps(sem("routing"), logits=1, turn=1, zero=1, lt=2, gt=1, eq=1, tie=1, rank=1, sum=1, sel=1,
               mx=1, sub=1, exp=1, tot=1, rtot=1, prob=1, chosen=1, two=1, rtwo=1, comb=1, back=1,
               backed=4, cum=1, place=1, one=1, pass1=1, pass2=1, pass3=1, last=1, ends=1, first=1,
               J0=1, J=1, shift=1, table=1, tables=4)
    ht_turned, ht_hi_ready, ht_lo_ready = sem("ht_turned"), sem("ht_hi_ready"), sem("ht_lo_ready")
    g_ready, gathered, weighed, cw_ready = (sem(n) for n in ("g_ready", "gathered", "weighed", "cw_ready"))
    hg_hi_ready, hg_lo_ready = sem("hg_hi_ready"), sem("hg_lo_ready")
    job_cols, placed, gt_ready = sem("job_cols"), sem("placed"), sem("gt_ready")
    m_sum, m_sig, m_gate, m_up, m_act = (sem(n) for n in ("m_sum", "m_sig", "m_gate", "m_up", "m_act"))
    table_loaded = sem("table_loaded")
    m_hi, m_lo = sem("m_hi"), sem("m_lo")
    yt_hi_ready, yt_lo_ready = sem("yt_hi_ready"), sem("yt_lo_ready")
    scattered, x_added = sem("scattered"), sem("x_added")
    gate_stored = [sem("gate_stored0"), sem("gate_stored1")]
    gate_in = [sem(f"gate_in{i}") for i in range(GATE_PLACES)]
    block = ctx.enter_context(nc.Block())

    def evac(o):
        return emptied[o % 2], o // 2 + 1

    def gate_slab(f):
        return 3 * f - 1 if f else 0

    def gate_back(l, k):
        at = N_GATES * l + k
        return at % GATE_PLACES, (gate_in[at % GATE_PLACES], 16 * (at // GATE_PLACES + 1))

    def gate_kept(l, k):
        return gate_stored[k % 2], 16 * (N_GATES // 2 * l + k // 2 + 1)

    def split_whole(n, j=0):
        return (lo_ready_gpsimd if rest_on_gpsimd(n) else lo_ready), rests(n, j)

    def out_ps(o):
        return ps[:, 2 * (o % 2):2 * (o % 2) + 2, 0:HALF]

    def gathered_ps(b):
        return ps[:, 2 * b:2 * b + 2, 0:2 * WIDE].rearrange("p b (a c) -> p b a c", a=2)[:, :, :, 0:CAP]

    def hg_part(b, lo):
        return hg[:, 4 * b:4 * b + 4, CAP * lo:CAP * (lo + 1)].rearrange("p (b a) c -> p b a c", a=2)

    def y_ps(ct):
        return ps[0:(P, REST)[ct], 4 + 2 * ct:6 + 2 * ct]

    def halves(ap):
        return ap.rearrange("p (a b) -> p a b", a=2)

    def mixers_done(l):
        return ((po.sem, po.after("y3", l)), (st_S, 16 * (l + 1)), (st_Ss, 32 * (l + 1)),
                (st_C, 16 * H * (l + 1)), (st_nm, 48 * (l + 1)), (st_Cs, 16 * H * (l + 1)),
                (st_ns, 16 * (l + 1)))

    @block.sync
    def _(sp):
        sp.dma_start(x[:], x_in).then_inc(loaded, 16)
        sp.dma_start(con[:], consts).then_inc(loaded, 16)
        sp.dma_start(vec[:], vectors).then_inc(loaded, 16)
        sp.dma_start(ifb[:], if_bias).then_inc(loaded, 16)
        for n in range(MOE0 + RAW):
            if n >= RAW:
                sp.wait_ge(*split_whole(slab_before(n)))
            sp.dma_start(raw[:, place(n)], slabs[n]).then_inc(arrived[place(n)], 16)
            l, i = divmod(n - 6 - Z_MO, LAYER1)
            if 0 <= i < N_GATES:
                sp.wait_ge(*evac(l * O_LAYER1 + Z_MO + i))
                sp.dma_start(gates_kept[l, i], sq[:, i % 2]).then_inc(gate_stored[i % 2], 16)
        sp.wait_ge(rt.sem, rt.after("tables"))
        passes_sp = sp.value_load(jt[:, NJ:NJ + 1], min_val=E, max_val=NJ - 2)
        with sp.Fori(0, passes_sp) as j:
            own = sp.value_load(jt[:, bass.ds(j, 1)], min_val=0, max_val=(E - 1) * S_JOB)
            after = sp.value_load(jt[:, bass.ds(j + 1, 1)], min_val=0, max_val=(E - 1) * S_JOB)
            for i in range(RAW, S_JOB + RAW):
                n = MOE0 + i
                first = own + n if i < S_JOB else after + (n - S_JOB)
                sp.wait_ge(*split_whole(slab_before(n), j))
                sp.dma_start(raw[:, place(n)],
                             slabs[bass.ds(first, 1)].rearrange("o p k c -> p (o k) c")).then_inc(
                                 arrived[place(n)], 16)
        sp.wait_ge(normed, 8 * 5)
        sp.dma_start(y_out, yfin[:]).then_inc(st_y, 16)
        sp.wait_ge(st_y, 16)
        sp.wait_ge(st_keep, 16)

    @block.gpsimd
    def _(pool):
        for l in range(DEPTH):
            if l > 0:
                pool.wait_ge(*evac(O_LAYER1 - 1))
                pool.wait_ge(*evac(O_LAYER1 - 2))
            else:
                pool.dma_start(pool_keep, pool_old).then_inc(st_keep, 16)
            pool.dma_start(m_s0[:], ml_m0[l]).then_inc(m0_in, 16)
            pool.dma_start(ggw[:], gate_w[l]).then_inc(ggw_in, 16)
            pool.wait_ge(gc.sem, gc.after("ns", TT * l + TT - 1))
            pool.dma_start(S_p[l], S[:]).then_inc(st_S, 16)
            for j in range(2):
                i = 2 * l + j
                if j == 0:
                    pool.wait_ge(st_S, 16 * (l + 1))
                else:
                    pool.wait_ge(st_Ss, 16 * i)
                pool.dma_start(Ss[:], gla_S0[l, j]).then_inc(S_in_s, 16)
                pool.wait_ge(dg.sem, dg.after("oc", i))
                pool.dma_start(S_s[l, j], Ss[:]).then_inc(st_Ss, 16)
            for h in range(H):
                i = H * l + h
                pool.wait_ge(ml.sem, ml.after("cst", i))
                pool.dma_start(C_p[l, h], C_t[:, h]).then_inc(st_C, 16)
            pool.dma_start(n_p[l], n_row[:]).then_inc(st_nm, 16)
            pool.dma_start(m_p[l], row_b[:, NP_TOK - 1:NP_TOK]).then_inc(st_nm, 16)
            pool.dma_start(m_s[l], m_new[:]).then_inc(st_nm, 16)
            pool.wait_ge(ml.sem, ml.after("h", H * l + H - 1))
            pool.wait_ge(st_C, 16 * H * (l + 1))
            pool.wait_ge(st_nm, 48 * (l + 1))
            pool.dma_start(n_s0[:], ml_n0[l]).then_inc(n0_in, 16)
            for h in range(H):
                i = H * l + h
                if h > 0:
                    pool.wait_ge(st_Cs, 16 * i)
                pool.dma_start(Cs[:], ml_C0[l, h]).then_inc(C_in, 16)
                pool.wait_ge(ds.sem, ds.after("h", i))
                pool.dma_start(C_s[l, h], Cs[:]).then_inc(st_Cs, 16)
            pool.dma_start(n_s[l], n_s0[:]).then_inc(st_ns, 16)
            pool.wait_ge(st_Cs, 16 * H * (l + 1))
            pool.wait_ge(st_ns, 16 * (l + 1))
            pool.dma_start(pw[:], pool_w[l]).then_inc(pool_loaded, 16)
            pool.dma_start(ext[:, :, :, 0:POOL_BUF], pool_in[l]).then_inc(pool_loaded, 16)
            pool.dma_start(pool_u[l], br[:, 8:12, NP_TOK - POOL_BUF:T]).then_inc(st_pu, 16)
            pool.wait_ge(st_pu, 16 * (l + 1))
            for s, n in mixers_done(l):
                pool.wait_ge(s, n)
            for k in range(N_GATES):
                if k >= GATE_PLACES:
                    before = k - GATE_PLACES
                    if before < 2 * H:
                        pool.wait_ge(gated, 2 * H * l + before + 1)
                    else:
                        pool.wait_ge(*evac(l * O_LAYER1 + branch_out(before)))
                pool.wait_ge(*gate_kept(l, k))
                at, back = gate_back(l, k)
                pool.dma_start(gs[:, at], gates_kept[l, k]).then_inc(back[0], 16)

        def rest(n, j=0):
            pool.wait_ge(hi_ready, j * S_JOB + (n + 1))
            nc.gpsimd.tensor_tensor(w_lo[:, n % SPL], raw[:, place(n)], w_hi[:, n % SPL].bitcast(F32),
                                    ALU.subtract).then_inc(lo_ready_gpsimd, 1)

        rest(MOE0 + 2)
        pool.wait_ge(rt.sem, rt.after("tables"))
        passes_pool = pool.value_load(jt[:, NJ:NJ + 1], min_val=E, max_val=NJ - 2)
        with pool.Fori(0, passes_pool) as j:
            for i in REST_ON_GPSIMD[1:] + [S_JOB + 2]:
                rest(MOE0 + i, j)

    @block.scalar
    def _(act):
        def split_hi(n, j=0):
            act.wait_ge(arrived[place(n)], arrivals(n, j))
            if n >= SPL:
                act.wait_ge(slab_done, j * S_JOB + (n - SPL + 1))
            nc.scalar.activation(w_hi[:, n % SPL], raw[:, place(n)], ACT.Copy).then_inc(hi_ready, 1)

        def out_done(n):
            act.wait_ge(slab_done, n + 1)

        def norm(r, hs, ready):
            if r > 0:
                act.wait_ge(h_lo_ready, 8 * hs)
            for kk in range(KT):
                i = 8 * r + kk
                for s, n in ready(kk):
                    act.wait_ge(s, n)
                if i >= 2:
                    act.wait_ge(squares_used, i - 1)
                nc.scalar.activation(sq[:, kk % 2], x[:, kk], ACT.Square).then_inc(squared, 1)
            act.wait_ge(squares_used, 8 * (r + 1))
            if r > 0:
                act.wait_ge(normed, 8 * r)
            nc.scalar.activation(halves(rs[:, 0]), ps[:, 4:6, 0:HALF], ACT.Ln, bias=eps,
                                 scale=1.0 / D).then_inc(rs_steps, 1)
            act.wait_ge(rs_steps, 2 * r + 1)
            nc.scalar.activation(rs[:, 0], rs[:, 0], ACT.Exp, scale=-0.5).then_inc(rs_steps, 1)
            if r < 4:
                for kk in range(KT):
                    act.wait_ge(normed, 8 * r + kk + 1)
                    nc.scalar.activation(h_hi[:, kk], sq[:, kk % 2], ACT.Copy).then_inc(h_hi_ready, 1)

        def inputs(l, nb, ob):
            for i in range(Z_MO):
                n, o = nb + i, ob + i
                split_hi(n + 2)
                if i == Z_SMALL:
                    out_done(n)
                    src = out_ps(o)
                    nc.scalar.activation(halves(row_i[:]), src[0:H], ACT.Identity,
                                         bias=ifb[:, l, 0:1]).then_inc(rows.sem, 1)
                    nc.scalar.activation(halves(row_f[:]), src[32:32 + H], ACT.Identity,
                                         bias=ifb[:, l, 1:2]).then_inc(rows.sem, 1)
                    nc.scalar.activation(halves(glr[:]), src[64:80], ACT.Copy).then_inc(emptied[o % 2], 1)
                    continue
                for first, buf, at in ((Z_GV, gv, 0), (Z_Q, q, 0), (Z_V, v, 0), (Z_PU, br, 8)):
                    if first <= i < first + 4:
                        out_done(n)
                        nc.scalar.activation(halves(buf[:, at + i - first]), out_ps(o),
                                             ACT.Copy).then_inc(emptied[o % 2], 1)

        def gla(l):
            act.wait_ge(g.sem, g.after("loga_pe", l))
            for j in range(2):
                nc.scalar.activation(halves(la[:, j]), ps[:, 4 + 2 * j:6 + 2 * j, 0:HALF], ACT.Identity,
                                     bias=vec[:, l, V_GB + j:V_GB + j + 1]).then_inc(g.sem, 1)
            fill(2)
            act.wait_ge(g.sem, g.after("abs", l))
            nc.scalar.activation(dec[:], dec[:], ACT.Exp, scale=-1.0).then_inc(g.sem, 1)
            act.wait_ge(g.sem, g.after("exp", l))
            nc.scalar.activation(dec[:], dec[:], ACT.Ln, bias=1.0).then_inc(g.sem, 1)
            fill(4)
            act.wait_ge(g.sem, g.after("clip", l))
            mid = dec[:, :, P // 2 - 1:NP_TOK:P]
            end = la[:, :, P - 1:NP_TOK:P]
            nc.scalar.activation(ge[:, 0], mid, ACT.Exp, scale=1.0 / 16).then_inc(g.sem, 1)
            nc.scalar.activation(ge[:, 1], end, ACT.Exp, scale=1.0 / 16).then_inc(g.sem, 1)
            nc.scalar.activation(ea[:], la[:, :, NP_TOK:T], ACT.Exp, scale=1.0 / 16).then_inc(g.sem, 1)
            act.wait_ge(g.sem, g.after("clip", l) + 3)
            nc.scalar.activation(dec[:, :, 0:NP_TOK], la[:, :, 0:NP_TOK], ACT.Exp,
                                 scale=1.0 / 16).then_inc(g.sem, 1)
            act.wait_ge(g.sem, g.after("clip", l) + 4)
            nc.scalar.activation(la[:, :, 0:NP_TOK], la[:, :, 0:NP_TOK], ACT.Exp,
                                 scale=-1.0 / 16).then_inc(g.sem, 1)
            fill(2)
            for tt in range(TT):
                act.wait_ge(g.sem, g.after("turn", l))
                nc.scalar.activation(gvt[:, tt], ps[:, 4 + tt], ACT.Copy).then_inc(g.sem, 1)
            fill(1)
            for tt in range(TT):
                act.wait_ge(g.sem, g.after("turnk", l))
                nc.scalar.activation(gkt[:, tt], ps[:, 4 + tt, 0:256], ACT.Copy).then_inc(g.sem, 1)
            fill(1)
            for tt in range(TT):
                rep = TT * l + tt
                fill(1)
                act.wait_ge(gc.sem, gc.after("o", rep))
                nc.scalar.activation(br[:, 4:8, token_tile(tt)],
                                     ps[:, 6, :].rearrange("p (h t) -> p h t", t=P),
                                     ACT.Copy).then_inc(gc.sem, 1)
                fill(1)
            for j in range(2):
                fill(4)

        def mlstm(l):
            act.wait_ge(rows.sem, rows.after("abs", l))
            nc.scalar.activation(row_M[:], row_M[:], ACT.Exp, scale=-1.0).then_inc(rows.sem, 1)
            act.wait_ge(rows.sem, rows.after("exp", l))
            nc.scalar.activation(row_M[:], row_M[:], ACT.Ln, bias=1.0).then_inc(rows.sem, 1)
            fill(2)
            act.wait_ge(rows.sem, rows.after("m", l))
            nc.scalar.activation(row_f[:, 0:NP_TOK], row_b[:, 0:NP_TOK], ACT.Exp,
                                 scale=-1.0).then_inc(rows.sem, 1)
            act.wait_ge(rows.sem, rows.after("sdiff", l))
            nc.scalar.activation(w3[:], w3[:], ACT.Exp).then_inc(rows.sem, 1)
            fill(2)
            for h in range(H):
                rep = H * l + h
                at = lambda name: act.wait_ge(ml.sem, ml.after(name, rep))
                at("turn")
                nc.scalar.activation(kt[:], ps[:, 4].rearrange("p (a d) -> p a d", d=P),
                                     ACT.Copy).then_inc(ml.sem, 1)
                fill(2)
                at("dm")
                for tt in range(TT):
                    nc.scalar.activation(wgt[:, tt, token_tile(tt)], dm[:, tt], ACT.Exp,
                                         bias=acol[:, tt, h:h + 1]).then_inc(ml.sem, 1)
                for tt in range(TT - 1):
                    rest = slice((tt + 1) * P, NP_TOK)
                    nc.scalar.activation(wgt[:, tt, rest], ps[:, 6, rest], ACT.Exp,
                                         bias=acol[:, tt, h:h + 1]).then_inc(ml.sem, 1)
                fill(2)
                at("out")
                nc.scalar.activation(C_t[:, h], ps[:, 5, 0:P], ACT.Copy).then_inc(ml.sem, 1)
                nc.scalar.activation(n_row[:, h * P:(h + 1) * P], ps[0:1, 5, P:2 * P],
                                     ACT.Copy).then_inc(ml.sem, 1)
                at("cst")
                nc.scalar.activation(den[:], ps[:, 7], ACT.Abs).then_inc(ml.sem, 1)
                fill(2)
            for h in range(H):
                fill(4)

        def pool_mix(l):
            for gi in range(4):
                fill(1)
                act.wait_ge(po.sem, po.after(f"mm{gi}", l))
                act.wait_ge(st_pu, 16 * (l + 1))
                nc.scalar.activation(halves(br[:, 8 + gi]), ps[:, 4:6, 0:HALF], ACT.Copy,
                                     scale=vec[:, l, V_PS + gi:V_PS + gi + 1]).then_inc(po.sem, 1)

        def head_norm(l):
            act.wait_ge(h_lo_ready, 8 * (3 * l + 1))
            act.wait_ge(ds.sem, ds.after("h", H * l + H - 1))
            for t in range(9):
                if t < 8:
                    i = 8 * l + t
                    if t >= 2:
                        act.wait_ge(hn_ssq, i - 1)
                    nc.scalar.activation(sq[:, t % 2], br[:, t], ACT.Square).then_inc(hn_sq, 1)
                if t > 0:
                    b, i = (t - 1) % 2, 8 * l + t - 1
                    act.wait_ge(hn_ssq, i + 1)
                    if t > 2:
                        act.wait_ge(hn_n, i - 1)
                    nc.scalar.activation(halves(rs[:, b]), ps[:, 4 + 2 * b:6 + 2 * b, 0:HALF], ACT.Ln,
                                         bias=eps, scale=1.0 / P).then_inc(hn_rs, 1)
                    act.wait_ge(hn_rs, 2 * i + 1)
                    nc.scalar.activation(rs[:, b], rs[:, b], ACT.Exp, scale=-0.5).then_inc(hn_rs, 1)

        def fill(k):
            for _ in range(k):
                i, half = divmod(fills[0], 2)
                fills[0] += 1
                if half or i >= N_GATES:
                    continue
                split_hi(fills[1] * LAYER1 + Z_MO + i + 2)
                if i > 0:
                    gate_out(fills[1], i - 1)

        def gate_out(l, i):
            n, o = l * LAYER1 + Z_MO + i, l * O_LAYER1 + Z_MO + i
            out_done(n)
            if i >= 2:
                act.wait_ge(*gate_kept(l, i - 2))
            to = emptied[o % 2] if not H <= i < 2 * H else gate_sig
            nc.scalar.activation(halves(sq[:, i % 2]), out_ps(o), ACT.Sigmoid).then_inc(to, 1)

        def filled(l):
            fill(2 * N_GATES - fills[0])
            gate_out(l, N_GATES - 1)
            for i in range(2):
                act.wait_ge(*gate_kept(l, N_GATES - 2 + i))

        def gates(l):
            for s, n in mixers_done(l):
                act.wait_ge(s, n)
            for j in range(12):
                if j < 8:
                    act.wait_ge(gated, 8 * l + j + 1)
                nc.scalar.activation(br_hi[:, j], br[:, j], ACT.Copy).then_inc(br_hi_ready, 1)

        def merge(l, nb, ob):
            for s in range(KT // 2 * 3):
                split_hi(nb + S_BRANCH + s + 2)
            act.wait_ge(slab_done, nb + S_BRANCH)
            act.wait_ge(mix_steps, 16 * (l + 1))
            for kk in range(KT):
                nc.scalar.activation(h_hi[:, kk], mixed[:, kk], ACT.Copy).then_inc(h_hi_ready, 1)
            for m in range(KT):
                split_hi(nb + S_OUT + m + 2)

        def feed_forward(nf, of):
            for f in range(F_TILES + 1):
                if f < F_TILES:
                    split_hi(nf + 2 * f + 2)
                    out_done(nf + 2 * f)
                    if f > 0:
                        act.wait_ge(*evac(of + 2 * f - 2))
                    nc.scalar.activation(halves(sig[:]), out_ps(of + 2 * f),
                                         ACT.Sigmoid).then_inc(sig_ready, 1)
                    split_hi(nf + 2 * f + 3)
                if f > 0:
                    act.wait_ge(*evac(of + 2 * f - 1))
                    nc.scalar.activation(a_hi[:, f - 1], af[:, (f - 1) % 2], ACT.Copy).then_inc(act_hi, 1)
            for s in range(F_TILES):
                split_hi(nf + S_DOWN + s + 2)


        def gathered_hi(p):
            act.wait_ge(gathered, p + 1)
            for b in range(2):
                nc.scalar.activation(hg_part(b, 0), gathered_ps(b), ACT.Copy).then_inc(hg_hi_ready, 1)

        def routing():
            split_hi(ROUTER + 2)
            act.wait_ge(rt.sem, rt.after("sub"))
            nc.scalar.activation(comb[:], comb[:], ACT.Exp).then_inc(rt.sem, 1)
            for i in range(5):
                rws = P if i < 4 else NS_TOK
                act.wait_ge(ht_turned, 2 * i + 1)
                nc.scalar.activation(ht_hi[0:rws, i].rearrange("p (a d) -> p a d", a=2), ps[0:rws, 4:6],
                                     ACT.Copy).then_inc(ht_hi_ready, 1)

        def expert_pass(j):
            s0, f0 = MOE0, j * FE_TILES
            nc.scalar.activation(msig[0:1, 0:1], eps[0:1], ACT.Sigmoid).then_inc(table_loaded, 1)
            for f in range(FE_TILES):
                if f > 0:
                    split_hi(s0 + gate_slab(f) + 2, j)
                act.wait_ge(m_sum, f0 + (f + 1))
                if f == 0:
                    act.wait_ge(table_loaded, j + 1)
                nc.scalar.activation(msig[:], gsum[:], ACT.Sigmoid).then_inc(m_sig, 1)
                split_hi(s0 + gate_slab(f) + 3, j)
                if f > 0:
                    split_hi(s0 + down_slab(f - 1) + 2, j)
                act.wait_ge(m_act, f0 + (f + 1))
                nc.scalar.activation(ma_hi[:, f % 2], ma[:, f % 2], ACT.Copy).then_inc(m_hi, 1)
            split_hi(s0 + down_slab(FE_TILES - 1) + 2, j)
            gathered_hi(j + 1)
            split_hi(s0 + 2, j + 1)
            act.wait_ge(slab_done, j * S_JOB + (s0 + S_JOB))
            act.wait_ge(cw_ready, j * 2 + 2)
            for ct in range(2):
                rws = slice(0, (P, REST)[ct])
                nc.scalar.activation(yt_hi[rws, ct].rearrange("p (a d) -> p a d", a=2), y_ps(ct),
                                     ACT.Copy, scale=cw[rws, ct:ct + 1]).then_inc(yt_hi_ready, 1)

        fills = [0, 0]
        act.wait_ge(loaded, 64)
        split_hi(0)
        split_hi(1)
        for l in range(DEPTH):
            nb, ob = l * LAYER1, l * O_LAYER1
            norm(2 * l, 3 * l, lambda kk: [evac(O_LAYER1 - KT + kk)] if l else [])
            inputs(l, nb, ob)
            fills[:] = 0, l
            gla(l)
            mlstm(l)
            pool_mix(l)
            filled(l)
            head_norm(l)
            gates(l)
            merge(l, nb, ob)
            norm(2 * l + 1, 3 * l + 2, lambda kk: [evac(ob + O_OUT + kk)])
            if l == 0:
                feed_forward(S_MIX, O_MIX)
            else:
                routing()
                act.wait_ge(rt.sem, rt.after("tables"))
                passes_act = act.value_load(jt[:, NJ:NJ + 1], min_val=E, max_val=NJ - 2)
                split_hi(MOE0 + 2)
                gathered_hi(0)
                with act.Fori(0, passes_act) as j:
                    expert_pass(j)
        norm(4, 6, lambda kk: [] if kk else [(x_added, passes_act * KT + KT)])

    @block.vector
    def _(dve):
        tt_op = nc.vector.tensor_tensor
        ts_op = nc.vector.tensor_scalar
        stt_op = nc.vector.scalar_tensor_tensor

        def split_lo(n, j=0):
            if rest_on_gpsimd(n):
                return
            dve.wait_ge(hi_ready, j * S_JOB + (n + 1))
            tt_op(w_lo[:, n % SPL], raw[:, place(n)], w_hi[:, n % SPL].bitcast(F32),
                  ALU.subtract).then_inc(lo_ready, 1)

        def out_done(n):
            dve.wait_ge(slab_done, n + 1)

        def norm(r, hs):
            gain = vec[:, 1, V_FN:V_FN + KT] if r == 4 else vec[:, r // 2, (V_N1, V_N2)[r % 2]:][:, 0:KT]
            dve.wait_ge(rs_steps, 2 * r + 2)
            for kk in range(KT + 1):
                if kk < KT:
                    if r < 4 and kk >= 2:
                        dve.wait_ge(h_lo_ready, 8 * hs + kk - 1)
                    to = yfin[:, kk] if r == 4 else sq[:, kk % 2]
                    stt_op(to, x[:, kk], gain[:, kk:kk + 1], rs[:, 0], ALU.mult,
                           ALU.mult).then_inc(normed, 1)
                if r < 4 and kk > 0:
                    dve.wait_ge(h_hi_ready, 8 * hs + kk)
                    tt_op(h_lo[:, kk - 1], sq[:, (kk - 1) % 2], h_hi[:, kk - 1].bitcast(F32),
                          ALU.subtract).then_inc(h_lo_ready, 1)

        def inputs(l, nb, ob):
            for i in range(Z_MO):
                n, o = nb + i, ob + i
                split_lo(n + 2)
                for first, last, buf, scale in ((Z_GK, Z_GQ, gk, 1.0), (Z_GQ, Z_GV, gq, DK ** -0.5),
                                                (Z_K, Z_V, k, P ** -0.5)):
                    if first <= i < last:
                        out_done(n)
                        ts_op(halves(buf[:, i - first]), out_ps(o), scale, None,
                              ALU.mult).then_inc(emptied[o % 2], 1)

        def gla(l):
            at = lambda name, more=0: dve.wait_ge(g.sem, g.after(name, l) + more)
            inc = lambda ins: ins.then_inc(g.sem, 1)
            at("y")
            inc(stt_op(dec[:], la[:], -1.0, la[:], ALU.mult, ALU.max))
            inc(ts_op(la[:], la[:], 0.0, None, ALU.min))
            fill(2)
            at("ln")
            inc(tt_op(la[:], la[:], dec[:], ALU.subtract))
            at("loga")
            for j in range(2):
                for tt in range(TT):
                    inc(nc.vector.tensor_tensor_scan(dec[:, j, token_tile(tt)], la[:, j, token_tile(tt)],
                                                     la[:, j, token_tile(tt)], 0.0, ALU.add, ALU.bypass))
            fill(2)
            at("scan")
            for j in range(2):
                for tt in range(TT):
                    c = tt * P + P // 2 - 1
                    inc(ts_op(la[:, j, token_tile(tt)], dec[:, j, token_tile(tt)], dec[:, j, c:c + 1],
                              -1280.0, ALU.subtract, ALU.max))
            at("diff")
            inc(ts_op(la[:, :, 0:NP_TOK], la[:, :, 0:NP_TOK], 1280.0, None, ALU.min))
            fill(2)
            at("e")
            for h in range(H):
                inc(stt_op(qz[:, h, 0:NP_TOK], gq[:, h // 2, 0:NP_TOK], head_half[:, h % 2:h % 2 + 1],
                           dec[:, h // 2, 0:NP_TOK], ALU.mult, ALU.mult))
                inc(ts_op(qz[:, h, NP_TOK:T], gq[:, h // 2, NP_TOK:T], head_half[:, h % 2:h % 2 + 1],
                          None, ALU.mult))
            inc(tt_op(gk[:, :, 0:NP_TOK], gk[:, :, 0:NP_TOK], la[:, :, 0:NP_TOK], ALU.mult))
            inc(tt_op(ge[:, 2], ge[:, 0], ge[:, 1], ALU.mult))
            inc(nc.vector.memset(S[:], 0.0))
            fill(4)
            at("copyk")
            for tt in range(TT):
                rep = TT * l + tt
                at = lambda name: dve.wait_ge(gc.sem, gc.after(name, rep))
                inc = lambda ins: ins.then_inc(gc.sem, 1)
                at("att")
                inc(tt_op(att[:], ps[:, 4].rearrange("p (h t) -> p h t", t=P),
                          keep_mask.unsqueeze(1).to_broadcast([P, H, P]), ALU.mult))
                for j in range(2):
                    inc(ts_op(S_in[:, j], S[:, j], ge[:, 0, j, tt:tt + 1], None, ALU.mult))
                fill(1)
                at("ocopy")
                for j in range(2):
                    for half in range(2):
                        rws = slice(64 * half, 64 * half + 64)
                        c = 256 * j + P * half
                        inc(ts_op(Ut[rws, j], ps[rws, 5, c:c + P], ge[rws, 1, j, tt:tt + 1], None,
                                  ALU.mult))
                at("su")
                for j in range(2):
                    inc(stt_op(S[:, j], S[:, j], ge[:, 2, j, tt:tt + 1], Ut[:, j], ALU.mult, ALU.add))
                fill(1)

        def gla_decode(l):
            for j in range(2):
                rep = 2 * l + j
                at = lambda name: dve.wait_ge(dg.sem, dg.after(name, rep))
                inc = lambda ins: ins.then_inc(dg.sem, 1)
                at("turn")
                inc(nc.vector.tensor_copy(gt8[:], ps[0:NS_TOK, 4, 0:3 * P].rearrange(
                    "b (a d) -> b a d", d=P)))
                at("copy")
                for half in range(2):
                    spread(inc, gdiag[:, half], gt8[:, 1 + half])
                fill(2)
                at("outer")
                dve.wait_ge(S_in_s, 16 * (rep + 1))
                inc(tt_op(Ss[:], Ss[:], ea[:, j].unsqueeze(2).to_broadcast([P, NS_TOK, P]), ALU.mult))
                at("decay")
                inc(tt_op(Ss[:].rearrange("p (a b) d -> p a (b d)", a=2), Ss[:].rearrange("p (a b) d -> p a (b d)", a=2),
                          ps[:, 4:6], ALU.add))
                fill(2)
                at("o")
                inc(nc.vector.tensor_copy(br[:, 4 + 2 * j:6 + 2 * j, NP_TOK:T],
                                          ps[:, 6, 0:16].rearrange("p (b h) -> p h b", h=2)))

        def spread(inc, to, rows8):
            inc(tt_op(to, rows8.unsqueeze(1).to_broadcast([NS_TOK, NS_TOK, P]),
                      ident[0:NS_TOK, 0:NS_TOK].unsqueeze(2).to_broadcast([NS_TOK, NS_TOK, P]),
                      ALU.mult))

        def mlstm_rows(l):
            at = lambda name: dve.wait_ge(rows.sem, rows.after(name, l))
            inc = lambda ins: ins.then_inc(rows.sem, 1)
            pr, sa = slice(0, NP_TOK), slice(NP_TOK, T)
            at("gates")
            inc(stt_op(row_M[:], row_f[:], -1.0, row_f[:], ALU.mult, ALU.max))
            inc(ts_op(row_f[:], row_f[:], 0.0, None, ALU.min))
            at("ln")
            inc(tt_op(row_f[:], row_f[:], row_M[:], ALU.subtract))
            at("logf")
            inc(nc.vector.tensor_tensor_scan(row_b[:, pr], row_f[:, pr], row_f[:, pr], 0.0, ALU.add,
                                             ALU.bypass))
            at("b")
            inc(tt_op(row_i[:, pr], row_i[:, pr], row_b[:, pr], ALU.subtract))
            at("a")
            inc(nc.vector.tensor_tensor_scan(row_M[:, pr], row_i[:, pr], row_i[:, pr], 0.0, ALU.max,
                                             ALU.bypass))
            at("M")
            inc(tt_op(row_b[:, pr], row_b[:, pr], row_M[:, pr], ALU.add))
            fill(2)
            dve.wait_ge(rows.sem, rows.after("M", l) + 1)
            inc(ts_op(row_M[:, pr], row_M[:, pr], -1.0, None, ALU.mult))
            at("enm")
            dve.wait_ge(m0_in, 16 * (l + 1))
            inc(tt_op(m_inter[:], row_f[:, sa], m_s0[:], ALU.add))
            at("inter")
            inc(tt_op(m_new[:], m_inter[:], row_i[:, sa], ALU.max))
            at("smax")
            inc(tt_op(w3[:, 0], row_i[:, sa], m_new[:], ALU.subtract))
            inc(tt_op(w3[:, 1], m_inter[:], m_new[:], ALU.subtract))
            inc(ts_op(w3[:, 2], m_new[:], -1.0, None, ALU.mult))
            fill(2)
            at("turn")
            inc(nc.vector.tensor_copy(acol[:], ps[:, 4, 0:16].rearrange("p (a h) -> p a h", h=H)))
            inc(nc.vector.tensor_copy(w3t[:], ps[0:NS_TOK, 4, 32:44].rearrange("p (a h) -> p a h", h=H)))
            inc(nc.vector.tensor_copy(w3b[:], ps[:, 5, 0:96].rearrange("p (h w) -> p h w", h=H)))
            at("turned")

        def mlstm(l):
            for h in range(H):
                rep = H * l + h
                at = lambda name: dve.wait_ge(ml.sem, ml.after(name, rep))
                inc = lambda ins: ins.then_inc(ml.sem, 1)
                at("turn")
                inc(nc.vector.tensor_copy(vt[:], ps[:, 5].rearrange("p (a d) -> p a d", d=P)))
                at("copies")
                inc(tt_op(dm[:], ps[:, 6].rearrange("p (a d) -> p a d", d=P),
                          neg_mask.unsqueeze(1).to_broadcast([P, TT, P]), ALU.add))
                fill(2)
                at("exps")
                inc(nc.vector.tensor_copy(wcol[:], wgt[:, :, NP_TOK - 1]))
                at("sc01")
                for tt in range(2):
                    inc(tt_op(wgt[:, tt, tt * P:], wgt[:, tt, tt * P:], ps[:, 4 + tt, 0:NP_TOK - tt * P],
                              ALU.mult))
                fill(1)
                at("sc23")
                for tt in range(2, 4):
                    at_ps = ps[:, 4, 256 * (tt - 2):256 * (tt - 2) + NP_TOK - tt * P]
                    inc(tt_op(wgt[:, tt, tt * P:], wgt[:, tt, tt * P:], at_ps, ALU.mult))
                at("scol")
                dve.wait_ge(ml.sem, ml.after("p23", rep))
                inc(tt_op(vw[:], vt[:], wcol[:].unsqueeze(2).to_broadcast([P, TT, P]), ALU.mult))
                fill(1)
                at("absd")
                inc(tt_op(den[:], den[:], ps[:, 4], ALU.max))
                at("maxd")
                inc(nc.vector.reciprocal(den2[:], den[:]))
                at("rec")
                inc(tt_op(br[:, h, 0:NP_TOK], ps[:, 6], den2[:], ALU.mult))
                fill(2)
                at("h")

        def mlstm_decode(l):
            dve.wait_ge(st_C, 16 * H * (l + 1))
            dve.wait_ge(st_nm, 48 * (l + 1))
            for h in range(H):
                rep = H * l + h
                at = lambda name: dve.wait_ge(ds.sem, ds.after(name, rep))
                inc = lambda ins: ins.then_inc(ds.sem, 1)
                if h > 0:
                    dve.wait_ge(ds.sem, ds.after("h", rep - 1))
                inc(tt_op(vs8[:], v[:, h, NP_TOK:T], w3b[:, h, 0:NS_TOK], ALU.mult))
                at("turn")
                inc(nc.vector.tensor_copy(tok8[:], ps[0:NS_TOK, 4, 0:3 * P].rearrange(
                    "b (a d) -> b a d", d=P)))
                at("copy")
                for a in range(2):
                    spread(inc, diag[:, a], tok8[:, 1 + a])
                fill(2)
                at("outer")
                dve.wait_ge(C_in, 16 * (rep + 1))
                inc(tt_op(Cs[:], Cs[:], w3b[:, h, NS_TOK:2 * NS_TOK].unsqueeze(2).to_broadcast(
                    [P, NS_TOK, P]), ALU.mult))
                at("carry")
                Cs2 = Cs[:].rearrange("p (a b) d -> p a (b d)", a=2)
                inc(tt_op(Cs2, Cs2, ps[:, 4:6], ALU.add))
                at("add")
                inc(tt_op(Cq[:].rearrange("p (a b) d -> p a (b d)", a=2), Cs2, ps[:, 6:8], ALU.mult))
                fill(2)
                at("cq")
                inc(nc.vector.tensor_reduce(num8[:], Cq[:], AX.X, ALU.add))
                at("num")
                inc(ts_op(n_tmp[:], tok8[:, 1], w3t[:, 0, h:h + 1], None, ALU.mult))
                at("nt")
                dve.wait_ge(n0_in, 16 * (l + 1))
                inc(stt_op(n_s0[:, h], n_s0[:, h], w3t[:, 1, h:h + 1], n_tmp[:], ALU.mult, ALU.add))
                at("n")
                inc(tt_op(nq[:], n_s0[:, h], tok8[:, 2], ALU.mult))
                at("nq")
                inc(nc.vector.tensor_reduce(dcol[:, 0:1], nq[:], AX.X, ALU.add))
                at("den")
                inc(stt_op(dcol[:, 1:2], dcol[:, 0:1], -1.0, dcol[:, 0:1], ALU.mult, ALU.max))
                at("dabs")
                inc(ts_op(dcol[:, 1:2], dcol[:, 1:2], w3t[:, 2, h:h + 1], None, ALU.max))
                at("dmax")
                inc(nc.vector.reciprocal(dcol[:, 2:3], dcol[:, 1:2]))
                at("drec")
                inc(ts_op(rdiag[:], ident[0:NS_TOK, 0:NS_TOK], dcol[:, 2:3], None, ALU.mult))
                at("rb")
                inc(tt_op(br[:, h, NP_TOK:T], num8[:], ps[:, 4, 0:NS_TOK], ALU.mult))

        def pool_mix(l):
            dve.wait_ge(pool_loaded, 32 * (l + 1))
            count = [po.total * l]

            def step(ins):
                ins.then_inc(po.sem, 1)
                count[0] += 1
                dve.wait_ge(po.sem, count[0])

            step(nc.vector.tensor_copy(ext[:, :, :, POOL_BUF], br[:, 8:12, NP_TOK:T]))
            for gi, w in enumerate(WINDOWS):
                src, shift = br[:, 8 + gi, 0:NP_TOK], 1
                for level in range(gi + 1):
                    to = pa[:, level % 2]
                    step(tt_op(to[:, shift:], src[:, shift:], src[:, 0:NP_TOK - shift], ALU.add))
                    step(nc.vector.tensor_copy(to[:, 0:shift], src[:, 0:shift]))
                    src, shift = to, 2 * shift
                step(ts_op(pd[:, 0:NP_TOK], src, 1.0 / w, None, ALU.mult))
                fill(1)
                step(tt_op(pd[:, 0:16], src[:, 0:16], inv_count[:, gi], ALU.mult))
                step(tt_op(pd[:, 0:NP_TOK], pd[:, 0:NP_TOK], br[:, 8 + gi, 0:NP_TOK], ALU.subtract))
                step(nc.vector.tensor_reduce(pred[:], ext[:, gi, :, 16 - w:16], AX.X, ALU.add))
                step(stt_op(pd[:, NP_TOK:T], pred[:], 1.0 / w, br[:, 8 + gi, NP_TOK:T], ALU.mult,
                            ALU.subtract))
                count[0] += 2
                dve.wait_ge(po.sem, po.after(f"y{gi}", l))

        def head_norm(l):
            for t in range(8):
                i = 8 * l + t
                dve.wait_ge(hn_rs, 2 * i + 2)
                gain = vec[:, l, V_ML + t:V_ML + t + 1]
                stt_op(br[:, t], br[:, t], gain, rs[:, t % 2], ALU.mult, ALU.mult).then_inc(hn_n, 1)

        def fill(k):
            for _ in range(k):
                i, half = divmod(fills[0], 2)
                fills[0] += 1
                if half or i >= N_GATES:
                    continue
                split_lo(fills[1] * LAYER1 + Z_MO + i + 2)
                if H < i <= 2 * H:
                    o = fills[1] * O_LAYER1 + Z_MO + i - 1
                    dve.wait_ge(gate_sig, H * fills[1] + i - H)
                    tt_op(halves(sq[:, (i - 1) % 2]), halves(sq[:, (i - 1) % 2]), out_ps(o),
                          ALU.mult).then_inc(emptied[o % 2], 1)

        def gates(l):
            for s, n in mixers_done(l):
                dve.wait_ge(s, n)
            for k in range(2 * H):
                at, back = gate_back(l, k)
                dve.wait_ge(*back)
                dve.wait_ge(hn_n, 2 * H * l + k + 1)
                tt_op(br[:, k], br[:, k], gs[:, at], ALU.mult).then_inc(gated, 1)
                if k > 0:
                    rest(l, k - 1)
            for t in range(2 * H - 1, 12):
                rest(l, t)

        def rest(l, t):
            dve.wait_ge(br_hi_ready, 12 * l + t + 1)
            tt_op(br_lo[:, t], br[:, t], br_hi[:, t].bitcast(F32), ALU.subtract).then_inc(br_lo_ready, 1)

        def merge(l, nb, ob):
            steps = 16 * l
            for mp in range(KT // 2):
                for s, outs in enumerate((((0, 0), (1, 0)), ((0, 1), (1, 1)), ((2, 0), (2, 1)))):
                    n = nb + S_BRANCH + 3 * mp + s
                    split_lo(n + 2)
                    out_done(n)
                    for i, (branch, m) in enumerate(outs):
                        k = 2 * H + 6 * mp + 2 * s + i
                        o = ob + branch_out(k)
                        at, back = gate_back(l, k)
                        dve.wait_ge(*back)
                        if branch > 0 and steps > 0:
                            dve.wait_ge(mix_steps, steps)
                        to = mixed[:, 2 * mp + m] if branch == 0 else gt[:]
                        tt_op(halves(to), out_ps(o), halves(gs[:, at]), ALU.mult).then_inc(
                            emptied[o % 2], 1)
                        if branch > 0:
                            dve.wait_ge(*evac(o))
                            dve.wait_ge(*evac(ob + branch_out(2 * H + 6 * mp + 2 * m)))
                            tt_op(mixed[:, 2 * mp + m], mixed[:, 2 * mp + m], gt[:], ALU.add).then_inc(
                                mix_steps, 1)
                            steps += 1
            for kk in range(KT):
                dve.wait_ge(h_hi_ready, 8 * (3 * l + 1) + kk + 1)
                tt_op(h_lo[:, kk], mixed[:, kk], h_hi[:, kk].bitcast(F32), ALU.subtract).then_inc(
                    h_lo_ready, 1)
            for m in range(KT):
                n, o = nb + S_OUT + m, ob + O_OUT + m
                split_lo(n + 2)
                out_done(n)
                tt_op(halves(x[:, m]), halves(x[:, m]), out_ps(o), ALU.add).then_inc(emptied[o % 2], 1)

        def feed_forward(nf, of):
            for f in range(F_TILES + 1):
                if f < F_TILES:
                    split_lo(nf + 2 * f + 2)
                    o = of + 2 * f
                    split_lo(nf + 2 * f + 3)
                    dve.wait_ge(sig_ready, f + 1)
                    if f >= 2:
                        dve.wait_ge(act_lo, f - 1)
                    tt_op(halves(af[:, f % 2]), out_ps(o), halves(sig[:]), ALU.mult).then_inc(
                        emptied[o % 2], 1)
                    dve.wait_ge(*evac(o))
                    out_done(nf + 2 * f + 1)
                    tt_op(halves(af[:, f % 2]), halves(af[:, f % 2]), out_ps(o + 1), ALU.mult).then_inc(
                        emptied[(o + 1) % 2], 1)
                if f > 0:
                    dve.wait_ge(act_hi, f)
                    tt_op(a_lo[:, f - 1], af[:, (f - 1) % 2], a_hi[:, f - 1].bitcast(F32),
                          ALU.subtract).then_inc(act_lo, 1)
            m = 0
            for s in range(F_TILES):
                split_lo(nf + S_DOWN + s + 2)
                while m < KT and (F_TILES * (m + 1) - 1) // 8 == s:
                    o = of + O_DOWN + m
                    out_done(nf + S_DOWN + s)
                    tt_op(halves(x[:, m]), halves(x[:, m]), out_ps(o), ALU.add).then_inc(
                        emptied[o % 2], 1)
                    m += 1


        def prepare(p):
            nc.vector.tensor_copy(pcol[:], postj[:, bass.ds(p, 1)].rearrange("p o t -> p (o t)")).then_inc(g_ready, 1)
            nc.vector.tensor_copy(ccol[:], combj[:, bass.ds(p, 1)].rearrange("p o t -> p (o t)")).then_inc(g_ready, 1)
            dve.wait_ge(g_ready, p * 7 + 2)
            for tt in range(5):
                rws = P if tt < 4 else NS_TOK
                ts_op(G[0:rws, tt], iota[0:rws], pcol[0:rws, tt:tt + 1], None, ALU.is_equal).then_inc(
                    g_ready, 1)

        def gathered_lo(p):
            for b in range(2):
                dve.wait_ge(hg_hi_ready, p * 2 + (b + 1))
                tt_op(hg_part(b, 1), gathered_ps(b), hg_part(b, 0).bitcast(F32),
                      ALU.subtract).then_inc(hg_lo_ready, 1)

        def routing():
            split_lo(ROUTER + 2)
            at = lambda name, more=0: dve.wait_ge(rt.sem, rt.after(name) + more)
            inc = lambda ins: ins.then_inc(rt.sem, 1)
            out_done(ROUTER)
            inc(nc.vector.tensor_copy(halves(lrow[:]), out_ps(O_ROUTER)[0:E]))
            at("turn")
            inc(nc.vector.memset(lt[:], 0.0))
            at("zero")
            inc(nc.vector.tensor_copy(lt[:, 0:4], ps[:, 4, 0:4 * E].rearrange("p (t e) -> p t e", e=E)))
            inc(nc.vector.tensor_copy(lt[0:NS_TOK, 4], ps[0:NS_TOK, 4, 4 * E:5 * E]))
            at("lt")
            other = lt[:].unsqueeze(2).to_broadcast([P, 5, E, E])
            own = lt[:].unsqueeze(3).to_broadcast([P, 5, E, E])
            rk4 = [rk[:, a].rearrange("p (t e) j -> p t e j", e=E) for a in range(2)]
            inc(tt_op(rk4[0], other, own, ALU.is_gt))
            inc(tt_op(rk4[1], other, own, ALU.is_equal))
            at("eq")
            inc(tt_op(rk4[1], rk4[1], tie.unsqueeze(1).to_broadcast([P, 5, E, E]), ALU.mult))
            at("tie")
            inc(tt_op(rk[:, 0], rk[:, 0], rk[:, 1], ALU.add))
            at("rank")
            inc(nc.vector.tensor_reduce(sel_t[:].rearrange("p t e -> p (t e)"), rk[:, 0], AX.X, ALU.add))
            at("sum")
            inc(ts_op(sel_t[:], sel_t[:], 2.0, None, ALU.is_lt))
            inc(nc.vector.tensor_reduce(red[:], lt[:], AX.X, ALU.max))
            at("mx")
            wide = red[:].unsqueeze(2).to_broadcast([P, 5, E])
            inc(tt_op(comb[:], lt[:], wide, ALU.subtract))
            at("exp")
            inc(nc.vector.tensor_reduce(red[:], comb[:], AX.X, ALU.add))
            at("tot")
            inc(nc.vector.reciprocal(red[:], red[:]))
            at("rtot")
            inc(tt_op(comb[:], comb[:], wide, ALU.mult))
            at("prob")
            inc(tt_op(comb[:], comb[:], sel_t[:], ALU.mult))
            at("chosen")
            inc(nc.vector.tensor_reduce(red[:], comb[:], AX.X, ALU.add))
            at("two")
            inc(nc.vector.reciprocal(red[:], red[:]))
            at("rtwo")
            inc(tt_op(comb[:], comb[:], wide, ALU.mult))
            at("back")
            inc(nc.vector.tensor_copy(lrow[:, 0:NP_TOK], ps[0:E, 4]))
            inc(nc.vector.tensor_copy(crow[:, 0:NP_TOK], ps[0:E, 5]))
            inc(nc.vector.tensor_copy(lrow[:, NP_TOK:T], ps[0:E, 6, 0:NS_TOK]))
            inc(nc.vector.tensor_copy(crow[:, NP_TOK:T], ps[0:E, 6, NS_TOK:2 * NS_TOK]))
            at("backed")
            inc(nc.vector.tensor_tensor_scan(cum[:], lrow[:], lrow[:], 0.0, ALU.add, ALU.bypass))
            at("cum")
            inc(tt_op(lrow[:], lrow[:], cum[:], ALU.mult))
            at("place")
            inc(ts_op(lrow[:], lrow[:], -1.0, None, ALU.add))
            n = cum[:, T - 1:T]
            inc(ts_op(passes[:, 0:1], n, float(CAP), 1.0, ALU.is_gt, ALU.add))
            at("pass1")
            inc(stt_op(passes[:, 0:1], n, float(2 * CAP), passes[:, 0:1], ALU.is_gt, ALU.add))
            at("pass2")
            inc(stt_op(passes[:, 0:1], n, float(3 * CAP), passes[:, 0:1], ALU.is_gt, ALU.add))
            at("last")
            inc(nc.vector.tensor_copy(passes[:, 1:2], ps[0:E, 7, 0:1]))
            at("ends")
            inc(tt_op(passes[:, 2:3], passes[:, 1:2], passes[:, 0:1], ALU.subtract))
            at("first")
            inc(ts_op(J[:], iota[0:E, 0:NJ], passes[:, 2:3], None, ALU.is_ge))
            at("J0")
            inc(stt_op(J[:], iota[0:E, 0:NJ], passes[:, 1:2], J[:], ALU.is_lt, ALU.mult))
            at("J")
            inc(stt_op(lrow[:], passes[:, 2:3].to_broadcast([E, T]), float(CAP), lrow[:], ALU.mult,
                       ALU.add))
            at("table")
            inc(stt_op(postj[:].rearrange("p j t -> p t j"), iota[:, 0:NJ].unsqueeze(1).to_broadcast([P, 5, NJ]),
                       -float(CAP), ps[:, 4, 0:5 * NJ].rearrange("p (t j) -> p t j", j=NJ), ALU.mult,
                       ALU.add))
            inc(nc.vector.tensor_copy(combj[:].rearrange("p j t -> p t j"),
                                      ps[:, 5, 0:5 * NJ].rearrange("p (t j) -> p t j", j=NJ)))
            inc(ts_op(jt[:, 0:NJ], ps[0:1, 6, 0:NJ], float(S_JOB), None, ALU.mult))
            inc(nc.vector.tensor_copy(jt[:, NJ:NJ + 1], ps[0:1, 6, NJ:NJ + 1]))
            at("tables")
            for i in range(5):
                rws = P if i < 4 else NS_TOK
                dve.wait_ge(ht_turned, 2 * i + 2)
                nc.vector.tensor_copy(ht_lo[0:rws, i].rearrange("p (a d) -> p a d", a=2),
                                      ps[0:rws, 6:8]).then_inc(ht_lo_ready, 1)
            for buf in (yt_hi, yt_lo):
                nc.vector.memset(buf[:].bitcast(F32), 0.0).then_inc(yt_lo_ready, 1)
            for ct in range(2):
                nc.vector.memset(GT[:, ct].bitcast(F32), 0.0).then_inc(gt_ready, 1)

        def addends(b):
            return ps[:, b, 0:2 * CAP].rearrange("p (a c) -> p c a", a=2)

        def scattered_in(j):
            for m in range(KT):
                dve.wait_ge(scattered, j * KT + (m + 1))
                b = 4 + 2 * (m % 2)
                tt_op(halves(x[:, m]), halves(x[:, m]), ps[:, b:b + 2, 0:HALF], ALU.add).then_inc(
                    x_added, 1)

        def expert_pass(j):
            s0, f0 = MOE0, j * FE_TILES
            nc.vector.tensor_copy(Jb[:], J[:, bass.ds(j, 1)].to_broadcast([E, P])).then_inc(job_cols, 1)
            nc.vector.tensor_copy(places[:], part_index[:, bass.ds(j, 1)].rearrange(
                "p o t -> p (o t)")).then_inc(job_cols, 1)
            for f in range(FE_TILES):
                if f > 0:
                    split_lo(s0 + gate_slab(f) + 2, j)
                dve.wait_ge(slab_done, j * S_JOB + (s0 + gate_slab(f) + 1))
                b = 2 * (f % 2)
                nc.vector.tensor_reduce(gsum[:], addends(b), AX.X, ALU.add).then_inc(m_sum, 1)
                dve.wait_ge(m_sig, f0 + (f + 1))
                tt_op(ma[:, f % 2], gsum[:], msig[:], ALU.mult).then_inc(m_gate, 1)
                if f != 1:
                    split_lo(s0 + gate_slab(f) + 3, j)
                if f == 1:
                    scattered_in(j)
                    dve.wait_ge(placed, j + 1)
                    dve.wait_ge(job_cols, j * 2 + 2)
                    for ct in range(2):
                        ts_op(halves(GT[:, ct]), ps[:, 4:6, 0:HALF], places[:, ct:ct + 1], None,
                              ALU.is_equal).then_inc(gt_ready, 1)
                    dve.wait_ge(weighed, j + 1)
                    for ct in range(2):
                        rws = slice(0, (P, REST)[ct])
                        nc.vector.tensor_copy(cw[rws, ct:ct + 1], ps[rws, 6, 400 + ct:401 + ct]).then_inc(
                            cw_ready, 1)
                    split_lo(s0 + gate_slab(f) + 3, j)
                dve.wait_ge(slab_done, j * S_JOB + (s0 + gate_slab(f) + 2))
                nc.vector.tensor_reduce(usum[:], addends(b + 1), AX.X, ALU.add).then_inc(m_up, 1)
                dve.wait_ge(m_up, f0 + (f + 1))
                tt_op(ma[:, f % 2], ma[:, f % 2], usum[:], ALU.mult).then_inc(m_act, 1)
                if f > 0:
                    split_lo(s0 + down_slab(f - 1) + 2, j)
                lo_of_act(f, f0)
                if f == 5:
                    prepare(j + 1)
            split_lo(s0 + down_slab(FE_TILES - 1) + 2, j)
            gathered_lo(j + 1)
            split_lo(s0 + 2, j + 1)
            for ct in range(2):
                rws = slice(0, (P, REST)[ct])
                dve.wait_ge(yt_hi_ready, j * 2 + (ct + 1))
                wide = yt_hi[rws, ct].bitcast(F32).rearrange("p (a d) -> p a d", a=2)
                stt_op(yt_lo[rws, ct].rearrange("p (a d) -> p a d", a=2), y_ps(ct),
                       cw[rws, ct:ct + 1], wide, ALU.mult, ALU.subtract).then_inc(yt_lo_ready, 1)
            dve.wait_ge(yt_lo_ready, j * 2 + 4)

        def lo_of_act(f, f0):
            dve.wait_ge(m_hi, f0 + (f + 1))
            tt_op(ma_lo[:, f % 2], ma[:, f % 2], ma_hi[:, f % 2].bitcast(F32), ALU.subtract).then_inc(
                m_lo, 1)

        fills = [0, 0]
        dve.wait_ge(loaded, 64)
        split_lo(0)
        split_lo(1)
        for l in range(DEPTH):
            nb, ob = l * LAYER1, l * O_LAYER1
            norm(2 * l, 3 * l)
            inputs(l, nb, ob)
            fills[:] = 0, l
            gla(l)
            gla_decode(l)
            mlstm_rows(l)
            mlstm(l)
            mlstm_decode(l)
            pool_mix(l)
            fill(2 * N_GATES - fills[0])
            head_norm(l)
            gates(l)
            merge(l, nb, ob)
            norm(2 * l + 1, 3 * l + 2)
            if l == 0:
                feed_forward(S_MIX, O_MIX)
            else:
                routing()
                passes_dve = dve.value_load(jt[:, NJ:NJ + 1], min_val=E, max_val=NJ - 2)
                prepare(0)
                split_lo(MOE0 + 2)
                gathered_lo(0)
                with dve.Fori(0, passes_dve) as j:
                    expert_pass(j)
                scattered_in(passes_dve)
        norm(4, 6)

    @block.tensor
    def _(pe):
        mm = nc.tensor.matmul

        def exact(out, a, b, start=True, stop=True):
            return mm(out, a, b, start=start, stop=stop, skip_group_check=True)

        def tile_product(out, slot, tile, in_hi, in_lo, kk, first, last):
            for wgt_part, in_part, ends in ((w_hi, in_hi, 0), (w_hi, in_lo, 0), (w_lo, in_hi, 1)):
                for hf in range(2):
                    ins = mm(out[:, hf], wgt_part[:, slot, tile], in_part[:, kk, HALF * hf:HALF * (hf + 1)],
                             start=first and not ends and in_part is in_hi, stop=last and bool(ends))
            return ins

        def slab_ready(n):
            pe.wait_ge(*split_whole(n))

        def out_free(o):
            if o >= 2:
                pe.wait_ge(*evac(o - 2))

        def slab_to_out(n, o, in_hi, in_lo):
            slab_ready(n)
            out_free(o)
            for kk in range(KT):
                ins = tile_product(out_ps(o), n % SPL, kk, in_hi, in_lo, kk, kk == 0, kk == KT - 1)
            ins.then_inc(slab_done, 1)

        def mean_squares(r, bank_free):
            for s, n in bank_free:
                pe.wait_ge(s, n)
            for kk in range(KT):
                pe.wait_ge(squared, 8 * r + kk + 1)
                for hf in range(2):
                    ins = exact(ps[:, 4 + hf, 0:HALF], ones, sq[:, kk % 2, HALF * hf:HALF * (hf + 1)],
                                kk == 0, kk == KT - 1)
                ins.then_inc(squares_used, 1)

        def normed_in(hs):
            pe.wait_ge(h_lo_ready, 8 * (hs + 1))

        def gla(l, ob):
            pe.wait_ge(ggw_in, 16 * (l + 1))
            pe.wait_ge(*evac(ob + Z_SMALL))
            pe.wait_ge(*evac(ob + Z_MO - 1))
            pe.wait_ge(*evac(ob + Z_MO - 2))
            for j in range(2):
                for hf in range(2):
                    ins = exact(ps[:, 4 + 2 * j + hf, 0:HALF], ggw[:, j * P:(j + 1) * P],
                                glr[:, HALF * hf:HALF * (hf + 1)])
            ins.then_inc(g.sem, 1)
            fill(8)
            pe.wait_ge(g.sem, g.after("qk", l))
            for tt in range(TT):
                for h in range(H):
                    ins = nc.tensor.transpose(ps[:, 4 + tt, h * P:(h + 1) * P], gv[:, h, token_tile(tt)],
                                              ident)
                ins.then_inc(g.sem, 1)
            fill(1)
            pe.wait_ge(g.sem, g.after("copy", l))
            for tt in range(TT):
                for j in range(2):
                    ins = nc.tensor.transpose(ps[:, 4 + tt, j * P:(j + 1) * P], gk[:, j, token_tile(tt)],
                                              ident)
                ins.then_inc(g.sem, 1)
            fill(1)
            pe.wait_ge(g.sem, g.after("copyk", l))
            for tt in range(TT):
                rep = TT * l + tt
                if tt > 0:
                    pe.wait_ge(gc.sem, gc.after("ns", rep - 1))
                for h in range(H):
                    exact(ps[:, 4, h * P:(h + 1) * P], gk[:, h // 2, token_tile(tt)],
                          qz[:, h, token_tile(tt)])
                for j in range(2):
                    ins = exact(ps[:, 5, 256 * j:256 * (j + 1)], gkt[:, tt, j * P:(j + 1) * P],
                                gvt[:, tt, 256 * j:256 * (j + 1)])
                ins.then_inc(gc.sem, 1)
                fill(1)
                pe.wait_ge(gc.sem, gc.after("sin", rep))
                for h in range(H):
                    out = ps[:, 6, h * P:(h + 1) * P]
                    exact(out, gvt[:, tt, h * P:(h + 1) * P], att[:, h], True, False)
                    ins = exact(out, S_in[:, h // 2], qz[:, h, token_tile(tt)], False, True)
                ins.then_inc(gc.sem, 1)
                fill(1)

        def gla_decode(l):
            pe.wait_ge(gc.sem, gc.after("ns", TT * l + TT - 1))
            for j in range(2):
                rep = 2 * l + j
                if j > 0:
                    pe.wait_ge(dg.sem, dg.after("oc", rep - 1))
                sa = slice(NP_TOK, T)
                nc.tensor.transpose(ps[0:NS_TOK, 4, 0:P], gk[:, j, sa], ident)
                nc.tensor.transpose(ps[0:NS_TOK, 4, P:2 * P], gv[:, 2 * j, sa], ident)
                nc.tensor.transpose(ps[0:NS_TOK, 4, 2 * P:3 * P], gv[:, 2 * j + 1, sa],
                                    ident).then_inc(dg.sem, 1)
                fill(2)
                pe.wait_ge(dg.sem, dg.after("diag", rep))
                for half in range(2):
                    for c in range(2):
                        ins = exact(ps[64 * half:64 * half + 64, 4 + c],
                                    gt8[:, 0, 64 * half:64 * half + 64],
                                    gdiag[:, half, 4 * c:4 * c + 4])
                ins.then_inc(dg.sem, 1)
                fill(2)
                pe.wait_ge(dg.sem, dg.after("add", rep))
                for b in range(NS_TOK):
                    ins = exact(ps[:, 6, 2 * b:2 * b + 2], Ss[:, b], qz[:, 2 * j:2 * j + 2, NP_TOK + b])
                ins.then_inc(dg.sem, 1)

        def mlstm(l):
            fill(4)
            pe.wait_ge(rows.sem, rows.after("sexp", l))
            pe.wait_ge(dg.sem, dg.after("oc", 2 * l + 1))
            for tt in range(TT):
                nc.tensor.transpose(ps[:, 4, H * tt:H * tt + H], row_i[:, token_tile(tt)],
                                    ident[0:H, 0:H])
            for a in range(3):
                nc.tensor.transpose(ps[0:NS_TOK, 4, 32 + H * a:32 + H * a + H], w3[:, a],
                                    ident[0:H, 0:H])
            for h in range(H):
                ins = exact(ps[:, 5, 24 * h:24 * h + 24], select[:, h], w3[:].rearrange("h a b -> h (a b)"))
            ins.then_inc(rows.sem, 1)
            pe.wait_ge(rows.sem, rows.after("turned", l))
            pe.wait_ge(st_Ss, 32 * (l + 1))
            for h in range(H):
                rep = H * l + h
                at = lambda name: pe.wait_ge(ml.sem, ml.after(name, rep))
                if h > 0:
                    pe.wait_ge(ml.sem, ml.after("h", rep - 1))
                for tt in range(TT):
                    nc.tensor.transpose(ps[:, 4, tt * P:(tt + 1) * P], k[:, h, token_tile(tt)], ident)
                    nc.tensor.transpose(ps[:, 5, tt * P:(tt + 1) * P], v[:, h, token_tile(tt)], ident)
                exact(ps[:, 6], select[:, h], row_M[:, 0:NP_TOK]).then_inc(ml.sem, 1)
                fill(2)
                at("scol")
                for tt in range(2):
                    ins = exact(ps[:, 4 + tt, 0:NP_TOK - tt * P], k[:, h, token_tile(tt)],
                                q[:, h, tt * P:NP_TOK])
                ins.then_inc(ml.sem, 1)
                fill(1)
                at("p01")
                for tt in range(2, 4):
                    c = 256 * (tt - 2)
                    ins = exact(ps[:, 4, c:c + NP_TOK - tt * P], k[:, h, token_tile(tt)],
                                q[:, h, tt * P:NP_TOK])
                ins.then_inc(ml.sem, 1)
                fill(1)
                at("vw")
                for tt in range(TT):
                    exact(ps[:, 6, tt * P:], vt[:, tt], wgt[:, tt, tt * P:], tt == 0, tt == TT - 1)
                for tt in range(TT):
                    exact(ps[:, 7, tt * P:], ones, wgt[:, tt, tt * P:], tt == 0, tt == TT - 1)
                exact(ps[:, 4], select[:, h], row_f[:, 0:NP_TOK])
                for tt in range(TT):
                    exact(ps[:, 5, 0:P], vw[:, tt], kt[:, tt], tt == 0, tt == TT - 1)
                for tt in range(TT):
                    ins = exact(ps[0:1, 5, P:2 * P], wcol[:, tt:tt + 1], kt[:, tt], tt == 0, tt == TT - 1)
                ins.then_inc(ml.sem, 1)
                fill(2)

        def mlstm_decode(l):
            for h in range(H):
                rep = H * l + h
                at = lambda name: pe.wait_ge(ds.sem, ds.after(name, rep))
                at("vs")
                nc.tensor.transpose(ps[0:NS_TOK, 4, 0:P], vs8[:], ident)
                nc.tensor.transpose(ps[0:NS_TOK, 4, P:2 * P], k[:, h, NP_TOK:T], ident)
                nc.tensor.transpose(ps[0:NS_TOK, 4, 2 * P:3 * P], q[:, h, NP_TOK:T],
                                    ident).then_inc(ds.sem, 1)
                fill(2)
                at("diag")
                for c in range(2):
                    exact(ps[:, 4 + c], tok8[:, 0], diag[:, 0, 4 * c:4 * c + 4])
                for c in range(2):
                    ins = exact(ps[:, 6 + c], ones[0:NS_TOK], diag[:, 1, 4 * c:4 * c + 4])
                ins.then_inc(ds.sem, 1)
                fill(2)
                at("rd")
                exact(ps[:, 4, 0:NS_TOK], ones[0:NS_TOK], rdiag[:]).then_inc(ds.sem, 1)

        def pool_mix(l):
            for gi in range(4):
                fill(1)
                pe.wait_ge(po.sem, po.after(f"w{gi}", l))
                for hf in range(2):
                    ins = exact(ps[:, 4 + hf, 0:HALF], pw[:, gi], pd[:, HALF * hf:HALF * (hf + 1)])
                ins.then_inc(po.sem, 1)

        def head_norm(l):
            pe.wait_ge(po.sem, po.after("y3", l))
            for t in range(8):
                i = 8 * l + t
                pe.wait_ge(hn_sq, i + 1)
                if t >= 2:
                    pe.wait_ge(hn_rs, 2 * i - 3)
                for hf in range(2):
                    ins = exact(ps[:, 4 + 2 * (t % 2) + hf, 0:HALF], ones,
                                sq[:, t % 2, HALF * hf:HALF * (hf + 1)])
                ins.then_inc(hn_ssq, 1)

        def fill(k):
            for _ in range(k):
                i, half = divmod(fills[0], 2)
                fills[0] += 1
                if i >= N_GATES:
                    continue
                n, o = fills[1] * LAYER1 + Z_MO + i, fills[1] * O_LAYER1 + Z_MO + i
                if not half:
                    slab_ready(n)
                    out_free(o)
                for kk in range(4 * half, 4 * half + 4):
                    ins = tile_product(out_ps(o), n % SPL, kk, h_hi, h_lo, kk, kk == 0, kk == KT - 1)
                if half:
                    ins.then_inc(slab_done, 1)

        def merge(l, nb, ob):
            for mp in range(KT // 2):
                for s, outs in enumerate(((0, 1), (0, 1), (2, 2))):
                    n, o = nb + S_BRANCH + 3 * mp + s, ob + O_BRANCH + 6 * mp + 2 * s
                    slab_ready(n)
                    pe.wait_ge(br_lo_ready, 12 * (l + 1))
                    for i, branch in enumerate(outs):
                        out_free(o + i)
                        for kk in range(4):
                            ins = tile_product(out_ps(o + i), n % SPL, 4 * i + kk, br_hi, br_lo,
                                               4 * branch + kk, kk == 0, kk == 3)
                    ins.then_inc(slab_done, 1)
            normed_in(3 * l + 1)
            for m in range(KT):
                slab_to_out(nb + S_OUT + m, ob + O_OUT + m, h_hi, h_lo)

        def feed_forward(nf, of):
            for i in range(2 * F_TILES):
                slab_to_out(nf + i, of + i, h_hi, h_lo)
            pe.wait_ge(act_lo, F_TILES)
            for s in range(F_TILES):
                n = nf + S_DOWN + s
                slab_ready(n)
                for tile in range(8):
                    m, f = divmod(8 * s + tile, F_TILES)
                    o = of + O_DOWN + m
                    if f == 0:
                        out_free(o)
                    ins = tile_product(out_ps(o), n % SPL, tile, a_hi, a_lo, f, f == 0, f == F_TILES - 1)
                ins.then_inc(slab_done, 1)


        def gather(p):
            pe.wait_ge(g_ready, p * 7 + 7)
            for m in range(KT):
                out = ps[:, m // 2, WIDE * (m % 2):WIDE * (m % 2 + 1)]
                for tt in range(5):
                    rws = P if tt < 4 else NS_TOK
                    for part in (ht_hi, ht_lo):
                        ins = mm(out, part[0:rws, tt, m * P:(m + 1) * P], G[0:rws, tt],
                                 start=m % 2 == 0 and tt == 0 and part is ht_hi, stop=True,
                                 skip_group_check=True)
            ins.then_inc(gathered, 1)

        def weigh(j):
            pe.wait_ge(job_cols, j * 2 + 2)
            pe.wait_ge(x_added, j * KT + (KT - 1))
            for hf in range(2):
                ins = exact(ps[:, 4 + hf, 0:HALF], Jb[:], lrow[:, HALF * hf:HALF * (hf + 1)])
            ins.then_inc(placed, 1)
            pe.wait_ge(x_added, j * KT + KT)
            for ct in range(2):
                c = slice(P * ct, min(CAP, P * (ct + 1)))
                for tt in range(5):
                    rws = P if tt < 4 else NS_TOK
                    ins = exact(ps[0:c.stop - c.start, 6, 400 + ct:401 + ct], G[0:rws, tt, c].bitcast(F32),
                                ccol[0:rws, tt:tt + 1], tt == 0, tt == 4)
            ins.then_inc(weighed, 1)

        def routing():
            slab_to_out(ROUTER, O_ROUTER, h_hi, h_lo)
            at = lambda name: pe.wait_ge(rt.sem, rt.after(name))
            at("logits")
            for i in range(5):
                rws = P if i < 4 else NS_TOK
                ins = nc.tensor.transpose(ps[0:rws, 4, E * i:E * (i + 1)], lrow[:, P * i:P * i + rws],
                                          ident[0:E, 0:E])
            ins.then_inc(rt.sem, 1)
            at("comb")
            for i in range(4):
                nc.tensor.transpose(ps[0:E, 4, P * i:P * (i + 1)], sel_t[:, i], ident)
                nc.tensor.transpose(ps[0:E, 5, P * i:P * (i + 1)], comb[:, i], ident)
            nc.tensor.transpose(ps[0:E, 6, 0:NS_TOK], sel_t[0:NS_TOK, 4], ident[0:NS_TOK, 0:NS_TOK])
            nc.tensor.transpose(ps[0:E, 6, NS_TOK:2 * NS_TOK], comb[0:NS_TOK, 4],
                                ident[0:NS_TOK, 0:NS_TOK]).then_inc(rt.sem, 1)
            at("pass3")
            exact(ps[0:E, 7, 0:1], keep_mask[0:E, 0:E], passes[:, 0:1]).then_inc(rt.sem, 1)
            at("shift")
            for i in range(5):
                rws = P if i < 4 else NS_TOK
                exact(ps[0:rws, 4, NJ * i:NJ * (i + 1)], lrow[:, P * i:P * i + rws], J[:])
                exact(ps[0:rws, 5, NJ * i:NJ * (i + 1)], crow[:, P * i:P * i + rws], J[:])
            exact(ps[0:1, 6, 0:NJ], part_index[0:E, 0, 0:1], J[:])
            exact(ps[0:1, 6, NJ:NJ + 1], ones[0:E, 0:1], passes[:, 0:1]).then_inc(rt.sem, 1)
            at("tables")
            for i in range(5):
                rws = P if i < 4 else NS_TOK
                if i > 0:
                    pe.wait_ge(ht_hi_ready, i)
                    pe.wait_ge(ht_lo_ready, i)
                for b, part in ((4, h_hi), (6, h_lo)):
                    for kk in range(KT):
                        ins = nc.tensor.transpose(
                            ps[0:rws, b + kk // 4, P * (kk % 4):P * (kk % 4 + 1)],
                            part[:, kk, P * i:P * i + rws].bitcast(F32), ident)
                    ins.then_inc(ht_turned, 1)
            pe.wait_ge(ht_hi_ready, 5)
            pe.wait_ge(ht_lo_ready, 5)

        def slab_ready_of(j, i):
            pe.wait_ge(*split_whole(MOE0 + i, j))

        def scatter(j):
            pe.wait_ge(yt_lo_ready, j * 2 + 2)
            pe.wait_ge(gt_ready, j * 2 + 2)
            for m in range(KT):
                if m >= 2:
                    pe.wait_ge(x_added, j * KT + (m - 1))
                for i, (ct, part) in enumerate(((0, yt_hi), (0, yt_lo), (1, yt_hi), (1, yt_lo))):
                    rws = slice(0, (P, REST)[ct])
                    for hf in range(2):
                        ins = mm(ps[:, 4 + 2 * (m % 2) + hf, 0:HALF], part[rws, ct, m * P:(m + 1) * P],
                                 GT[rws, ct, HALF * hf:HALF * (hf + 1)], start=i == 0, stop=i == 3)
                ins.then_inc(scattered, 1)

        def expert_pass(j):
            s0, f0 = MOE0, j * FE_TILES

            def gate_or_up(f, i):
                s = gate_slab(f) + i
                slab_ready_of(j, s)
                out = ps[:, 2 * (f % 2) + i]
                for kk in range(KT):
                    mm(out[:, 0:2 * CAP], w_hi[:, (s0 + s) % SPL, kk], hg[:, kk], start=kk == 0,
                       stop=False, skip_group_check=True)
                    ins = mm(out[:, 0:WIDE], w_lo[:, (s0 + s) % SPL, kk], hg[:, kk, 0:WIDE],
                             start=False, stop=kk == KT - 1, skip_group_check=True)
                ins.then_inc(slab_done, 1)

            def down(f):
                s = down_slab(f)
                slab_ready_of(j, s)
                pe.wait_ge(m_lo, f0 + (f + 1))
                for ct in range(2):
                    c = slice(P * ct, min(CAP, P * (ct + 1)))
                    for a, (t, w) in enumerate(((ma_hi, w_hi), (ma_hi, w_lo), (ma_lo, w_hi))):
                        for hf in range(2):
                            ins = mm(y_ps(ct)[:, hf], t[:, f % 2, c],
                                     w[:, (s0 + s) % SPL, 4 * hf:4 * hf + 4],
                                     start=f == 0 and a == 0, stop=f == FE_TILES - 1 and a == 2)
                ins.then_inc(slab_done, 1)

            pe.wait_ge(hg_lo_ready, j * 2 + 2)
            for f in range(FE_TILES):
                if f >= 2:
                    pe.wait_ge(m_act, f0 + (f - 1))
                gate_or_up(f, 0)
                if f == 1:
                    scatter(j)
                    weigh(j)
                gate_or_up(f, 1)
                if f == 1:
                    pe.wait_ge(gt_ready, j * 2 + 4)
                    pe.wait_ge(cw_ready, j * 2 + 2)
                if f > 0:
                    down(f - 1)
            pe.wait_ge(m_act, f0 + FE_TILES)
            gather(j + 1)
            down(FE_TILES - 1)

        fills = [0, 0]
        pe.wait_ge(loaded, 64)
        for l in range(DEPTH):
            nb, ob = l * LAYER1, l * O_LAYER1
            mean_squares(2 * l, [])
            normed_in(3 * l)
            for i in range(Z_MO):
                slab_to_out(nb + i, ob + i, h_hi, h_lo)
            fills[:] = 0, l
            gla(l, ob)
            gla_decode(l)
            mlstm(l)
            mlstm_decode(l)
            pool_mix(l)
            fill(2 * N_GATES - fills[0])
            head_norm(l)
            merge(l, nb, ob)
            mean_squares(2 * l + 1, [])
            normed_in(3 * l + 2)
            if l == 0:
                feed_forward(S_MIX, O_MIX)
            else:
                routing()
                passes_pe = pe.value_load(jt[:, NJ:NJ + 1], min_val=E, max_val=NJ - 2)
                gather(0)
                with pe.Fori(0, passes_pe) as j:
                    expert_pass(j)
                scatter(passes_pe)
        mean_squares(4, [(x_added, passes_pe * KT + KT)])

    ctx.close()


def _tiles(w):
    kk, m = w.shape
    return w.reshape(kk // P, P, m // P, P).transpose(2, 1, 0, 3)


def _columns(w, groups):
    return [w[:, c:c + P].reshape(-1, P, P).transpose(1, 0, 2) for c in groups]


def _slabs(a):
    out = []
    widths = (512, 512, 512, 4, 4, 512, 256, 256, 512, 16, 512, 512, 3072)
    mq, mk, mv, mi, mf, mo, gq, gk, gv, glr, go, pu, gates = np.cumsum((0,) + widths[:-1]).tolist()
    for l in range(DEPTH):
        w = a["w_in"][l]
        small = np.zeros((D, P), w.dtype)
        small[:, 0:4], small[:, 32:36], small[:, 64:80] = (
            w[:, mi:mi + 4], w[:, mf:mf + 4], w[:, glr:glr + 16])
        out += _columns(small, (0,))
        for start, tiles in ((gk, 2), (gq, 2), (gv, 4), (mq, 4), (mk, 4), (mv, 4), (pu, 4), (mo, 4), (go, 4)):
            out += _columns(w, range(start, start + tiles * P, P))
        for m in range(0, D, 2 * P):
            out += _columns(w, (gates + c + D * n for n, c in (
                (0, m), (1, m), (0, m + P), (1, m + P), (2, m), (2, m + P))))
        wb = a["w_branch"][l]
        for m in range(0, D, 2 * P):
            half = {(n, c): _columns(wb[n], (c,))[0] for n in range(3) for c in (m, m + P)}
            for c in (m, m + P):
                out.append(np.concatenate((half[0, c], half[1, c]), 1))
            out.append(np.concatenate((half[2, m], half[2, m + P]), 1))
        out += list(_tiles(a["w_out"][l]))
        if l == 0:
            up, gate = _tiles(a["ffn_wu"][0]), _tiles(a["ffn_wg"][0])
            for f in range(F_TILES):
                out += [gate[f], up[f]]
            down = _tiles(a["ffn_wd"][0]).transpose(0, 2, 1, 3).reshape(-1, 8, P, P)
            out += list(down.transpose(0, 2, 1, 3))
        else:
            router = np.zeros((D, P), w.dtype)
            router[:, 0:E] = a["router_w"][0]
            out += _columns(router, (0,))
            for e in range(E):
                up, gate = _tiles(a["moe_wu"][0, e]), _tiles(a["moe_wg"][0, e])
                down = a["moe_wd"][0, e].reshape(FE_TILES, P, KT, P)
                for f in range(FE_TILES):
                    out += [gate[f], up[f]] + [down[f - 1]] * (f > 0)
                out.append(down[FE_TILES - 1])
    assert len(out) == N_SLABS
    return np.stack(out)


def _constants():
    con = np.zeros((P, N_CONST), np.float32)
    con[:, C_ID:C_ID + P] = np.eye(P)
    con[:, C_ONE:C_ONE + P] = 1
    causal = np.arange(P)[:, None] <= np.arange(P)[None, :]
    con[:, C_NEG:C_NEG + P] = np.where(causal, 0, MASKED)
    con[:, C_KEEP:C_KEEP + P] = causal
    for r in range(H):
        con[r, C_SEL + r * P:C_SEL + (r + 1) * P] = 1
    for gi, w in enumerate(WINDOWS):
        con[:, C_INV + 16 * gi:C_INV + 16 * gi + 16] = 1 / np.minimum(np.arange(16) + 1, w)
    con[:, C_IOTA:C_IOTA + WIDE] = np.arange(WIDE)
    con[:, C_PART:C_PART + 2 * NJ] = (np.arange(P)[:, None, None] + CAP * np.arange(NJ)[:, None] +
                                      P * np.arange(2)).reshape(P, 2 * NJ)
    con[:, C_TIE:C_TIE + 64] = (np.arange(8)[None, :] < np.arange(8)[:, None]).reshape(1, 64)
    con[:, C_EPS] = EPS
    con[:64, C_HM], con[64:, C_HM + 1] = 1, 1
    return con


def _vector(v):
    return v.reshape(-1, P).T


def kernel(**inputs):
    import concourse.bacc as bacc
    from concourse.bass_utils import run_bass_kernel_spmd

    a = {name: np.asarray(value) for name, value in inputs.items()}
    tokens = np.concatenate((a["x_prompt"].reshape(NP_TOK, D), a["x_sample"].reshape(NS_TOK, D)))
    vectors = np.stack([np.concatenate([_vector(a[n][l]) for n in (
        "norm1_g", "norm2_g", "mlstm_norm_g", "gla_norm_g", "gla_gate_b", "pool_scale")] +
        [_vector(a["final_norm_g"])], 1) for l in range(DEPTH)], 1)
    arrays = {
        "slabs": _slabs(a),
        "x_in": tokens.reshape(T, KT, P).transpose(2, 1, 0),
        "vectors": vectors,
        "if_bias": a["mlstm_if_bias"].transpose(2, 0, 1),
        "gate_w": a["gla_gate_w"],
        "pool_w": a["pool_w"].transpose(0, 2, 1, 3),
        "consts": _constants(),
        "ml_m0": a["state_mlstm_m"].transpose(0, 2, 1),
        "ml_n0": a["state_mlstm_n"],
        "ml_C0": a["state_mlstm_C"].transpose(0, 2, 3, 1, 4),
        "gla_S0": a["state_gla_S"].reshape(DEPTH, NS_TOK, 2, P, P).transpose(0, 2, 3, 1, 4),
        "pool_in": a["state_pool_buf"].reshape(DEPTH, NS_TOK, POOL_BUF, 4, P).transpose(0, 4, 3, 1, 2),
        "pool_old": a["state_pool_buf"][:, :, 1:],
    }
    outs = {
        "y_out": (P, KT, T), "C_p": (DEPTH, H, P, P), "C_s": (DEPTH, H, P, NS_TOK, P),
        "n_p": (DEPTH, 1, H * P), "n_s": (DEPTH, NS_TOK, H, P), "m_p": (DEPTH, H, 1),
        "m_s": (DEPTH, H, NS_TOK), "S_p": (DEPTH, P, 2, P), "S_s": (DEPTH, 2, P, NS_TOK, P),
        "pool_u": (DEPTH, P, 4, POOL_BUF + NS_TOK), "pool_keep": (DEPTH, NS_TOK, POOL_BUF - 1, 512),
    }
    nc = bacc.Bacc("TRN2", target_bir_lowering=False, num_devices=1)
    args = []
    for name in arrays:
        arrays[name] = np.ascontiguousarray(arrays[name])
        args.append(nc.dram_tensor(name, arrays[name].shape, F32, kind="ExternalInput").ap())
    for name, shape in outs.items():
        args.append(nc.dram_tensor(name, shape, F32, kind="ExternalOutput").ap())
    args.append(nc.dram_tensor("gates_kept", (DEPTH, N_GATES, P, T), F32).ap())
    decoder(nc, *args)
    got = run_bass_kernel_spmd(nc, [arrays], core_ids=[0]).results[0]

    y = got["y_out"].transpose(2, 1, 0).reshape(T, D)
    u = got["pool_u"].transpose(0, 3, 2, 1).reshape(DEPTH, POOL_BUF + NS_TOK, 512)
    return (
        y[:NP_TOK].reshape(1, NP_TOK, D), y[NP_TOK:].reshape(NS_TOK, 1, D),
        got["C_p"].reshape(DEPTH, 1, H, P, P), got["C_s"].transpose(0, 3, 1, 2, 4),
        got["n_p"].reshape(DEPTH, 1, H, P), got["n_s"].reshape(DEPTH, NS_TOK, H, P),
        got["m_p"].reshape(DEPTH, 1, H), got["m_s"].transpose(0, 2, 1),
        got["S_p"].transpose(0, 2, 1, 3).reshape(DEPTH, 1, H, DK, P),
        got["S_s"].transpose(0, 3, 1, 2, 4).reshape(DEPTH, NS_TOK, H, DK, P),
        u[:, None, :POOL_BUF], np.concatenate((got["pool_keep"], u[:, POOL_BUF:][:, :, None]), 2),
    )
```

```python
from contextlib import ExitStack

import numpy as np

import concourse.bass as bass
from concourse import mybir

F32 = mybir.dt.float32
F32R = mybir.dt.float32r
ALU = mybir.AluOpType
ACT = mybir.ActivationFunctionType
AX = mybir.AxisListType

P = 128
DEPTH = 2
D = 1024
KT = D // P
NP_TOK, NS_TOK = 512, 8
T = NP_TOK + NS_TOK
HALF = T // 2
TT = NP_TOK // P
H = 4
DK = 64
WINDOWS = (2, 4, 8, 16)
POOL_BUF = 15
F_TILES = 2816 // P
E = 8
NJ = 16
FE_TILES = 1408 // P
CAP = 168
WIDE = 192
REST = CAP - P
EPS = 1e-6
MASKED = -1e30

Z_SMALL, Z_GK, Z_GQ, Z_GV, Z_Q, Z_K, Z_V, Z_PU, Z_MO = 0, 1, 3, 5, 9, 13, 17, 21, 25
N_GATES = 2 * H + 3 * KT
S_BRANCH = Z_MO + N_GATES
S_OUT = S_BRANCH + KT // 2 * 3
S_MIX = S_OUT + KT
S_DOWN = 2 * F_TILES
S_FFN = S_DOWN + F_TILES
S_JOB = 3 * FE_TILES
LAYER1 = S_MIX + S_FFN
ROUTER = LAYER1 + S_MIX
MOE0 = ROUTER + 1
N_SLABS = MOE0 + E * S_JOB
O_BRANCH = Z_MO + N_GATES
O_OUT = O_BRANCH + KT // 2 * 6
O_MIX = O_OUT + KT
O_DOWN = 2 * F_TILES
O_FFN = O_DOWN + KT
O_LAYER1 = O_MIX + O_FFN
O_ROUTER = O_LAYER1 + O_MIX
RAW = 4
SPL = 3
FF_TILES = 6
FF_TURN = 2 * FF_TILES
FF_TURNS, FF_REST = divmod(F_TILES, FF_TILES)
GATE_PLACES = 6

C_ID, C_ONE, C_NEG, C_KEEP, C_SEL, C_INV, C_IOTA = 0, 128, 256, 384, 512, 1024, 1088
C_PART = C_IOTA + WIDE
C_TIE, C_EPS, C_HM = C_PART + 2 * NJ, C_PART + 2 * NJ + 64, C_PART + 2 * NJ + 65
N_CONST = C_HM + 2
V_N1, V_N2, V_ML, V_GLA, V_GB, V_PS, V_FN, N_VEC = 0, 8, 16, 20, 24, 26, 30, 38


class Steps:

    def __init__(self, sem, **phases):
        self.sem, self.end, n = sem, {}, 0
        for name, k in phases.items():
            n += k
            self.end[name] = n
        self.total = n

    def after(self, name, rep=0):
        return rep * self.total + self.end[name]


JOB_PLACE = [i % RAW for i in range(6 * RAW)] + [i % (RAW - 1) for i in range(S_JOB - 6 * RAW)]


def place(n):
    return n % RAW if n < MOE0 else (MOE0 + JOB_PLACE[(n - MOE0) % S_JOB]) % RAW


def arrivals(n, j=0):
    before = sum(place(m) == place(n) for m in range(n + 1))
    a_turn = range(MOE0, MOE0 + S_JOB) if n >= MOE0 else range(FF_TURN)
    return 16 * before + j * (16 * sum(place(m) == place(n) for m in a_turn))


def turn(n):
    return S_JOB if n >= MOE0 else FF_TURN


def down_slab(f):
    return 3 * f + 4 if f < FE_TILES - 1 else S_JOB - 1


REST_ON_GPSIMD = [2, 3] + [down_slab(f) for f in range(FE_TILES)]


def rest_on_gpsimd(n):
    return n >= MOE0 and (n - MOE0) % S_JOB in REST_ON_GPSIMD


def rests(n, j=0):
    own = rest_on_gpsimd(n)
    return (sum(rest_on_gpsimd(m) == own for m in range(n + 1)) +
            j * (sum(rest_on_gpsimd(m) == own for m in range(MOE0, MOE0 + S_JOB))
                 if n >= MOE0 else FF_TURN))


def slab_before(n):
    return max(m for m in range(n) if place(m) == place(n))


def token_tile(tt):
    return slice(tt * P, (tt + 1) * P)


def branch_out(k):
    return O_BRANCH + k - 2 * H


def decoder(nc, slabs, x_in, vectors, if_bias, gate_w, pool_w, consts, ml_m0, ml_n0, ml_C0,
            gla_S0, pool_in, pool_old, y_out, C_p, C_s, n_p, n_s, m_p, m_s, S_p, S_s, pool_u,
            pool_keep, gates_kept):
    ctx = ExitStack()

    def sb(name, shape, dt=F32, where=ctx):
        return where.enter_context(nc.sbuf_tensor(name, shape, dt))

    def sem(name):
        return ctx.enter_context(nc.semaphore(name))

    ps = ctx.enter_context(nc.psum_tensor("ps", [P, 8, 512], F32))
    x = sb("x", [P, KT, T])
    h_hi = sb("h_hi", [P, KT, T], F32R)
    h_lo = sb("h_lo", [P, KT, T], F32R)
    raw = sb("raw", [P, RAW, KT, P])
    w_hi = sb("w_hi", [P, SPL, KT, P], F32R)
    w_lo = sb("w_lo", [P, SPL, KT, P], F32R)
    con = sb("con", [P, N_CONST])
    vec = sb("vec", [P, DEPTH, N_VEC])
    ifb = sb("ifb", [H, DEPTH, 2])
    sq = sb("sq", [P, 2, T])
    rs = sb("rs", [P, 2, T])

    ident = con[:, C_ID:C_ID + P]
    ones = con[:, C_ONE:C_ONE + P]
    neg_mask = con[:, C_NEG:C_NEG + P]
    keep_mask = con[:, C_KEEP:C_KEEP + P]
    select = con[0:H, C_SEL:C_SEL + H * P].rearrange("k (r c) -> k r c", c=P)
    inv_count = con[:, C_INV:C_INV + 64].rearrange("p (g t) -> p g t", t=16)
    iota = con[:, C_IOTA:C_IOTA + WIDE]
    part_index = con[:, C_PART:C_PART + 2 * NJ].rearrange("p (j a) -> p j a", a=2)
    tie = con[:, C_TIE:C_TIE + 64].rearrange("p (e j) -> p e j", j=8)
    eps = con[:, C_EPS:C_EPS + 1]
    head_half = con[:, C_HM:C_HM + 2]

    mix, early, late = ExitStack(), ExitStack(), ExitStack()
    br = sb("br", [P, 12, T], where=mix)
    gla_in = ExitStack()
    gq = sb("gq", [P, 2, T], where=gla_in)
    gk = sb("gk", [P, 2, T], where=gla_in)
    gv = sb("gv", [P, H, T], where=gla_in)
    gla_in.close()
    pa = sb("pa", [P, 2, NP_TOK], where=early)
    pd = sb("pd", [P, T], where=early)
    pw = sb("pw", [P, 4, P], where=early)
    ext = sb("ext", [P, 4, NS_TOK, 16], where=early)
    pred = sb("pred", [P, NS_TOK], where=early)
    sb("rest_of_gv", [P, (4 + H) * T - 2 * NP_TOK - T - 2 * 4 * P - NS_TOK], where=early)
    q = sb("q", [P, H, T], where=early)
    k = sb("k", [P, H, T], where=early)
    v = sb("v", [P, H, T], where=early)
    row_i = sb("row_i", [H, T], where=early)
    row_f = sb("row_f", [H, T], where=early)
    row_b = sb("row_b", [H, T], where=early)
    row_M = sb("row_M", [H, T], where=early)
    acol = sb("acol", [P, TT, H], where=early)
    w3 = sb("w3", [H, 3, NS_TOK], where=early)
    w3b = sb("w3b", [P, H, 3 * NS_TOK], where=early)
    w3t = sb("w3t", [NS_TOK, 3, H], where=early)
    m_s0 = sb("m_s0", [H, NS_TOK], where=early)
    m_new = sb("m_new", [H, NS_TOK], where=early)
    m_inter = sb("m_inter", [H, NS_TOK], where=early)
    ea = sb("ea", [P, 2, NS_TOK], where=early)
    gla_mem, gla_a, gla_b, gla_c = ExitStack(), ExitStack(), ExitStack(), ExitStack()
    qz = sb("qz", [P, H, T], where=gla_mem)
    la = sb("la", [P, 2, T], where=gla_a)
    gvt = sb("gvt", [P, TT, H * P], where=gla_a)
    gkt = sb("gkt", [P, TT, 256], where=gla_a)
    ge = sb("ge", [P, 3, 2, TT], where=gla_a)
    S = sb("S", [P, 2, P], where=gla_a)
    gla_i = ExitStack()
    glr = sb("glr", [16, T], where=gla_i)
    ggw = sb("ggw", [16, 256], where=gla_i)
    gla_i.close()
    dec = sb("dec", [P, 2, T], where=gla_b)
    gla_b.close()
    att = sb("att", [P, H, P], where=gla_c)
    S_in = sb("S_in", [P, 2, P], where=gla_c)
    Ut = sb("Ut", [P, 2, P], where=gla_c)
    gla_c.close()
    gla_a.close()
    gd = ExitStack()
    Ss = sb("Ss", [P, NS_TOK, P], where=gd)
    gdiag = sb("gdiag", [NS_TOK, 2, NS_TOK, P], where=gd)
    gt8 = sb("gt8", [NS_TOK, 3, P], where=gd)
    gd.close()
    gla_mem.close()
    ml_mem = ExitStack()
    kt = sb("kt", [P, TT, P], where=ml_mem)
    vt = sb("vt", [P, TT, P], where=ml_mem)
    wgt = sb("wgt", [P, TT, NP_TOK], where=ml_mem)
    dm = sb("dm", [P, TT, P], where=ml_mem)
    den = sb("den", [P, NP_TOK], where=ml_mem)
    den2 = sb("den2", [P, NP_TOK], where=ml_mem)
    vw = sb("vw", [P, TT, P], where=ml_mem)
    wcol = sb("wcol", [P, TT], where=ml_mem)
    C_t = sb("C_t", [P, H, P], where=ml_mem)
    n_row = sb("n_row", [1, H * P], where=ml_mem)
    ml_mem.close()
    samp = ExitStack()
    Cs = sb("Cs", [P, 2, NS_TOK, P], where=samp)
    Cq = sb("Cq", [P, NS_TOK, P], where=samp)
    diag = sb("diag", [NS_TOK, 2, NS_TOK, P], where=samp)
    tok8 = sb("tok8", [NS_TOK, 3, P], where=samp)
    n_s0 = sb("n_s0", [NS_TOK, H, P], where=samp)
    nq = sb("nq", [NS_TOK, P], where=samp)
    n_tmp = sb("n_tmp", [NS_TOK, P], where=samp)
    dcol = sb("dcol", [NS_TOK, 3], where=samp)
    rdiag = sb("rdiag", [NS_TOK, NS_TOK], where=samp)
    num8 = sb("num8", [P, NS_TOK], where=samp)
    vs8 = sb("vs8", [P, NS_TOK], where=samp)
    samp.close()
    early.close()
    br_hi = sb("br_hi", [P, 12, T], F32R, where=late)
    br_lo = sb("br_lo", [P, 12, T], F32R, where=late)
    mixed = sb("mixed", [P, KT, T], where=late)
    gs = sb("gs", [P, GATE_PLACES, T], where=late)
    gt = sb("gt", [P, T], where=late)
    late.close()
    mix.close()

    ffn = ExitStack()
    a_hi = sb("a_hi", [P, F_TILES, T], F32R, where=ffn)
    a_lo = sb("a_lo", [P, F_TILES, T], F32R, where=ffn)
    sig = sb("sig", [P, T], where=ffn)
    af = sb("af", [P, 2, T], where=ffn)
    ffn.close()

    moe = ExitStack()
    ht_hi = sb("ht_hi", [P, 5, D], F32R, where=moe)
    ht_lo = sb("ht_lo", [P, 5, D], F32R, where=moe)
    lrow = sb("lrow", [E, T], where=moe)
    crow = sb("crow", [E, T], where=moe)
    cum = sb("cum", [E, T], where=moe)
    lt = sb("lt", [P, 5, E], where=moe)
    rk = sb("rk", [P, 2, 5 * E, E], where=moe)
    sel_t = sb("sel_t", [P, 5, E], where=moe)
    comb = sb("comb", [P, 5, E], where=moe)
    red = sb("red", [P, 5], where=moe)
    passes = sb("passes", [E, 3], where=moe)
    J = sb("J", [E, NJ], where=moe)
    jt = sb("jt", [1, NJ + 1], mybir.dt.int32, where=moe)
    postj = sb("postj", [P, NJ, 5], where=moe)
    combj = sb("combj", [P, NJ, 5], where=moe)
    pcol = sb("pcol", [P, 5], where=moe)
    ccol = sb("ccol", [P, 5], where=moe)
    Jb = sb("Jb", [E, P], where=moe)
    places = sb("places", [P, 2], where=moe)
    G = sb("G", [P, 5, WIDE], F32R, where=moe)
    GT = sb("GT", [P, 2, T], F32R, where=moe)
    hg = sb("hg", [P, KT, 2 * CAP], F32R, where=moe)
    gsum = sb("gsum", [P, CAP], where=moe)
    usum = sb("usum", [P, CAP], where=moe)
    msig = sb("msig", [P, CAP], where=moe)
    ma = sb("ma", [P, 2, CAP], where=moe)
    ma_hi = sb("ma_hi", [P, 2, CAP], F32R, where=moe)
    ma_lo = sb("ma_lo", [P, 2, CAP], F32R, where=moe)
    yt_hi = sb("yt_hi", [P, 2, D], F32R, where=moe)
    yt_lo = sb("yt_lo", [P, 2, D], F32R, where=moe)
    cw = sb("cw", [P, 2], where=moe)
    moe.close()
    last = ExitStack()
    yfin = sb("yfin", [P, KT, T], where=last)
    last.close()

    loaded = sem("loaded")
    x_in_half = [sem("x_in_half0"), sem("x_in_half1")]
    arrived = [sem(f"arrived{i}") for i in range(RAW)]
    hi_ready, lo_ready, lo_ready_gpsimd = sem("hi_ready"), sem("lo_ready"), sem("lo_ready_gpsimd")
    slab_done = sem("slab_done")
    first_out_done = sem("first_out_done")
    emptied = [sem("emptied0"), sem("emptied1")]
    squared, squares_used = sem("squared"), sem("squares_used")
    rs_steps, normed = sem("rs_steps"), sem("normed")
    h_hi_ready, h_lo_ready = sem("h_hi_ready"), sem("h_lo_ready")
    ggw_in, m0_in, n0_in = sem("ggw_in"), sem("m0_in"), sem("n0_in")
    S_in_s, C_in, pool_loaded = sem("S_in_s"), [sem("C_in0"), sem("C_in1")], sem("pool_loaded")
    st_S, st_C, st_nm, st_Cs, st_ns, st_Ss, st_pu, st_y, st_keep = (
        sem(n) for n in ("st_S", "st_C", "st_nm", "st_Cs", "st_ns", "st_Ss", "st_pu", "st_y", "st_keep"))
    g = Steps(sem("gla"), loga_pe=1, y=2, abs=2, exp=1, ln=1, loga=1, scan=8, diff=8, clip=1, e=5,
              qk=11, turn=TT, copy=TT, turnk=TT, copyk=TT)
    gc = Steps(sem("gla_chunk"), att=1, mask=1, sin=2, o=1, ocopy=1, su=4, ns=2)
    dg = Steps(sem("gla_decode"), turn=1, copy=1, diag=2, decay=1, add=1, o=1, oc=1)
    rows = Steps(sem("rows"), gates=2, abs=2, exp=1, ln=1, logf=1, b=1, a=1, M=1, m=2, enm=1,
                 inter=1, smax=1, sdiff=3, sexp=1, turn=1, turned=3)
    ml = Steps(sem("mlstm"), turn=1, copies=2, dm=1, exps=7, scol=1, sc01=1, p01=2, sc23=1, p23=2,
               vw=1, out=1, cst=2, absd=1, maxd=1, rec=1, h=1)
    ds = Steps(sem("mlstm_decode"), vs=1, turn=1, copy=1, diag=2, carry=1, nt=1, n=1, nq=1, den=1,
               dabs=1, dmax=1, drec=1, rd=1, add=1, cq=1, num=1, h=1)
    outer_done, gla_outer_done = sem("outer_done"), sem("gla_outer_done")
    reciprocals_spread = sem("reciprocals_spread")
    pool_phases = {"ext": 1}
    for gi in range(4):
        pool_phases[f"w{gi}"] = 3 * (gi + 1) + 5
        pool_phases[f"mm{gi}"] = 1
        pool_phases[f"y{gi}"] = 1
    po = Steps(sem("pool"), **pool_phases)
    hn_n, hn_sq, hn_ssq = sem("head_normed"), sem("head_squared"), sem("head_ssq")
    hn_ln, hn_rs = sem("head_ln"), sem("head_rs")
    br_lo_gpsimd = sem("br_lo_gpsimd")
    gated, br_hi_ready, br_lo_ready = sem("gated"), sem("br_hi_ready"), sem("br_lo_ready")
    gate_sig, mix_steps = sem("gate_sig"), sem("mix_steps")
    gate_stored = [sem("gate_stored0"), sem("gate_stored1")]
    gate_in = [sem(f"gate_in{i}") for i in range(GATE_PLACES)]
    sig_ready, act_hi, act_lo = sem("sig_ready"), sem("act_hi"), sem("act_lo")
    rt = Steps(sem("routing"), logits=1, turn=1, zero=1, lt=2, gt=1, eq=1, tie=1, rank=1, sum=1, sel=1,
               mx=1, sub=1, exp=1, tot=1, rtot=1, prob=1, chosen=1, two=1, rtwo=1, comb=1, back=1,
               backed=4, cum=1, place=1, one=1, pass1=1, pass2=1, pass3=1, last=1, ends=1, first=1,
               J0=1, J=1, shift=1, table=1, tables=4)
    ht_turned, ht_hi_ready, ht_lo_ready = sem("ht_turned"), sem("ht_hi_ready"), sem("ht_lo_ready")
    g_ready, gathered, weighed, cw_ready = (sem(n) for n in ("g_ready", "gathered", "weighed", "cw_ready"))
    hg_hi_ready, hg_lo_ready = sem("hg_hi_ready"), sem("hg_lo_ready")
    job_cols, placed, gt_ready = sem("job_cols"), sem("placed"), sem("gt_ready")
    m_sum, m_sig, m_gate, m_up, m_act = (sem(n) for n in ("m_sum", "m_sig", "m_gate", "m_up", "m_act"))
    table_loaded = sem("table_loaded")
    m_hi, m_lo = sem("m_hi"), sem("m_lo")
    yt_hi_ready, yt_lo_ready = sem("yt_hi_ready"), sem("yt_lo_ready")
    scattered, x_added = sem("scattered"), sem("x_added")
    block = ctx.enter_context(nc.Block())

    def evac(o, j=0):
        return emptied[o % 2], j * FF_TILES + (o // 2 + 1)

    def hidden(buf, j, t):
        return buf[:, bass.ds(j * FF_TILES + t, 1)].rearrange("p o t -> p (o t)")

    def gate_slab(f):
        return 3 * f - 1 if f else 0

    def gate_back(l, k):
        at = N_GATES * l + k
        return at % GATE_PLACES, (gate_in[at % GATE_PLACES], 16 * (at // GATE_PLACES + 1))

    def gate_kept(l, k):
        return gate_stored[k % 2], 16 * (N_GATES // 2 * l + k // 2 + 1)

    def split_whole(n, j=0):
        return (lo_ready_gpsimd if rest_on_gpsimd(n) else lo_ready), rests(n, j)

    def out_ps(o):
        return ps[:, 2 * (o % 2):2 * (o % 2) + 2, 0:HALF]

    def gathered_ps(b):
        return ps[:, 2 * b:2 * b + 2, 0:2 * WIDE].rearrange("p b (a c) -> p b a c", a=2)[:, :, :, 0:CAP]

    def hg_part(b, lo):
        return hg[:, 4 * b:4 * b + 4, CAP * lo:CAP * (lo + 1)].rearrange("p (b a) c -> p b a c", a=2)

    def y_ps(ct):
        return ps[0:(P, REST)[ct], 4 + 2 * ct:6 + 2 * ct]

    def halves(ap):
        return ap.rearrange("p (a b) -> p a b", a=2)

    def mixers_done(l):
        return ((po.sem, po.after("y3", l)), (st_S, 16 * (l + 1)), (st_Ss, 32 * (l + 1)),
                (st_C, 16 * H * (l + 1)), (st_nm, 48 * (l + 1)), (st_Cs, 16 * H * (l + 1)),
                (st_ns, 16 * (l + 1)))

    @block.sync
    def _(sp):
        sp.dma_start(con[:], consts).then_inc(loaded, 16)
        for i in range(2):
            half = slice(i * KT // 2, (i + 1) * KT // 2)
            sp.dma_start(x[:, half], x_in[:, half]).then_inc(x_in_half[i], 16)
        sp.dma_start(vec[:], vectors).then_inc(loaded, 16)
        sp.dma_start(ifb[:], if_bias).then_inc(loaded, 16)
        def load(n):
            if n >= RAW:
                sp.wait_ge(*split_whole(slab_before(n)))
            sp.dma_start(raw[:, place(n)], slabs[n]).then_inc(arrived[place(n)], 16)
            l, i = divmod(n - 6 - Z_MO, LAYER1)
            if 0 <= i < N_GATES:
                sp.wait_ge(*evac(l * O_LAYER1 + Z_MO + i))
                sp.dma_start(gates_kept[l, i], sq[:, i % 2]).then_inc(gate_stored[i % 2], 16)

        turns_from = S_MIX + 2 * FF_REST
        for n in range(turns_from):
            load(n)
        with sp.Fori(0, FF_TURNS) as j:
            for n in range(turns_from, turns_from + FF_TURN):
                sp.wait_ge(*split_whole(slab_before(n), j))
                sp.dma_start(raw[:, place(n)], slabs[bass.ds(j * FF_TURN + n, 1)].rearrange(
                    "o p k c -> p (o k) c")).then_inc(arrived[place(n)], 16)
        for n in range(turns_from + FF_TURNS * FF_TURN, MOE0 + RAW):
            load(n)
        sp.wait_ge(rt.sem, rt.after("tables"))
        passes_sp = sp.value_load(jt[:, NJ:NJ + 1], min_val=E, max_val=NJ - 2)
        with sp.Fori(0, passes_sp) as j:
            own = sp.value_load(jt[:, bass.ds(j, 1)], min_val=0, max_val=(E - 1) * S_JOB)
            after = sp.value_load(jt[:, bass.ds(j + 1, 1)], min_val=0, max_val=(E - 1) * S_JOB)
            for i in range(RAW, S_JOB + RAW):
                n = MOE0 + i
                first = own + n if i < S_JOB else after + (n - S_JOB)
                sp.wait_ge(*split_whole(slab_before(n), j))
                sp.dma_start(raw[:, place(n)],
                             slabs[bass.ds(first, 1)].rearrange("o p k c -> p (o k) c")).then_inc(
                                 arrived[place(n)], 16)
        for half in range(2):
            tiles = slice(KT // 2 * half, KT // 2 * (half + 1))
            sp.wait_ge(normed, KT * 4 + tiles.stop)
            sp.dma_start(y_out[:, tiles], yfin[:, tiles]).then_inc(st_y, 16)
        sp.wait_ge(st_y, 32)
        sp.wait_ge(st_keep, 16)

    @block.gpsimd
    def _(pool):
        steps = [0]

        def step(ins):
            ins.then_inc(po.sem, 1)
            steps[0] += 1
            pool.wait_ge(po.sem, steps[0])

        def pool_average(l, gi):
            w, tt_op = WINDOWS[gi], nc.gpsimd.tensor_tensor
            src, shift = br[:, 8 + gi, 0:NP_TOK], 1
            for level in range(gi + 1):
                to = pa[:, level % 2]
                step(tt_op(to[:, shift:], src[:, shift:], src[:, 0:NP_TOK - shift], ALU.add))
                step(nc.gpsimd.tensor_copy(to[:, 0:shift], src[:, 0:shift]))
                src, shift = to, 2 * shift
            if gi > 0:
                pool.wait_ge(po.sem, po.after(f"mm{gi - 1}", l))
            step(nc.gpsimd.tensor_scalar(pd[:, 0:NP_TOK], src, 1.0 / w, None, ALU.mult))
            step(tt_op(pd[:, 0:16], src[:, 0:16], inv_count[:, gi], ALU.mult))
            step(tt_op(pd[:, 0:NP_TOK], pd[:, 0:NP_TOK], br[:, 8 + gi, 0:NP_TOK], ALU.subtract))
            half = w // 2
            while half:
                step(tt_op(ext[:, gi, :, 16 - half:], ext[:, gi, :, 16 - half:],
                           ext[:, gi, :, 16 - 2 * half:16 - half], ALU.add))
                half //= 2
            step(nc.gpsimd.tensor_scalar(pred[:], ext[:, gi, :, 15], 1.0 / w, None, ALU.mult))
            step(tt_op(pd[:, NP_TOK:T], pred[:], br[:, 8 + gi, NP_TOK:T], ALU.subtract))
            steps[0] += 2
            pool.wait_ge(po.sem, po.after(f"y{gi}", l))

        for l in range(DEPTH):
            if l > 0:
                pool.wait_ge(*evac(O_LAYER1 - 1))
                pool.wait_ge(*evac(O_LAYER1 - 2))
            else:
                pool.dma_start(pool_keep, pool_old).then_inc(st_keep, 16)
            pool.dma_start(m_s0[:], ml_m0[l]).then_inc(m0_in, 16)
            pool.dma_start(ggw[:], gate_w[l]).then_inc(ggw_in, 16)
            pool.wait_ge(gc.sem, gc.after("ns", TT * l + TT - 1))
            pool.dma_start(S_p[l], S[:]).then_inc(st_S, 16)
            for j in range(2):
                i = 2 * l + j
                if j == 0:
                    pool.wait_ge(st_S, 16 * (l + 1))
                else:
                    pool.wait_ge(st_Ss, 16 * i)
                pool.dma_start(Ss[:], gla_S0[l, j]).then_inc(S_in_s, 16)
                pool.wait_ge(dg.sem, dg.after("oc", i))
                pool.dma_start(S_s[l, j], Ss[:]).then_inc(st_Ss, 16)
            pool.dma_start(pw[:], pool_w[l]).then_inc(pool_loaded, 16)
            pool.dma_start(ext[:, :, :, 0:POOL_BUF], pool_in[l]).then_inc(pool_loaded, 16)
            pool.wait_ge(*evac(l * O_LAYER1 + Z_MO - 1))
            pool.wait_ge(*evac(l * O_LAYER1 + Z_MO - 2))
            pool.dma_start(pool_u[l], br[:, 8:12, NP_TOK - POOL_BUF:T]).then_inc(st_pu, 16)
            pool.wait_ge(pool_loaded, 32 * (l + 1))
            steps[0] = po.total * l
            step(nc.gpsimd.tensor_copy(ext[:, :, :, POOL_BUF], br[:, 8:12, NP_TOK:T]))
            for h in range(H):
                pool_average(l, h)
                i = H * l + h
                pool.wait_ge(ml.sem, ml.after("cst", i))
                pool.dma_start(C_p[l, h], C_t[:, h]).then_inc(st_C, 16)
            pool.dma_start(n_p[l], n_row[:]).then_inc(st_nm, 16)
            pool.dma_start(m_p[l], row_b[:, NP_TOK - 1:NP_TOK]).then_inc(st_nm, 16)
            pool.dma_start(m_s[l], m_new[:]).then_inc(st_nm, 16)
            pool.wait_ge(ml.sem, ml.after("h", H * l + H - 1))
            pool.wait_ge(st_C, 16 * H * (l + 1))
            pool.wait_ge(st_nm, 48 * (l + 1))
            pool.dma_start(n_s0[:], ml_n0[l]).then_inc(n0_in, 16)
            for h in range(H):
                i = H * l + h
                if h == 0:
                    pool.dma_start(Cs[:, 0], ml_C0[l, 0]).then_inc(C_in[0], 16)
                if h > 0:
                    pool.wait_ge(st_Cs, 16 * i)
                if h + 1 < H:
                    pool.dma_start(Cs[:, (h + 1) % 2], ml_C0[l, h + 1]).then_inc(C_in[(h + 1) % 2], 16)
                pool.wait_ge(ds.sem, ds.after("h", i))
                pool.dma_start(C_s[l, h], Cs[:, h % 2]).then_inc(st_Cs, 16)
            pool.dma_start(n_s[l], n_s0[:]).then_inc(st_ns, 16)
            pool.wait_ge(st_Cs, 16 * H * (l + 1))
            pool.wait_ge(st_ns, 16 * (l + 1))
            for s, n in mixers_done(l):
                pool.wait_ge(s, n)

            def branch_rest(t, nth):
                pool.wait_ge(br_hi_ready, 12 * l + nth)
                nc.gpsimd.tensor_tensor(br_lo[:, t], br[:, t], br_hi[:, t].bitcast(F32),
                                        ALU.subtract).then_inc(br_lo_gpsimd, 1)

            for k in range(N_GATES):
                if k == GATE_PLACES:
                    for t in range(8, 12):
                        branch_rest(t, t - 7)
                if k in (10, 11, 12, 13):
                    branch_rest(k - 6, k - 1)
                if k >= GATE_PLACES:
                    before = k - GATE_PLACES
                    if before < 2 * H:
                        pool.wait_ge(gated, 2 * H * l + before + 1)
                    else:
                        pool.wait_ge(*evac(l * O_LAYER1 + branch_out(before)))
                pool.wait_ge(*gate_kept(l, k))
                at, back = gate_back(l, k)
                pool.dma_start(gs[:, at], gates_kept[l, k]).then_inc(back[0], 16)

        def rest(n, j=0):
            pool.wait_ge(hi_ready, j * S_JOB + (n + 1))
            nc.gpsimd.tensor_tensor(w_lo[:, n % SPL], raw[:, place(n)], w_hi[:, n % SPL].bitcast(F32),
                                    ALU.subtract).then_inc(lo_ready_gpsimd, 1)

        pool.wait_ge(h_lo_ready, 8 * 6)
        for buf in (yt_hi, yt_lo):
            nc.gpsimd.memset(buf[:].bitcast(F32), 0.0).then_inc(yt_lo_ready, 1)
        for ct in range(2):
            nc.gpsimd.memset(GT[:, ct].bitcast(F32), 0.0).then_inc(gt_ready, 1)
        rest(MOE0 + 2)
        pool.wait_ge(rt.sem, rt.after("tables"))
        passes_pool = pool.value_load(jt[:, NJ:NJ + 1], min_val=E, max_val=NJ - 2)
        with pool.Fori(0, passes_pool) as j:
            for i in REST_ON_GPSIMD[1:] + [S_JOB + 2]:
                rest(MOE0 + i, j)

    @block.scalar
    def _(act):
        def split_hi(n, j=0):
            act.wait_ge(arrived[place(n)], arrivals(n, j))
            if n >= SPL:
                act.wait_ge(slab_done, j * turn(n) + (n - SPL + 1))
            nc.scalar.activation(w_hi[:, n % SPL], raw[:, place(n)], ACT.Copy).then_inc(hi_ready, 1)

        def out_done(n):
            act.wait_ge(slab_done, n + 1)

        def norm(r, hs, ready):
            if r > 0:
                act.wait_ge(h_lo_ready, 8 * hs)
            for kk in range(KT):
                i = 8 * r + kk
                for s, n in ready(kk):
                    act.wait_ge(s, n)
                if i >= 2:
                    act.wait_ge(squares_used, i - 1)
                nc.scalar.activation(sq[:, kk % 2], x[:, kk], ACT.Square).then_inc(squared, 1)
            if r == 0:
                split_hi(0)
                split_hi(1)
            act.wait_ge(squares_used, 8 * (r + 1))
            if r > 0:
                act.wait_ge(normed, 8 * r)
            nc.scalar.activation(halves(rs[:, 0]), ps[:, 4:6, 0:HALF], ACT.Ln, bias=eps,
                                 scale=1.0 / D).then_inc(rs_steps, 1)
            act.wait_ge(rs_steps, 2 * r + 1)
            nc.scalar.activation(rs[:, 0], rs[:, 0], ACT.Exp, scale=-0.5).then_inc(rs_steps, 1)
            if r < 4:
                for kk in range(KT):
                    act.wait_ge(normed, 8 * r + kk + 1)
                    nc.scalar.activation(h_hi[:, kk], sq[:, kk % 2], ACT.Copy).then_inc(h_hi_ready, 1)

        def inputs(l, nb, ob):
            for i in range(Z_MO):
                n, o = nb + i, ob + i
                split_hi(n + 2)
                if i == Z_SMALL:
                    out_done(n)
                    src = out_ps(o)
                    nc.scalar.activation(halves(row_i[:]), src[0:H], ACT.Identity,
                                         bias=ifb[:, l, 0:1]).then_inc(rows.sem, 1)
                    nc.scalar.activation(halves(row_f[:]), src[32:32 + H], ACT.Identity,
                                         bias=ifb[:, l, 1:2]).then_inc(rows.sem, 1)
                    nc.scalar.activation(halves(glr[:]), src[64:80], ACT.Copy).then_inc(emptied[o % 2], 1)
                    continue
                for first, buf, at in ((Z_GV, gv, 0), (Z_Q, q, 0), (Z_V, v, 0), (Z_PU, br, 8)):
                    if first <= i < first + 4:
                        out_done(n)
                        nc.scalar.activation(halves(buf[:, at + i - first]), out_ps(o),
                                             ACT.Copy).then_inc(emptied[o % 2], 1)

        def gla(l):
            act.wait_ge(g.sem, g.after("loga_pe", l))
            for j in range(2):
                nc.scalar.activation(halves(la[:, j]), ps[:, 4 + 2 * j:6 + 2 * j, 0:HALF], ACT.Identity,
                                     bias=vec[:, l, V_GB + j:V_GB + j + 1]).then_inc(g.sem, 1)
            fill(2)
            act.wait_ge(g.sem, g.after("abs", l))
            nc.scalar.activation(dec[:], dec[:], ACT.Exp, scale=-1.0).then_inc(g.sem, 1)
            act.wait_ge(g.sem, g.after("exp", l))
            nc.scalar.activation(dec[:], dec[:], ACT.Ln, bias=1.0).then_inc(g.sem, 1)
            fill(4)
            act.wait_ge(g.sem, g.after("clip", l))
            mid = dec[:, :, P // 2 - 1:NP_TOK:P]
            end = la[:, :, P - 1:NP_TOK:P]
            nc.scalar.activation(ge[:, 0], mid, ACT.Exp, scale=1.0 / 16).then_inc(g.sem, 1)
            nc.scalar.activation(ge[:, 1], end, ACT.Exp, scale=1.0 / 16).then_inc(g.sem, 1)
            nc.scalar.activation(ea[:], la[:, :, NP_TOK:T], ACT.Exp, scale=1.0 / 16).then_inc(g.sem, 1)
            act.wait_ge(g.sem, g.after("clip", l) + 3)
            nc.scalar.activation(dec[:, :, 0:NP_TOK], la[:, :, 0:NP_TOK], ACT.Exp,
                                 scale=1.0 / 16).then_inc(g.sem, 1)
            act.wait_ge(g.sem, g.after("clip", l) + 4)
            nc.scalar.activation(la[:, :, 0:NP_TOK], la[:, :, 0:NP_TOK], ACT.Exp,
                                 scale=-1.0 / 16).then_inc(g.sem, 1)
            fill(2)
            for tt in range(TT):
                act.wait_ge(g.sem, g.after("turn", l))
                nc.scalar.activation(gvt[:, tt], ps[:, 4 + tt], ACT.Copy).then_inc(g.sem, 1)
            fill(1)
            for tt in range(TT):
                act.wait_ge(g.sem, g.after("turnk", l))
                nc.scalar.activation(gkt[:, tt], ps[:, 4 + tt, 0:256], ACT.Copy).then_inc(g.sem, 1)
            fill(1)
            for tt in range(TT):
                rep = TT * l + tt
                fill(1)
                act.wait_ge(gc.sem, gc.after("o", rep))
                nc.scalar.activation(br[:, 4:8, token_tile(tt)],
                                     ps[:, 6, :].rearrange("p (h t) -> p h t", t=P),
                                     ACT.Copy).then_inc(gc.sem, 1)
                fill(1)
            for j in range(2):
                fill(4)

        def mlstm(l):
            act.wait_ge(rows.sem, rows.after("abs", l))
            nc.scalar.activation(row_M[:], row_M[:], ACT.Exp, scale=-1.0).then_inc(rows.sem, 1)
            act.wait_ge(rows.sem, rows.after("exp", l))
            nc.scalar.activation(row_M[:], row_M[:], ACT.Ln, bias=1.0).then_inc(rows.sem, 1)
            fill(2)
            act.wait_ge(rows.sem, rows.after("m", l))
            nc.scalar.activation(row_f[:, 0:NP_TOK], row_b[:, 0:NP_TOK], ACT.Exp,
                                 scale=-1.0).then_inc(rows.sem, 1)
            act.wait_ge(rows.sem, rows.after("sdiff", l))
            nc.scalar.activation(w3[:], w3[:], ACT.Exp).then_inc(rows.sem, 1)
            fill(2)
            for h in range(H):
                rep = H * l + h
                at = lambda name: act.wait_ge(ml.sem, ml.after(name, rep))
                at("turn")
                nc.scalar.activation(kt[:], ps[:, 4].rearrange("p (a d) -> p a d", d=P),
                                     ACT.Copy).then_inc(ml.sem, 1)
                fill(2)
                at("dm")
                for tt in range(TT):
                    nc.scalar.activation(wgt[:, tt, token_tile(tt)], dm[:, tt], ACT.Exp,
                                         bias=acol[:, tt, h:h + 1]).then_inc(ml.sem, 1)
                for tt in range(TT - 1):
                    rest = slice((tt + 1) * P, NP_TOK)
                    nc.scalar.activation(wgt[:, tt, rest], ps[:, 6, rest], ACT.Exp,
                                         bias=acol[:, tt, h:h + 1]).then_inc(ml.sem, 1)
                fill(2)
                at("out")
                nc.scalar.activation(C_t[:, h], ps[:, 5, 0:P], ACT.Copy).then_inc(ml.sem, 1)
                nc.scalar.activation(n_row[:, h * P:(h + 1) * P], ps[0:1, 5, P:2 * P],
                                     ACT.Copy).then_inc(ml.sem, 1)
                at("cst")
                nc.scalar.activation(den[:], ps[:, 7], ACT.Abs).then_inc(ml.sem, 1)
                fill(2)
                pool_out(l, h)
                fill(1)
            for h in range(H):
                fill(4)

        def pool_out(l, gi):
            act.wait_ge(po.sem, po.after(f"mm{gi}", l))
            act.wait_ge(st_pu, 16 * (l + 1))
            nc.scalar.activation(halves(br[:, 8 + gi]), ps[:, 4:6, 0:HALF], ACT.Copy,
                                 scale=vec[:, l, V_PS + gi:V_PS + gi + 1]).then_inc(po.sem, 1)

        def head_norm(l):
            act.wait_ge(h_lo_ready, 8 * (3 * l + 1))
            act.wait_ge(ds.sem, ds.after("h", H * l + H - 1))
            for t in range(9):
                if t < 8:
                    i = 8 * l + t
                    if t >= 2:
                        act.wait_ge(hn_ssq, i - 1)
                    nc.scalar.activation(sq[:, t % 2], br[:, t], ACT.Square).then_inc(hn_sq, 1)
                if t == 1:
                    for s, n in mixers_done(l):
                        act.wait_ge(s, n)
                if t > 0:
                    b, i = (t - 1) % 2, 8 * l + t - 1
                    act.wait_ge(hn_ssq, i + 1)
                    nc.scalar.activation(halves(mixed[:, t - 1]), ps[:, 4 + 2 * b:6 + 2 * b, 0:HALF],
                                         ACT.Ln, bias=eps, scale=1.0 / P).then_inc(hn_ln, 1)
            act.wait_ge(hn_ln, 8 * (l + 1))
            for t in range(0, 8, 2):
                nc.scalar.activation(mixed[:, t:t + 2], mixed[:, t:t + 2], ACT.Exp,
                                     scale=-0.5).then_inc(hn_rs, 1)

        def fill(k):
            for _ in range(k):
                i, half = divmod(fills[0], 2)
                fills[0] += 1
                if half or i >= N_GATES:
                    continue
                split_hi(fills[1] * LAYER1 + Z_MO + i + 2)
                if i > 0:
                    gate_out(fills[1], i - 1)

        def gate_out(l, i):
            n, o = l * LAYER1 + Z_MO + i, l * O_LAYER1 + Z_MO + i
            out_done(n)
            if i >= 2:
                act.wait_ge(*gate_kept(l, i - 2))
            to = emptied[o % 2] if not H <= i < 2 * H else gate_sig
            nc.scalar.activation(halves(sq[:, i % 2]), out_ps(o), ACT.Sigmoid).then_inc(to, 1)

        def filled(l):
            fill(2 * N_GATES - fills[0])
            gate_out(l, N_GATES - 1)
            for i in range(2):
                act.wait_ge(*gate_kept(l, N_GATES - 2 + i))

        def gates(l):
            for j in (8, 9, 10, 11, 0, 1, 2, 3, 4, 5, 6, 7):
                if j < 8:
                    act.wait_ge(gated, 8 * l + j + 1)
                nc.scalar.activation(br_hi[:, j], br[:, j], ACT.Copy).then_inc(br_hi_ready, 1)

        def merge(l, nb, ob):
            for s in range(KT // 2 * 3):
                split_hi(nb + S_BRANCH + s + 2)
            act.wait_ge(slab_done, nb + S_BRANCH)
            act.wait_ge(mix_steps, 16 * (l + 1))
            for kk in range(KT):
                nc.scalar.activation(h_hi[:, kk], mixed[:, kk], ACT.Copy).then_inc(h_hi_ready, 1)
            for m in range(KT):
                split_hi(nb + S_OUT + m + 2)

        def hidden_tiles(nf, of, j, tiles):
            for t in range(tiles):
                split_hi(nf + 2 * t + 2, j)
                act.wait_ge(slab_done, j * FF_TURN + (nf + 2 * t + 1))
                nc.scalar.activation(halves(sig[:]), out_ps(of + 2 * t), ACT.Sigmoid).then_inc(sig_ready, 1)
                split_hi(nf + 2 * t + 3, j)
                act.wait_ge(*evac(of + 2 * t + 1, j))
                nc.scalar.activation(hidden(a_hi, j, t), af[:, t % 2], ACT.Copy).then_inc(act_hi, 1)

        def feed_forward(nf, of):
            with act.Fori(0, FF_TURNS) as j:
                hidden_tiles(nf, of, j, FF_TILES)
            hidden_tiles(nf, of, FF_TURNS, FF_REST)
            for s in range(F_TILES):
                split_hi(nf + S_DOWN + s + 2)


        def gathered_hi(p, b):
            act.wait_ge(gathered, p * 2 + (b + 1))
            nc.scalar.activation(hg_part(b, 0), gathered_ps(b), ACT.Copy).then_inc(hg_hi_ready, 1)

        def turned(i):
            rws = P if i < 4 else NS_TOK
            for a, (to, ready) in enumerate(((ht_hi, ht_hi_ready), (ht_lo, ht_lo_ready))):
                act.wait_ge(ht_turned, 2 * i + a + 1)
                nc.scalar.activation(to[0:rws, i].rearrange("p (a d) -> p a d", a=2),
                                     ps[0:rws, 2 * a:2 * a + 2], ACT.Copy).then_inc(ready, 1)

        def routing():
            split_hi(ROUTER + 2)
            for i in range(2):
                turned(i)
            act.wait_ge(rt.sem, rt.after("sub"))
            nc.scalar.activation(comb[:], comb[:], ACT.Exp).then_inc(rt.sem, 1)
            for i in range(2, 5):
                turned(i)

        def expert_pass(j):
            s0, f0 = MOE0, j * FE_TILES
            nc.scalar.activation(msig[0:1, 0:1], eps[0:1], ACT.Sigmoid).then_inc(table_loaded, 1)
            for f in range(FE_TILES):
                if f > 0:
                    split_hi(s0 + gate_slab(f) + 2, j)
                act.wait_ge(m_sum, f0 + (f + 1))
                if f == 0:
                    act.wait_ge(table_loaded, j + 1)
                nc.scalar.activation(msig[:], gsum[:], ACT.Sigmoid).then_inc(m_sig, 1)
                split_hi(s0 + gate_slab(f) + 3, j)
                if f > 0:
                    split_hi(s0 + down_slab(f - 1) + 2, j)
                act.wait_ge(m_act, f0 + (f + 1))
                nc.scalar.activation(ma_hi[:, f % 2], ma[:, f % 2], ACT.Copy).then_inc(m_hi, 1)
            split_hi(s0 + down_slab(FE_TILES - 1) + 2, j)
            gathered_hi(j + 1, 0)
            split_hi(s0 + 2, j + 1)
            act.wait_ge(slab_done, j * S_JOB + (s0 + S_JOB))
            act.wait_ge(cw_ready, j * 2 + 2)
            for ct in range(2):
                rws = slice(0, (P, REST)[ct])
                nc.scalar.activation(yt_hi[rws, ct].rearrange("p (a d) -> p a d", a=2), y_ps(ct),
                                     ACT.Copy, scale=cw[rws, ct:ct + 1]).then_inc(yt_hi_ready, 1)
            gathered_hi(j + 1, 1)

        fills = [0, 0]
        act.wait_ge(loaded, 48)
        for l in range(DEPTH):
            nb, ob = l * LAYER1, l * O_LAYER1
            norm(2 * l, 3 * l, lambda kk: [evac(O_LAYER1 - KT + kk) if l else (x_in_half[kk // 4], 16)])
            inputs(l, nb, ob)
            fills[:] = 0, l
            gla(l)
            mlstm(l)
            filled(l)
            head_norm(l)
            gates(l)
            merge(l, nb, ob)
            norm(2 * l + 1, 3 * l + 2, lambda kk: [evac(ob + O_OUT + kk)])
            if l == 0:
                feed_forward(S_MIX, O_MIX)
            else:
                routing()
                act.wait_ge(rt.sem, rt.after("tables"))
                passes_act = act.value_load(jt[:, NJ:NJ + 1], min_val=E, max_val=NJ - 2)
                split_hi(MOE0 + 2)
                gathered_hi(0, 0)
                gathered_hi(0, 1)
                with act.Fori(0, passes_act) as j:
                    expert_pass(j)
        norm(4, 6, lambda kk: [] if kk else [(x_added, passes_act * KT + KT)])

    @block.vector
    def _(dve):
        tt_op = nc.vector.tensor_tensor
        ts_op = nc.vector.tensor_scalar
        stt_op = nc.vector.scalar_tensor_tensor

        def split_lo(n, j=0):
            if rest_on_gpsimd(n):
                return
            dve.wait_ge(hi_ready, j * turn(n) + (n + 1))
            tt_op(w_lo[:, n % SPL], raw[:, place(n)], w_hi[:, n % SPL].bitcast(F32),
                  ALU.subtract).then_inc(lo_ready, 1)

        def out_done(n):
            dve.wait_ge(slab_done, n + 1)

        def norm(r, hs):
            gain = vec[:, 1, V_FN:V_FN + KT] if r == 4 else vec[:, r // 2, (V_N1, V_N2)[r % 2]:][:, 0:KT]
            dve.wait_ge(rs_steps, 2 * r + 2)
            for kk in range(KT + 1):
                if kk < KT:
                    if r < 4 and kk >= 2:
                        dve.wait_ge(h_lo_ready, 8 * hs + kk - 1)
                    to = yfin[:, kk] if r == 4 else sq[:, kk % 2]
                    stt_op(to, x[:, kk], gain[:, kk:kk + 1], rs[:, 0], ALU.mult,
                           ALU.mult).then_inc(normed, 1)
                if r < 4 and kk > 0:
                    dve.wait_ge(h_hi_ready, 8 * hs + kk)
                    tt_op(h_lo[:, kk - 1], sq[:, (kk - 1) % 2], h_hi[:, kk - 1].bitcast(F32),
                          ALU.subtract).then_inc(h_lo_ready, 1)

        def inputs(l, nb, ob):
            for i in range(Z_MO):
                n, o = nb + i, ob + i
                split_lo(n + 2)
                for first, last, buf, scale in ((Z_GK, Z_GQ, gk, 1.0), (Z_GQ, Z_GV, gq, DK ** -0.5),
                                                (Z_K, Z_V, k, P ** -0.5)):
                    if first <= i < last:
                        out_done(n)
                        ts_op(halves(buf[:, i - first]), out_ps(o), scale, None,
                              ALU.mult).then_inc(emptied[o % 2], 1)

        def gla(l):
            at = lambda name, more=0: dve.wait_ge(g.sem, g.after(name, l) + more)
            inc = lambda ins: ins.then_inc(g.sem, 1)
            at("y")
            inc(stt_op(dec[:], la[:], -1.0, la[:], ALU.mult, ALU.max))
            inc(ts_op(la[:], la[:], 0.0, None, ALU.min))
            fill(2)
            at("ln")
            inc(tt_op(la[:], la[:], dec[:], ALU.subtract))
            at("loga")
            for j in range(2):
                for tt in range(TT):
                    inc(nc.vector.tensor_tensor_scan(dec[:, j, token_tile(tt)], la[:, j, token_tile(tt)],
                                                     la[:, j, token_tile(tt)], 0.0, ALU.add, ALU.bypass))
            fill(2)
            at("scan")
            for j in range(2):
                for tt in range(TT):
                    c = tt * P + P // 2 - 1
                    inc(ts_op(la[:, j, token_tile(tt)], dec[:, j, token_tile(tt)], dec[:, j, c:c + 1],
                              -1280.0, ALU.subtract, ALU.max))
            at("diff")
            inc(ts_op(la[:, :, 0:NP_TOK], la[:, :, 0:NP_TOK], 1280.0, None, ALU.min))
            fill(2)
            at("e")
            for h in range(H):
                inc(stt_op(qz[:, h, 0:NP_TOK], gq[:, h // 2, 0:NP_TOK], head_half[:, h % 2:h % 2 + 1],
                           dec[:, h // 2, 0:NP_TOK], ALU.mult, ALU.mult))
                inc(ts_op(qz[:, h, NP_TOK:T], gq[:, h // 2, NP_TOK:T], head_half[:, h % 2:h % 2 + 1],
                          None, ALU.mult))
            inc(tt_op(gk[:, :, 0:NP_TOK], gk[:, :, 0:NP_TOK], la[:, :, 0:NP_TOK], ALU.mult))
            inc(tt_op(ge[:, 2], ge[:, 0], ge[:, 1], ALU.mult))
            inc(nc.vector.memset(S[:], 0.0))
            fill(4)
            at("copyk")
            for tt in range(TT):
                rep = TT * l + tt
                at = lambda name: dve.wait_ge(gc.sem, gc.after(name, rep))
                inc = lambda ins: ins.then_inc(gc.sem, 1)
                at("att")
                inc(tt_op(att[:], ps[:, 4].rearrange("p (h t) -> p h t", t=P),
                          keep_mask.unsqueeze(1).to_broadcast([P, H, P]), ALU.mult))
                for j in range(2):
                    inc(ts_op(S_in[:, j], S[:, j], ge[:, 0, j, tt:tt + 1], None, ALU.mult))
                fill(1)
                at("ocopy")
                for j in range(2):
                    for half in range(2):
                        rws = slice(64 * half, 64 * half + 64)
                        c = 256 * j + P * half
                        inc(ts_op(Ut[rws, j], ps[rws, 5, c:c + P], ge[rws, 1, j, tt:tt + 1], None,
                                  ALU.mult))
                at("su")
                for j in range(2):
                    inc(stt_op(S[:, j], S[:, j], ge[:, 2, j, tt:tt + 1], Ut[:, j], ALU.mult, ALU.add))
                fill(1)

        def gla_decode(l):
            for j in range(2):
                rep = 2 * l + j
                at = lambda name: dve.wait_ge(dg.sem, dg.after(name, rep))
                inc = lambda ins: ins.then_inc(dg.sem, 1)
                at("turn")
                inc(nc.vector.tensor_copy(gt8[:], ps[0:NS_TOK, 4, 0:3 * P].rearrange(
                    "b (a d) -> b a d", d=P)))
                at("copy")
                for half in range(2):
                    spread(inc, gdiag[:, half], gt8[:, 1 + half])
                fill(2)
                dve.wait_ge(S_in_s, 16 * (rep + 1))
                inc(tt_op(Ss[:], Ss[:], ea[:, j].unsqueeze(2).to_broadcast([P, NS_TOK, P]), ALU.mult))
                at("decay")
                dve.wait_ge(gla_outer_done, rep + 1)
                inc(tt_op(Ss[:].rearrange("p (a b) d -> p a (b d)", a=2), Ss[:].rearrange("p (a b) d -> p a (b d)", a=2),
                          ps[:, 4:6], ALU.add))
                fill(2)
                at("o")
                inc(nc.vector.tensor_copy(br[:, 4 + 2 * j:6 + 2 * j, NP_TOK:T],
                                          ps[:, 6, 0:16].rearrange("p (b h) -> p h b", h=2)))

        def spread(inc, to, rows8):
            inc(tt_op(to, rows8.unsqueeze(1).to_broadcast([NS_TOK, NS_TOK, P]),
                      ident[0:NS_TOK, 0:NS_TOK].unsqueeze(2).to_broadcast([NS_TOK, NS_TOK, P]),
                      ALU.mult))

        def mlstm_rows(l):
            at = lambda name: dve.wait_ge(rows.sem, rows.after(name, l))
            inc = lambda ins: ins.then_inc(rows.sem, 1)
            pr, sa = slice(0, NP_TOK), slice(NP_TOK, T)
            at("gates")
            inc(stt_op(row_M[:], row_f[:], -1.0, row_f[:], ALU.mult, ALU.max))
            inc(ts_op(row_f[:], row_f[:], 0.0, None, ALU.min))
            at("ln")
            inc(tt_op(row_f[:], row_f[:], row_M[:], ALU.subtract))
            at("logf")
            inc(nc.vector.tensor_tensor_scan(row_b[:, pr], row_f[:, pr], row_f[:, pr], 0.0, ALU.add,
                                             ALU.bypass))
            at("b")
            inc(tt_op(row_i[:, pr], row_i[:, pr], row_b[:, pr], ALU.subtract))
            at("a")
            inc(nc.vector.tensor_tensor_scan(row_M[:, pr], row_i[:, pr], row_i[:, pr], 0.0, ALU.max,
                                             ALU.bypass))
            at("M")
            inc(tt_op(row_b[:, pr], row_b[:, pr], row_M[:, pr], ALU.add))
            fill(2)
            dve.wait_ge(rows.sem, rows.after("M", l) + 1)
            inc(ts_op(row_M[:, pr], row_M[:, pr], -1.0, None, ALU.mult))
            at("enm")
            dve.wait_ge(m0_in, 16 * (l + 1))
            inc(tt_op(m_inter[:], row_f[:, sa], m_s0[:], ALU.add))
            at("inter")
            inc(tt_op(m_new[:], m_inter[:], row_i[:, sa], ALU.max))
            at("smax")
            inc(tt_op(w3[:, 0], row_i[:, sa], m_new[:], ALU.subtract))
            inc(tt_op(w3[:, 1], m_inter[:], m_new[:], ALU.subtract))
            inc(ts_op(w3[:, 2], m_new[:], -1.0, None, ALU.mult))
            fill(2)
            at("turn")
            inc(nc.vector.tensor_copy(acol[:], ps[:, 4, 0:16].rearrange("p (a h) -> p a h", h=H)))
            inc(nc.vector.tensor_copy(w3t[:], ps[0:NS_TOK, 4, 32:44].rearrange("p (a h) -> p a h", h=H)))
            inc(nc.vector.tensor_copy(w3b[:], ps[:, 5, 0:96].rearrange("p (h w) -> p h w", h=H)))
            at("turned")

        def mlstm(l):
            for h in range(H):
                rep = H * l + h
                at = lambda name: dve.wait_ge(ml.sem, ml.after(name, rep))
                inc = lambda ins: ins.then_inc(ml.sem, 1)
                at("turn")
                inc(nc.vector.tensor_copy(vt[:], ps[:, 5].rearrange("p (a d) -> p a d", d=P)))
                at("copies")
                inc(tt_op(dm[:], ps[:, 6].rearrange("p (a d) -> p a d", d=P),
                          neg_mask.unsqueeze(1).to_broadcast([P, TT, P]), ALU.add))
                fill(2)
                at("exps")
                inc(nc.vector.tensor_copy(wcol[:], wgt[:, :, NP_TOK - 1]))
                at("sc01")
                for tt in range(2):
                    inc(tt_op(wgt[:, tt, tt * P:], wgt[:, tt, tt * P:], ps[:, 4 + tt, 0:NP_TOK - tt * P],
                              ALU.mult))
                fill(1)
                at("sc23")
                for tt in range(2, 4):
                    at_ps = ps[:, 4, 256 * (tt - 2):256 * (tt - 2) + NP_TOK - tt * P]
                    inc(tt_op(wgt[:, tt, tt * P:], wgt[:, tt, tt * P:], at_ps, ALU.mult))
                at("scol")
                dve.wait_ge(ml.sem, ml.after("p23", rep))
                inc(tt_op(vw[:], vt[:], wcol[:].unsqueeze(2).to_broadcast([P, TT, P]), ALU.mult))
                fill(1)
                at("absd")
                inc(tt_op(den[:], den[:], ps[:, 4], ALU.max))
                at("maxd")
                inc(nc.vector.reciprocal(den2[:], den[:]))
                at("rec")
                inc(tt_op(br[:, h, 0:NP_TOK], ps[:, 6], den2[:], ALU.mult))
                fill(3)
                at("h")

        def mlstm_decode(l):
            dve.wait_ge(st_C, 16 * H * (l + 1))
            dve.wait_ge(st_nm, 48 * (l + 1))
            for h in range(H):
                rep, C_h = H * l + h, Cs[:, h % 2]
                at = lambda name: dve.wait_ge(ds.sem, ds.after(name, rep))
                inc = lambda ins: ins.then_inc(ds.sem, 1)
                if h > 0:
                    dve.wait_ge(ds.sem, ds.after("h", rep - 1))
                inc(tt_op(vs8[:], v[:, h, NP_TOK:T], w3b[:, h, 0:NS_TOK], ALU.mult))
                at("turn")
                inc(nc.vector.tensor_copy(tok8[:], ps[0:NS_TOK, 4, 0:3 * P].rearrange(
                    "b (a d) -> b a d", d=P)))
                at("copy")
                for a in range(2):
                    spread(inc, diag[:, a], tok8[:, 1 + a])
                fill(2)
                dve.wait_ge(C_in[h % 2], 16 * (rep // 2 + 1))
                inc(tt_op(C_h, C_h, w3b[:, h, NS_TOK:2 * NS_TOK].unsqueeze(2).to_broadcast(
                    [P, NS_TOK, P]), ALU.mult))
                inc(ts_op(n_tmp[:], tok8[:, 1], w3t[:, 0, h:h + 1], None, ALU.mult))
                at("nt")
                dve.wait_ge(n0_in, 16 * (l + 1))
                inc(stt_op(n_s0[:, h], n_s0[:, h], w3t[:, 1, h:h + 1], n_tmp[:], ALU.mult, ALU.add))
                at("n")
                inc(tt_op(nq[:], n_s0[:, h], tok8[:, 2], ALU.mult))
                at("nq")
                inc(nc.vector.tensor_reduce(dcol[:, 0:1], nq[:], AX.X, ALU.add))
                at("den")
                inc(stt_op(dcol[:, 1:2], dcol[:, 0:1], -1.0, dcol[:, 0:1], ALU.mult, ALU.max))
                at("dabs")
                inc(ts_op(dcol[:, 1:2], dcol[:, 1:2], w3t[:, 2, h:h + 1], None, ALU.max))
                at("dmax")
                inc(nc.vector.reciprocal(dcol[:, 2:3], dcol[:, 1:2]))
                at("drec")
                inc(ts_op(rdiag[:], ident[0:NS_TOK, 0:NS_TOK], dcol[:, 2:3], None, ALU.mult))
                dve.wait_ge(outer_done, rep + 1)
                C2 = C_h.rearrange("p (a b) d -> p a (b d)", a=2)
                inc(tt_op(C2, C2, ps[:, 4:6], ALU.add))
                at("add")
                inc(tt_op(Cq[:].rearrange("p (a b) d -> p a (b d)", a=2), C2, ps[:, 6:8], ALU.mult))
                fill(2)
                at("cq")
                inc(nc.vector.tensor_reduce(num8[:], Cq[:], AX.X, ALU.add))
                at("num")
                dve.wait_ge(reciprocals_spread, rep + 1)
                inc(tt_op(br[:, h, NP_TOK:T], num8[:], ps[:, 4, 0:NS_TOK], ALU.mult))

        def fill(k):
            for _ in range(k):
                i, half = divmod(fills[0], 2)
                fills[0] += 1
                if half or i >= N_GATES:
                    continue
                split_lo(fills[1] * LAYER1 + Z_MO + i + 2)
                if H < i <= 2 * H:
                    o = fills[1] * O_LAYER1 + Z_MO + i - 1
                    dve.wait_ge(gate_sig, H * fills[1] + i - H)
                    tt_op(halves(sq[:, (i - 1) % 2]), halves(sq[:, (i - 1) % 2]), out_ps(o),
                          ALU.mult).then_inc(emptied[o % 2], 1)

        def gates(l):
            for s, n in mixers_done(l):
                dve.wait_ge(s, n)
            for k in range(2 * H):
                dve.wait_ge(hn_rs, 4 * l + k // 2 + 1)
                gain = vec[:, l, V_ML + k:V_ML + k + 1]
                stt_op(br[:, k], br[:, k], gain, mixed[:, k], ALU.mult, ALU.mult).then_inc(hn_n, 1)
                at, back = gate_back(l, k)
                dve.wait_ge(*back)
                dve.wait_ge(hn_n, 2 * H * l + k + 1)
                tt_op(br[:, k], br[:, k], gs[:, at], ALU.mult).then_inc(gated, 1)
                if 0 < k <= H:
                    dve.wait_ge(br_hi_ready, 12 * l + 4 + k)
                    tt_op(br_lo[:, k - 1], br[:, k - 1], br_hi[:, k - 1].bitcast(F32),
                          ALU.subtract).then_inc(br_lo_ready, 1)

        def merge(l, nb, ob):
            steps = 16 * l
            for mp in range(KT // 2):
                for s, outs in enumerate((((0, 0), (1, 0)), ((0, 1), (1, 1)), ((2, 0), (2, 1)))):
                    n = nb + S_BRANCH + 3 * mp + s
                    split_lo(n + 2)
                    for i, (branch, m) in enumerate(outs):
                        if i == 0:
                            dve.wait_ge(first_out_done, 12 * l + 3 * mp + s + 1)
                        else:
                            out_done(n)
                        k = 2 * H + 6 * mp + 2 * s + i
                        o = ob + branch_out(k)
                        at, back = gate_back(l, k)
                        dve.wait_ge(*back)
                        if branch > 0 and steps > 0:
                            dve.wait_ge(mix_steps, steps)
                        to = mixed[:, 2 * mp + m] if branch == 0 else gt[:]
                        tt_op(halves(to), out_ps(o), halves(gs[:, at]), ALU.mult).then_inc(
                            emptied[o % 2], 1)
                        if branch > 0:
                            dve.wait_ge(*evac(o))
                            dve.wait_ge(*evac(ob + branch_out(2 * H + 6 * mp + 2 * m)))
                            tt_op(mixed[:, 2 * mp + m], mixed[:, 2 * mp + m], gt[:], ALU.add).then_inc(
                                mix_steps, 1)
                            steps += 1
            for kk in range(KT):
                dve.wait_ge(h_hi_ready, 8 * (3 * l + 1) + kk + 1)
                tt_op(h_lo[:, kk], mixed[:, kk], h_hi[:, kk].bitcast(F32), ALU.subtract).then_inc(
                    h_lo_ready, 1)
            for m in range(KT):
                n, o = nb + S_OUT + m, ob + O_OUT + m
                split_lo(n + 2)
                out_done(n)
                tt_op(halves(x[:, m]), halves(x[:, m]), out_ps(o), ALU.add).then_inc(emptied[o % 2], 1)

        def hidden_tiles(nf, of, j, tiles):
            for t in range(tiles):
                o, f = of + 2 * t, j * FF_TILES + (t + 1)
                split_lo(nf + 2 * t + 2, j)
                split_lo(nf + 2 * t + 3, j)
                dve.wait_ge(sig_ready, f)
                tt_op(halves(af[:, t % 2]), out_ps(o), halves(sig[:]), ALU.mult).then_inc(
                    emptied[o % 2], 1)
                dve.wait_ge(*evac(o, j))
                dve.wait_ge(slab_done, j * FF_TURN + (nf + 2 * t + 2))
                tt_op(halves(af[:, t % 2]), halves(af[:, t % 2]), out_ps(o + 1), ALU.mult).then_inc(
                    emptied[(o + 1) % 2], 1)
                dve.wait_ge(act_hi, f)
                tt_op(hidden(a_lo, j, t), af[:, t % 2], hidden(a_hi, j, t).bitcast(F32),
                      ALU.subtract).then_inc(act_lo, 1)
                dve.wait_ge(act_lo, f)

        def feed_forward(nf, of):
            with dve.Fori(0, FF_TURNS) as j:
                hidden_tiles(nf, of, j, FF_TILES)
            hidden_tiles(nf, of, FF_TURNS, FF_REST)
            m = 0
            for s in range(F_TILES):
                split_lo(nf + S_DOWN + s + 2)
                while m < KT and (F_TILES * (m + 1) - 1) // 8 == s:
                    o = of + O_DOWN + m
                    out_done(nf + S_DOWN + s)
                    tt_op(halves(x[:, m]), halves(x[:, m]), out_ps(o), ALU.add).then_inc(
                        emptied[o % 2], 1)
                    m += 1


        def prepare(p):
            nc.vector.tensor_copy(pcol[:], postj[:, bass.ds(p, 1)].rearrange("p o t -> p (o t)")).then_inc(g_ready, 1)
            nc.vector.tensor_copy(ccol[:], combj[:, bass.ds(p, 1)].rearrange("p o t -> p (o t)")).then_inc(g_ready, 1)
            dve.wait_ge(g_ready, p * 7 + 2)
            for tt in range(5):
                rws = P if tt < 4 else NS_TOK
                ts_op(G[0:rws, tt], iota[0:rws], pcol[0:rws, tt:tt + 1], None, ALU.is_equal).then_inc(
                    g_ready, 1)

        def gathered_lo(p, b):
            dve.wait_ge(hg_hi_ready, p * 2 + (b + 1))
            tt_op(hg_part(b, 1), gathered_ps(b), hg_part(b, 0).bitcast(F32),
                  ALU.subtract).then_inc(hg_lo_ready, 1)

        def routing():
            split_lo(ROUTER + 2)
            at = lambda name, more=0: dve.wait_ge(rt.sem, rt.after(name) + more)
            inc = lambda ins: ins.then_inc(rt.sem, 1)
            out_done(ROUTER)
            inc(nc.vector.tensor_copy(halves(lrow[:]), out_ps(O_ROUTER)[0:E]))
            at("turn")
            inc(nc.vector.memset(lt[:], 0.0))
            at("zero")
            inc(nc.vector.tensor_copy(lt[:, 0:4], ps[:, 4, 0:4 * E].rearrange("p (t e) -> p t e", e=E)))
            inc(nc.vector.tensor_copy(lt[0:NS_TOK, 4], ps[0:NS_TOK, 4, 4 * E:5 * E]))
            at("lt")
            other = lt[:].unsqueeze(2).to_broadcast([P, 5, E, E])
            own = lt[:].unsqueeze(3).to_broadcast([P, 5, E, E])
            rk4 = [rk[:, a].rearrange("p (t e) j -> p t e j", e=E) for a in range(2)]
            inc(tt_op(rk4[0], other, own, ALU.is_gt))
            inc(tt_op(rk4[1], other, own, ALU.is_equal))
            at("eq")
            inc(tt_op(rk4[1], rk4[1], tie.unsqueeze(1).to_broadcast([P, 5, E, E]), ALU.mult))
            at("tie")
            inc(tt_op(rk[:, 0], rk[:, 0], rk[:, 1], ALU.add))
            at("rank")
            inc(nc.vector.tensor_reduce(sel_t[:].rearrange("p t e -> p (t e)"), rk[:, 0], AX.X, ALU.add))
            at("sum")
            inc(ts_op(sel_t[:], sel_t[:], 2.0, None, ALU.is_lt))
            inc(nc.vector.tensor_reduce(red[:], lt[:], AX.X, ALU.max))
            at("mx")
            wide = red[:].unsqueeze(2).to_broadcast([P, 5, E])
            inc(tt_op(comb[:], lt[:], wide, ALU.subtract))
            at("exp")
            inc(nc.vector.tensor_reduce(red[:], comb[:], AX.X, ALU.add))
            at("tot")
            inc(nc.vector.reciprocal(red[:], red[:]))
            at("rtot")
            inc(tt_op(comb[:], comb[:], wide, ALU.mult))
            at("prob")
            inc(tt_op(comb[:], comb[:], sel_t[:], ALU.mult))
            at("chosen")
            inc(nc.vector.tensor_reduce(red[:], comb[:], AX.X, ALU.add))
            at("two")
            inc(nc.vector.reciprocal(red[:], red[:]))
            at("rtwo")
            inc(tt_op(comb[:], comb[:], wide, ALU.mult))
            at("back")
            inc(nc.vector.tensor_copy(lrow[:, 0:NP_TOK], ps[0:E, 4]))
            inc(nc.vector.tensor_copy(crow[:, 0:NP_TOK], ps[0:E, 5]))
            inc(nc.vector.tensor_copy(lrow[:, NP_TOK:T], ps[0:E, 6, 0:NS_TOK]))
            inc(nc.vector.tensor_copy(crow[:, NP_TOK:T], ps[0:E, 6, NS_TOK:2 * NS_TOK]))
            at("backed")
            inc(nc.vector.tensor_tensor_scan(cum[:], lrow[:], lrow[:], 0.0, ALU.add, ALU.bypass))
            at("cum")
            inc(tt_op(lrow[:], lrow[:], cum[:], ALU.mult))
            at("place")
            inc(ts_op(lrow[:], lrow[:], -1.0, None, ALU.add))
            n = cum[:, T - 1:T]
            inc(ts_op(passes[:, 0:1], n, float(CAP), 1.0, ALU.is_gt, ALU.add))
            at("pass1")
            inc(stt_op(passes[:, 0:1], n, float(2 * CAP), passes[:, 0:1], ALU.is_gt, ALU.add))
            at("pass2")
            inc(stt_op(passes[:, 0:1], n, float(3 * CAP), passes[:, 0:1], ALU.is_gt, ALU.add))
            at("last")
            inc(nc.vector.tensor_copy(passes[:, 1:2], ps[0:E, 7, 0:1]))
            at("ends")
            inc(tt_op(passes[:, 2:3], passes[:, 1:2], passes[:, 0:1], ALU.subtract))
            at("first")
            inc(ts_op(J[:], iota[0:E, 0:NJ], passes[:, 2:3], None, ALU.is_ge))
            at("J0")
            inc(stt_op(J[:], iota[0:E, 0:NJ], passes[:, 1:2], J[:], ALU.is_lt, ALU.mult))
            at("J")
            inc(stt_op(lrow[:], passes[:, 2:3].to_broadcast([E, T]), float(CAP), lrow[:], ALU.mult,
                       ALU.add))
            at("table")
            inc(stt_op(postj[:].rearrange("p j t -> p t j"), iota[:, 0:NJ].unsqueeze(1).to_broadcast([P, 5, NJ]),
                       -float(CAP), ps[:, 4, 0:5 * NJ].rearrange("p (t j) -> p t j", j=NJ), ALU.mult,
                       ALU.add))
            inc(nc.vector.tensor_copy(combj[:].rearrange("p j t -> p t j"),
                                      ps[:, 5, 0:5 * NJ].rearrange("p (t j) -> p t j", j=NJ)))
            inc(ts_op(jt[:, 0:NJ], ps[0:1, 6, 0:NJ], float(S_JOB), None, ALU.mult))
            inc(nc.vector.tensor_copy(jt[:, NJ:NJ + 1], ps[0:1, 6, NJ:NJ + 1]))
            at("tables")

        def addends(b):
            return ps[:, b, 0:2 * CAP].rearrange("p (a c) -> p c a", a=2)

        def scattered_in(j):
            for m in range(KT):
                dve.wait_ge(scattered, j * KT + (m + 1))
                b = 4 + 2 * (m % 2)
                tt_op(halves(x[:, m]), halves(x[:, m]), ps[:, b:b + 2, 0:HALF], ALU.add).then_inc(
                    x_added, 1)

        def expert_pass(j):
            s0, f0 = MOE0, j * FE_TILES
            for f in range(FE_TILES):
                if f > 0:
                    split_lo(s0 + gate_slab(f) + 2, j)
                dve.wait_ge(slab_done, j * S_JOB + (s0 + gate_slab(f) + 1))
                b = 2 * (f % 2)
                nc.vector.tensor_reduce(gsum[:], addends(b), AX.X, ALU.add).then_inc(m_sum, 1)
                dve.wait_ge(m_sig, f0 + (f + 1))
                tt_op(ma[:, f % 2], gsum[:], msig[:], ALU.mult).then_inc(m_gate, 1)
                if f != 1:
                    split_lo(s0 + gate_slab(f) + 3, j)
                if f == 0:
                    nc.vector.tensor_copy(Jb[:], J[:, bass.ds(j, 1)].to_broadcast([E, P])).then_inc(
                        job_cols, 1)
                    nc.vector.tensor_copy(places[:], part_index[:, bass.ds(j, 1)].rearrange(
                        "p o t -> p (o t)")).then_inc(job_cols, 1)
                if f == 1:
                    scattered_in(j)
                    dve.wait_ge(placed, j + 1)
                    dve.wait_ge(job_cols, j * 2 + 2)
                    for ct in range(2):
                        ts_op(halves(GT[:, ct]), ps[:, 4:6, 0:HALF], places[:, ct:ct + 1], None,
                              ALU.is_equal).then_inc(gt_ready, 1)
                    dve.wait_ge(weighed, j + 1)
                    for ct in range(2):
                        rws = slice(0, (P, REST)[ct])
                        nc.vector.tensor_copy(cw[rws, ct:ct + 1], ps[rws, 6, 400 + ct:401 + ct]).then_inc(
                            cw_ready, 1)
                    split_lo(s0 + gate_slab(f) + 3, j)
                dve.wait_ge(slab_done, j * S_JOB + (s0 + gate_slab(f) + 2))
                nc.vector.tensor_reduce(usum[:], addends(b + 1), AX.X, ALU.add).then_inc(m_up, 1)
                dve.wait_ge(m_up, f0 + (f + 1))
                tt_op(ma[:, f % 2], ma[:, f % 2], usum[:], ALU.mult).then_inc(m_act, 1)
                if f > 0:
                    split_lo(s0 + down_slab(f - 1) + 2, j)
                lo_of_act(f, f0)
                if f == 5:
                    prepare(j + 1)
            split_lo(s0 + down_slab(FE_TILES - 1) + 2, j)
            gathered_lo(j + 1, 0)
            split_lo(s0 + 2, j + 1)
            for ct in range(2):
                rws = slice(0, (P, REST)[ct])
                dve.wait_ge(yt_hi_ready, j * 2 + (ct + 1))
                wide = yt_hi[rws, ct].bitcast(F32).rearrange("p (a d) -> p a d", a=2)
                stt_op(yt_lo[rws, ct].rearrange("p (a d) -> p a d", a=2), y_ps(ct),
                       cw[rws, ct:ct + 1], wide, ALU.mult, ALU.subtract).then_inc(yt_lo_ready, 1)
            dve.wait_ge(yt_lo_ready, j * 2 + 4)
            gathered_lo(j + 1, 1)

        def lo_of_act(f, f0):
            dve.wait_ge(m_hi, f0 + (f + 1))
            tt_op(ma_lo[:, f % 2], ma[:, f % 2], ma_hi[:, f % 2].bitcast(F32), ALU.subtract).then_inc(
                m_lo, 1)

        fills = [0, 0]
        split_lo(0)
        split_lo(1)
        dve.wait_ge(loaded, 48)
        for half in x_in_half:
            dve.wait_ge(half, 16)
        for l in range(DEPTH):
            nb, ob = l * LAYER1, l * O_LAYER1
            norm(2 * l, 3 * l)
            inputs(l, nb, ob)
            fills[:] = 0, l
            gla(l)
            gla_decode(l)
            mlstm_rows(l)
            mlstm(l)
            mlstm_decode(l)
            fill(2 * N_GATES - fills[0])
            gates(l)
            merge(l, nb, ob)
            norm(2 * l + 1, 3 * l + 2)
            if l == 0:
                feed_forward(S_MIX, O_MIX)
            else:
                routing()
                passes_dve = dve.value_load(jt[:, NJ:NJ + 1], min_val=E, max_val=NJ - 2)
                prepare(0)
                split_lo(MOE0 + 2)
                gathered_lo(0, 0)
                gathered_lo(0, 1)
                with dve.Fori(0, passes_dve) as j:
                    expert_pass(j)
                scattered_in(passes_dve)
        norm(4, 6)

    @block.tensor
    def _(pe):
        mm = nc.tensor.matmul

        def exact(out, a, b, start=True, stop=True):
            return mm(out, a, b, start=start, stop=stop, skip_group_check=True)

        def tile_product(out, slot, tile, in_hi, in_lo, kk, first, last):
            for wgt_part, in_part, ends in ((w_hi, in_hi, 0), (w_hi, in_lo, 0), (w_lo, in_hi, 1)):
                for hf in range(2):
                    ins = mm(out[:, hf], wgt_part[:, slot, tile], in_part[:, kk, HALF * hf:HALF * (hf + 1)],
                             start=first and not ends and in_part is in_hi, stop=last and bool(ends))
            return ins

        def slab_ready(n, j=0):
            pe.wait_ge(*split_whole(n, j))

        def out_free(o, j=0):
            if o >= 2:
                pe.wait_ge(*evac(o - 2, j))

        def slab_to_out(n, o, in_hi, in_lo, norm=None, j=0):
            slab_ready(n, j)
            out_free(o, j)
            for kk in range(KT):
                if norm is not None:
                    pe.wait_ge(h_lo_ready, 8 * norm + kk + 1)
                ins = tile_product(out_ps(o), n % SPL, kk, in_hi, in_lo, kk, kk == 0, kk == KT - 1)
            ins.then_inc(slab_done, 1)

        def mean_squares(r, bank_free):
            for s, n in bank_free:
                pe.wait_ge(s, n)
            for kk in range(KT):
                pe.wait_ge(squared, 8 * r + kk + 1)
                for hf in range(2):
                    ins = exact(ps[:, 4 + hf, 0:HALF], ones, sq[:, kk % 2, HALF * hf:HALF * (hf + 1)],
                                kk == 0, kk == KT - 1)
                ins.then_inc(squares_used, 1)

        def gla(l, ob):
            pe.wait_ge(ggw_in, 16 * (l + 1))
            pe.wait_ge(*evac(ob + Z_SMALL))
            pe.wait_ge(*evac(ob + Z_MO - 1))
            pe.wait_ge(*evac(ob + Z_MO - 2))
            for j in range(2):
                for hf in range(2):
                    ins = exact(ps[:, 4 + 2 * j + hf, 0:HALF], ggw[:, j * P:(j + 1) * P],
                                glr[:, HALF * hf:HALF * (hf + 1)])
            ins.then_inc(g.sem, 1)
            fill(8)
            pe.wait_ge(g.sem, g.after("qk", l))
            for tt in range(TT):
                for h in range(H):
                    ins = nc.tensor.transpose(ps[:, 4 + tt, h * P:(h + 1) * P], gv[:, h, token_tile(tt)],
                                              ident)
                ins.then_inc(g.sem, 1)
            fill(1)
            pe.wait_ge(g.sem, g.after("copy", l))
            for tt in range(TT):
                for j in range(2):
                    ins = nc.tensor.transpose(ps[:, 4 + tt, j * P:(j + 1) * P], gk[:, j, token_tile(tt)],
                                              ident)
                ins.then_inc(g.sem, 1)
            fill(1)
            pe.wait_ge(g.sem, g.after("copyk", l))
            for tt in range(TT):
                rep = TT * l + tt
                if tt > 0:
                    pe.wait_ge(gc.sem, gc.after("ns", rep - 1))
                for h in range(H):
                    exact(ps[:, 4, h * P:(h + 1) * P], gk[:, h // 2, token_tile(tt)],
                          qz[:, h, token_tile(tt)])
                for j in range(2):
                    ins = exact(ps[:, 5, 256 * j:256 * (j + 1)], gkt[:, tt, j * P:(j + 1) * P],
                                gvt[:, tt, 256 * j:256 * (j + 1)])
                ins.then_inc(gc.sem, 1)
                fill(1)
                pe.wait_ge(gc.sem, gc.after("sin", rep))
                for h in range(H):
                    out = ps[:, 6, h * P:(h + 1) * P]
                    exact(out, gvt[:, tt, h * P:(h + 1) * P], att[:, h], True, False)
                    ins = exact(out, S_in[:, h // 2], qz[:, h, token_tile(tt)], False, True)
                ins.then_inc(gc.sem, 1)
                fill(1)

        def gla_decode(l):
            pe.wait_ge(gc.sem, gc.after("ns", TT * l + TT - 1))
            for j in range(2):
                rep = 2 * l + j
                if j > 0:
                    pe.wait_ge(dg.sem, dg.after("oc", rep - 1))
                sa = slice(NP_TOK, T)
                nc.tensor.transpose(ps[0:NS_TOK, 4, 0:P], gk[:, j, sa], ident)
                nc.tensor.transpose(ps[0:NS_TOK, 4, P:2 * P], gv[:, 2 * j, sa], ident)
                nc.tensor.transpose(ps[0:NS_TOK, 4, 2 * P:3 * P], gv[:, 2 * j + 1, sa],
                                    ident).then_inc(dg.sem, 1)
                fill(2)
                pe.wait_ge(dg.sem, dg.after("diag", rep))
                for half in range(2):
                    for c in range(2):
                        ins = exact(ps[64 * half:64 * half + 64, 4 + c],
                                    gt8[:, 0, 64 * half:64 * half + 64],
                                    gdiag[:, half, 4 * c:4 * c + 4])
                ins.then_inc(gla_outer_done, 1)
                fill(2)
                pe.wait_ge(dg.sem, dg.after("add", rep))
                for b in range(NS_TOK):
                    ins = exact(ps[:, 6, 2 * b:2 * b + 2], Ss[:, b], qz[:, 2 * j:2 * j + 2, NP_TOK + b])
                ins.then_inc(dg.sem, 1)

        def mlstm(l):
            fill(4)
            pe.wait_ge(rows.sem, rows.after("sexp", l))
            pe.wait_ge(dg.sem, dg.after("oc", 2 * l + 1))
            for tt in range(TT):
                nc.tensor.transpose(ps[:, 4, H * tt:H * tt + H], row_i[:, token_tile(tt)],
                                    ident[0:H, 0:H])
            for a in range(3):
                nc.tensor.transpose(ps[0:NS_TOK, 4, 32 + H * a:32 + H * a + H], w3[:, a],
                                    ident[0:H, 0:H])
            for h in range(H):
                ins = exact(ps[:, 5, 24 * h:24 * h + 24], select[:, h], w3[:].rearrange("h a b -> h (a b)"))
            ins.then_inc(rows.sem, 1)
            pe.wait_ge(rows.sem, rows.after("turned", l))
            pe.wait_ge(st_Ss, 32 * (l + 1))
            for h in range(H):
                rep = H * l + h
                at = lambda name: pe.wait_ge(ml.sem, ml.after(name, rep))
                if h > 0:
                    pe.wait_ge(po.sem, po.after(f"y{h - 1}", l))
                for tt in range(TT):
                    nc.tensor.transpose(ps[:, 4, tt * P:(tt + 1) * P], k[:, h, token_tile(tt)], ident)
                    nc.tensor.transpose(ps[:, 5, tt * P:(tt + 1) * P], v[:, h, token_tile(tt)], ident)
                exact(ps[:, 6], select[:, h], row_M[:, 0:NP_TOK]).then_inc(ml.sem, 1)
                fill(2)
                at("scol")
                for tt in range(2):
                    ins = exact(ps[:, 4 + tt, 0:NP_TOK - tt * P], k[:, h, token_tile(tt)],
                                q[:, h, tt * P:NP_TOK])
                ins.then_inc(ml.sem, 1)
                fill(1)
                at("p01")
                for tt in range(2, 4):
                    c = 256 * (tt - 2)
                    ins = exact(ps[:, 4, c:c + NP_TOK - tt * P], k[:, h, token_tile(tt)],
                                q[:, h, tt * P:NP_TOK])
                ins.then_inc(ml.sem, 1)
                fill(1)
                at("vw")
                for tt in range(TT):
                    exact(ps[:, 6, tt * P:], vt[:, tt], wgt[:, tt, tt * P:], tt == 0, tt == TT - 1)
                for tt in range(TT):
                    exact(ps[:, 7, tt * P:], ones, wgt[:, tt, tt * P:], tt == 0, tt == TT - 1)
                exact(ps[:, 4], select[:, h], row_f[:, 0:NP_TOK])
                for tt in range(TT):
                    exact(ps[:, 5, 0:P], vw[:, tt], kt[:, tt], tt == 0, tt == TT - 1)
                for tt in range(TT):
                    ins = exact(ps[0:1, 5, P:2 * P], wcol[:, tt:tt + 1], kt[:, tt], tt == 0, tt == TT - 1)
                ins.then_inc(ml.sem, 1)
                fill(2)
                pe.wait_ge(ml.sem, ml.after("h", rep))
                pe.wait_ge(po.sem, po.after(f"w{h}", l))
                for hf in range(2):
                    ins = exact(ps[:, 4 + hf, 0:HALF], pw[:, h], pd[:, HALF * hf:HALF * (hf + 1)])
                ins.then_inc(po.sem, 1)
                fill(1)

        def mlstm_decode(l):
            pe.wait_ge(po.sem, po.after("y3", l))
            for h in range(H):
                rep = H * l + h
                at = lambda name: pe.wait_ge(ds.sem, ds.after(name, rep))
                at("vs")
                nc.tensor.transpose(ps[0:NS_TOK, 4, 0:P], vs8[:], ident)
                nc.tensor.transpose(ps[0:NS_TOK, 4, P:2 * P], k[:, h, NP_TOK:T], ident)
                nc.tensor.transpose(ps[0:NS_TOK, 4, 2 * P:3 * P], q[:, h, NP_TOK:T],
                                    ident).then_inc(ds.sem, 1)
                fill(2)
                at("diag")
                for c in range(2):
                    exact(ps[:, 4 + c], tok8[:, 0], diag[:, 0, 4 * c:4 * c + 4])
                for c in range(2):
                    ins = exact(ps[:, 6 + c], ones[0:NS_TOK], diag[:, 1, 4 * c:4 * c + 4])
                ins.then_inc(outer_done, 1)
                fill(2)
                at("add")
                exact(ps[:, 4, 0:NS_TOK], ones[0:NS_TOK], rdiag[:]).then_inc(reciprocals_spread, 1)

        def head_norm(l):
            pe.wait_ge(po.sem, po.after("y3", l))
            for t in range(8):
                i = 8 * l + t
                pe.wait_ge(hn_sq, i + 1)
                if t >= 2:
                    pe.wait_ge(hn_ln, i - 1)
                for hf in range(2):
                    ins = exact(ps[:, 4 + 2 * (t % 2) + hf, 0:HALF], ones,
                                sq[:, t % 2, HALF * hf:HALF * (hf + 1)])
                ins.then_inc(hn_ssq, 1)

        def fill(k):
            for _ in range(k):
                i, half = divmod(fills[0], 2)
                fills[0] += 1
                if i >= N_GATES:
                    continue
                n, o = fills[1] * LAYER1 + Z_MO + i, fills[1] * O_LAYER1 + Z_MO + i
                if not half:
                    slab_ready(n)
                    out_free(o)
                for kk in range(4 * half, 4 * half + 4):
                    ins = tile_product(out_ps(o), n % SPL, kk, h_hi, h_lo, kk, kk == 0, kk == KT - 1)
                if half:
                    ins.then_inc(slab_done, 1)

        def merge(l, nb, ob):
            for mp in range(KT // 2):
                for s, outs in enumerate(((0, 1), (0, 1), (2, 2))):
                    n, o = nb + S_BRANCH + 3 * mp + s, ob + O_BRANCH + 6 * mp + 2 * s
                    slab_ready(n)
                    for i, branch in enumerate(outs):
                        if mp == 0 and s == 0:
                            pe.wait_ge(*((br_lo_ready, H * (l + 1)), (br_lo_gpsimd, 2 * H * (l + 1)))[branch])
                        out_free(o + i)
                        for kk in range(4):
                            ins = tile_product(out_ps(o + i), n % SPL, 4 * i + kk, br_hi, br_lo,
                                               4 * branch + kk, kk == 0, kk == 3)
                        ins.then_inc((first_out_done, slab_done)[i], 1)
            for m in range(KT):
                slab_to_out(nb + S_OUT + m, ob + O_OUT + m, h_hi, h_lo, None if m else 3 * l + 1)

        def feed_forward(nf, of):
            with pe.Fori(0, FF_TURNS) as j:
                for i in range(FF_TURN):
                    slab_to_out(nf + i, of + i, h_hi, h_lo, None if i else 2, j)
            for i in range(2 * FF_REST):
                slab_to_out(nf + i, of + i, h_hi, h_lo, None, FF_TURNS)
            pe.wait_ge(act_lo, F_TILES)
            for s in range(F_TILES):
                n = nf + S_DOWN + s
                slab_ready(n)
                for tile in range(8):
                    m, f = divmod(8 * s + tile, F_TILES)
                    o = of + O_DOWN + m
                    if f == 0:
                        out_free(o)
                    ins = tile_product(out_ps(o), n % SPL, tile, a_hi, a_lo, f, f == 0, f == F_TILES - 1)
                ins.then_inc(slab_done, 1)


        def gather(p, b):
            pe.wait_ge(g_ready, p * 7 + 7)
            for m in range(4 * b, 4 * b + 4):
                out = ps[:, m // 2, WIDE * (m % 2):WIDE * (m % 2 + 1)]
                for tt in range(5):
                    rws = P if tt < 4 else NS_TOK
                    for part in (ht_hi, ht_lo):
                        ins = mm(out, part[0:rws, tt, m * P:(m + 1) * P], G[0:rws, tt],
                                 start=m % 2 == 0 and tt == 0 and part is ht_hi, stop=True,
                                 skip_group_check=True)
            ins.then_inc(gathered, 1)

        def weigh(j):
            pe.wait_ge(job_cols, j * 2 + 2)
            pe.wait_ge(x_added, j * KT + (KT - 1))
            for hf in range(2):
                ins = exact(ps[:, 4 + hf, 0:HALF], Jb[:], lrow[:, HALF * hf:HALF * (hf + 1)])
            ins.then_inc(placed, 1)
            pe.wait_ge(x_added, j * KT + KT)
            for ct in range(2):
                c = slice(P * ct, min(CAP, P * (ct + 1)))
                for tt in range(5):
                    rws = P if tt < 4 else NS_TOK
                    ins = exact(ps[0:c.stop - c.start, 6, 400 + ct:401 + ct], G[0:rws, tt, c].bitcast(F32),
                                ccol[0:rws, tt:tt + 1], tt == 0, tt == 4)
            ins.then_inc(weighed, 1)

        def routing():
            slab_to_out(ROUTER, O_ROUTER, h_hi, h_lo, 5)
            at = lambda name: pe.wait_ge(rt.sem, rt.after(name))
            at("logits")
            for i in range(5):
                rws = P if i < 4 else NS_TOK
                ins = nc.tensor.transpose(ps[0:rws, 4, E * i:E * (i + 1)], lrow[:, P * i:P * i + rws],
                                          ident[0:E, 0:E])
            ins.then_inc(rt.sem, 1)
            for i in range(5):
                rws = P if i < 4 else NS_TOK
                for b, part, taken in ((0, h_hi, ht_hi_ready), (2, h_lo, ht_lo_ready)):
                    if i > 0:
                        pe.wait_ge(taken, i)
                    for kk in range(KT):
                        ins = nc.tensor.transpose(
                            ps[0:rws, b + kk // 4, P * (kk % 4):P * (kk % 4 + 1)],
                            part[:, kk, P * i:P * i + rws].bitcast(F32), ident)
                    ins.then_inc(ht_turned, 1)
            at("comb")
            for i in range(4):
                nc.tensor.transpose(ps[0:E, 4, P * i:P * (i + 1)], sel_t[:, i], ident)
                nc.tensor.transpose(ps[0:E, 5, P * i:P * (i + 1)], comb[:, i], ident)
            nc.tensor.transpose(ps[0:E, 6, 0:NS_TOK], sel_t[0:NS_TOK, 4], ident[0:NS_TOK, 0:NS_TOK])
            nc.tensor.transpose(ps[0:E, 6, NS_TOK:2 * NS_TOK], comb[0:NS_TOK, 4],
                                ident[0:NS_TOK, 0:NS_TOK]).then_inc(rt.sem, 1)
            at("pass3")
            exact(ps[0:E, 7, 0:1], keep_mask[0:E, 0:E], passes[:, 0:1]).then_inc(rt.sem, 1)
            at("shift")
            for i in range(5):
                rws = P if i < 4 else NS_TOK
                exact(ps[0:rws, 4, NJ * i:NJ * (i + 1)], lrow[:, P * i:P * i + rws], J[:])
                exact(ps[0:rws, 5, NJ * i:NJ * (i + 1)], crow[:, P * i:P * i + rws], J[:])
            exact(ps[0:1, 6, 0:NJ], part_index[0:E, 0, 0:1], J[:])
            exact(ps[0:1, 6, NJ:NJ + 1], ones[0:E, 0:1], passes[:, 0:1]).then_inc(rt.sem, 1)
            at("tables")

        def slab_ready_of(j, i):
            pe.wait_ge(*split_whole(MOE0 + i, j))

        def scatter(j):
            pe.wait_ge(yt_lo_ready, j * 2 + 2)
            pe.wait_ge(gt_ready, j * 2 + 2)
            for m in range(KT):
                if m >= 2:
                    pe.wait_ge(x_added, j * KT + (m - 1))
                for i, (ct, part) in enumerate(((0, yt_hi), (0, yt_lo), (1, yt_hi), (1, yt_lo))):
                    rws = slice(0, (P, REST)[ct])
                    for hf in range(2):
                        ins = mm(ps[:, 4 + 2 * (m % 2) + hf, 0:HALF], part[rws, ct, m * P:(m + 1) * P],
                                 GT[rws, ct, HALF * hf:HALF * (hf + 1)], start=i == 0, stop=i == 3)
                ins.then_inc(scattered, 1)

        def expert_pass(j):
            s0, f0 = MOE0, j * FE_TILES

            def gate_or_up(f, i):
                s = gate_slab(f) + i
                slab_ready_of(j, s)
                out = ps[:, 2 * (f % 2) + i]
                for kk in range(KT):
                    if s == 0 and kk % 4 == 0:
                        pe.wait_ge(hg_lo_ready, j * 2 + (2 if kk else 1))
                    mm(out[:, 0:2 * CAP], w_hi[:, (s0 + s) % SPL, kk], hg[:, kk], start=kk == 0,
                       stop=False, skip_group_check=True)
                    ins = mm(out[:, 0:WIDE], w_lo[:, (s0 + s) % SPL, kk], hg[:, kk, 0:WIDE],
                             start=False, stop=kk == KT - 1, skip_group_check=True)
                ins.then_inc(slab_done, 1)

            def down(f):
                s = down_slab(f)
                slab_ready_of(j, s)
                pe.wait_ge(m_lo, f0 + (f + 1))
                for ct in range(2):
                    c = slice(P * ct, min(CAP, P * (ct + 1)))
                    for a, (t, w) in enumerate(((ma_hi, w_hi), (ma_hi, w_lo), (ma_lo, w_hi))):
                        for hf in range(2):
                            ins = mm(y_ps(ct)[:, hf], t[:, f % 2, c],
                                     w[:, (s0 + s) % SPL, 4 * hf:4 * hf + 4],
                                     start=f == 0 and a == 0, stop=f == FE_TILES - 1 and a == 2)
                ins.then_inc(slab_done, 1)

            for f in range(FE_TILES):
                if f >= 2:
                    pe.wait_ge(m_act, f0 + (f - 1))
                gate_or_up(f, 0)
                if f == 1:
                    scatter(j)
                    weigh(j)
                gate_or_up(f, 1)
                if f == 1:
                    pe.wait_ge(gt_ready, j * 2 + 4)
                    pe.wait_ge(cw_ready, j * 2 + 2)
                if f > 0:
                    down(f - 1)
            pe.wait_ge(m_act, f0 + FE_TILES)
            gather(j + 1, 0)
            down(FE_TILES - 1)
            gather(j + 1, 1)

        fills = [0, 0]
        pe.wait_ge(loaded, 48)
        for l in range(DEPTH):
            nb, ob = l * LAYER1, l * O_LAYER1
            mean_squares(2 * l, [])
            for i in range(Z_MO):
                slab_to_out(nb + i, ob + i, h_hi, h_lo, None if i else 3 * l)
            fills[:] = 0, l
            gla(l, ob)
            gla_decode(l)
            mlstm(l)
            mlstm_decode(l)
            fill(2 * N_GATES - fills[0])
            head_norm(l)
            merge(l, nb, ob)
            mean_squares(2 * l + 1, [])
            if l == 0:
                feed_forward(S_MIX, O_MIX)
            else:
                routing()
                passes_pe = pe.value_load(jt[:, NJ:NJ + 1], min_val=E, max_val=NJ - 2)
                pe.wait_ge(ht_hi_ready, 5)
                pe.wait_ge(ht_lo_ready, 5)
                gather(0, 0)
                gather(0, 1)
                with pe.Fori(0, passes_pe) as j:
                    expert_pass(j)
                scatter(passes_pe)
        mean_squares(4, [(x_added, passes_pe * KT + KT)])

    ctx.close()


def _tiles(w):
    kk, m = w.shape
    return w.reshape(kk // P, P, m // P, P).transpose(2, 1, 0, 3)


def _columns(w, groups):
    return [w[:, c:c + P].reshape(-1, P, P).transpose(1, 0, 2) for c in groups]


def _slabs(a):
    out = []
    widths = (512, 512, 512, 4, 4, 512, 256, 256, 512, 16, 512, 512, 3072)
    mq, mk, mv, mi, mf, mo, gq, gk, gv, glr, go, pu, gates = np.cumsum((0,) + widths[:-1]).tolist()
    for l in range(DEPTH):
        w = a["w_in"][l]
        small = np.zeros((D, P), w.dtype)
        small[:, 0:4], small[:, 32:36], small[:, 64:80] = (
            w[:, mi:mi + 4], w[:, mf:mf + 4], w[:, glr:glr + 16])
        out += _columns(small, (0,))
        for start, tiles in ((gk, 2), (gq, 2), (gv, 4), (mq, 4), (mk, 4), (mv, 4), (pu, 4), (mo, 4), (go, 4)):
            out += _columns(w, range(start, start + tiles * P, P))
        for m in range(0, D, 2 * P):
            out += _columns(w, (gates + c + D * n for n, c in (
                (0, m), (1, m), (0, m + P), (1, m + P), (2, m), (2, m + P))))
        wb = a["w_branch"][l]
        for m in range(0, D, 2 * P):
            half = {(n, c): _columns(wb[n], (c,))[0] for n in range(3) for c in (m, m + P)}
            for c in (m, m + P):
                out.append(np.concatenate((half[0, c], half[1, c]), 1))
            out.append(np.concatenate((half[2, m], half[2, m + P]), 1))
        out += list(_tiles(a["w_out"][l]))
        if l == 0:
            up, gate = _tiles(a["ffn_wu"][0]), _tiles(a["ffn_wg"][0])
            for f in range(F_TILES):
                out += [gate[f], up[f]]
            down = _tiles(a["ffn_wd"][0]).transpose(0, 2, 1, 3).reshape(-1, 8, P, P)
            out += list(down.transpose(0, 2, 1, 3))
        else:
            router = np.zeros((D, P), w.dtype)
            router[:, 0:E] = a["router_w"][0]
            out += _columns(router, (0,))
            for e in range(E):
                up, gate = _tiles(a["moe_wu"][0, e]), _tiles(a["moe_wg"][0, e])
                down = a["moe_wd"][0, e].reshape(FE_TILES, P, KT, P)
                for f in range(FE_TILES):
                    out += [gate[f], up[f]] + [down[f - 1]] * (f > 0)
                out.append(down[FE_TILES - 1])
    assert len(out) == N_SLABS
    return np.stack(out)


def _constants():
    con = np.zeros((P, N_CONST), np.float32)
    con[:, C_ID:C_ID + P] = np.eye(P)
    con[:, C_ONE:C_ONE + P] = 1
    causal = np.arange(P)[:, None] <= np.arange(P)[None, :]
    con[:, C_NEG:C_NEG + P] = np.where(causal, 0, MASKED)
    con[:, C_KEEP:C_KEEP + P] = causal
    for r in range(H):
        con[r, C_SEL + r * P:C_SEL + (r + 1) * P] = 1
    for gi, w in enumerate(WINDOWS):
        con[:, C_INV + 16 * gi:C_INV + 16 * gi + 16] = 1 / np.minimum(np.arange(16) + 1, w)
    con[:, C_IOTA:C_IOTA + WIDE] = np.arange(WIDE)
    con[:, C_PART:C_PART + 2 * NJ] = (np.arange(P)[:, None, None] + CAP * np.arange(NJ)[:, None] +
                                      P * np.arange(2)).reshape(P, 2 * NJ)
    con[:, C_TIE:C_TIE + 64] = (np.arange(8)[None, :] < np.arange(8)[:, None]).reshape(1, 64)
    con[:, C_EPS] = EPS
    con[:64, C_HM], con[64:, C_HM + 1] = 1, 1
    return con


def _vector(v):
    return v.reshape(-1, P).T


def kernel(**inputs):
    import concourse.bacc as bacc
    from concourse.bass_utils import run_bass_kernel_spmd

    a = {name: np.asarray(value) for name, value in inputs.items()}
    tokens = np.concatenate((a["x_prompt"].reshape(NP_TOK, D), a["x_sample"].reshape(NS_TOK, D)))
    vectors = np.stack([np.concatenate([_vector(a[n][l]) for n in (
        "norm1_g", "norm2_g", "mlstm_norm_g", "gla_norm_g", "gla_gate_b", "pool_scale")] +
        [_vector(a["final_norm_g"])], 1) for l in range(DEPTH)], 1)
    arrays = {
        "slabs": _slabs(a),
        "x_in": tokens.reshape(T, KT, P).transpose(2, 1, 0),
        "vectors": vectors,
        "if_bias": a["mlstm_if_bias"].transpose(2, 0, 1),
        "gate_w": a["gla_gate_w"],
        "pool_w": a["pool_w"].transpose(0, 2, 1, 3),
        "consts": _constants(),
        "ml_m0": a["state_mlstm_m"].transpose(0, 2, 1),
        "ml_n0": a["state_mlstm_n"],
        "ml_C0": a["state_mlstm_C"].transpose(0, 2, 3, 1, 4),
        "gla_S0": a["state_gla_S"].reshape(DEPTH, NS_TOK, 2, P, P).transpose(0, 2, 3, 1, 4),
        "pool_in": a["state_pool_buf"].reshape(DEPTH, NS_TOK, POOL_BUF, 4, P).transpose(0, 4, 3, 1, 2),
        "pool_old": a["state_pool_buf"][:, :, 1:],
    }
    outs = {
        "y_out": (P, KT, T), "C_p": (DEPTH, H, P, P), "C_s": (DEPTH, H, P, NS_TOK, P),
        "n_p": (DEPTH, 1, H * P), "n_s": (DEPTH, NS_TOK, H, P), "m_p": (DEPTH, H, 1),
        "m_s": (DEPTH, H, NS_TOK), "S_p": (DEPTH, P, 2, P), "S_s": (DEPTH, 2, P, NS_TOK, P),
        "pool_u": (DEPTH, P, 4, POOL_BUF + NS_TOK), "pool_keep": (DEPTH, NS_TOK, POOL_BUF - 1, 512),
    }
    nc = bacc.Bacc("TRN2", target_bir_lowering=False, num_devices=1)
    args = []
    for name in arrays:
        arrays[name] = np.ascontiguousarray(arrays[name])
        args.append(nc.dram_tensor(name, arrays[name].shape, F32, kind="ExternalInput").ap())
    for name, shape in outs.items():
        args.append(nc.dram_tensor(name, shape, F32, kind="ExternalOutput").ap())
    args.append(nc.dram_tensor("gates_kept", (DEPTH, N_GATES, P, T), F32).ap())
    decoder(nc, *args)
    got = run_bass_kernel_spmd(nc, [arrays], core_ids=[0]).results[0]

    y = got["y_out"].transpose(2, 1, 0).reshape(T, D)
    u = got["pool_u"].transpose(0, 3, 2, 1).reshape(DEPTH, POOL_BUF + NS_TOK, 512)
    return (
        y[:NP_TOK].reshape(1, NP_TOK, D), y[NP_TOK:].reshape(NS_TOK, 1, D),
        got["C_p"].reshape(DEPTH, 1, H, P, P), got["C_s"].transpose(0, 3, 1, 2, 4),
        got["n_p"].reshape(DEPTH, 1, H, P), got["n_s"].reshape(DEPTH, NS_TOK, H, P),
        got["m_p"].reshape(DEPTH, 1, H), got["m_s"].transpose(0, 2, 1),
        got["S_p"].transpose(0, 2, 1, 3).reshape(DEPTH, 1, H, DK, P),
        got["S_s"].transpose(0, 3, 1, 2, 4).reshape(DEPTH, NS_TOK, H, DK, P),
        u[:, None, :POOL_BUF], np.concatenate((got["pool_keep"], u[:, POOL_BUF:][:, :, None]), 2),
    )
```
